# Optimizing a Trainium2 kernel written in Bass

```python
import jax, jax.numpy as jnp
from jax import lax
import numpy as np

D_MODEL = 1024
BATCH = 1
SEQ = 512
DEPTH = 1

CHUNK = 64
MIX_WIDTH = D_MODEL
M_HEADS = 4
M_HEAD_DIM = 128
M_WIDTH = M_HEADS * M_HEAD_DIM
CONV_WIDTH = 4
A_HEADS = 4
A_HEAD_DIM = 128
A_WIDTH = A_HEADS * A_HEAD_DIM
IDX_HEADS = 4
IDX_DIM = 64
TOPK_KEYS_MAX = 256
Q_BLOCK = 128
ROPE_THETA = 500000.0
ROPE_FRACTION_DIV = 4
N_EXPERTS = 64
N_GROUPS = 8
TOPK_GROUPS = 4
TOPK_EXPERTS = 8
D_EXPERT = 256
D_SHARED = 256
ROUTE_SCALE = 2.5
EXPERT_BLOCK = 512
NORM_EPS = 1e-6
STAB_INIT = -1e30
SPLIT_SIZES = (M_WIDTH, M_WIDTH, M_WIDTH, M_WIDTH, M_HEADS, M_HEADS, A_WIDTH, A_HEAD_DIM, A_HEAD_DIM, IDX_HEADS * IDX_DIM, IDX_DIM, IDX_HEADS)
IN_DIM = 4 * M_WIDTH + 2 * M_HEADS + A_WIDTH + 2 * A_HEAD_DIM + IDX_HEADS * IDX_DIM + IDX_DIM + IDX_HEADS

kernel_name = "hymba_mlstm_dsa_moe_block"

def rms_norm(x, g):
    xf = x.astype(jnp.float32)
    y = xf * lax.rsqrt(jnp.mean(xf * xf, axis=-1, keepdims=True) + NORM_EPS)
    return (y * g.astype(jnp.float32)).astype(x.dtype)

def layer_norm(x, g, b):
    xf = x.astype(jnp.float32)
    mu = jnp.mean(xf, axis=-1, keepdims=True)
    var = jnp.mean(jnp.square(xf - mu), axis=-1, keepdims=True)
    y = (xf - mu) * lax.rsqrt(var + NORM_EPS)
    return (y * g.astype(jnp.float32) + b.astype(jnp.float32)).astype(x.dtype)

def head_rms_norm(h, g):
    y = h * lax.rsqrt(jnp.mean(h * h, axis=-1, keepdims=True) + NORM_EPS)
    return y * g.astype(jnp.float32).reshape(h.shape[-2:])

def partial_rope(x, pos):
    dh = x.shape[-1]
    rot = dh // ROPE_FRACTION_DIV
    half = rot // 2
    inv_freq = jnp.exp(-jnp.log(jnp.float32(ROPE_THETA)) * jnp.arange(half, dtype=jnp.float32) * (2.0 / rot))
    ang = pos.astype(jnp.float32)[:, None] * inv_freq[None, :]
    shape = (1, pos.shape[0]) + (1,) * (x.ndim - 3) + (half,)
    cos = jnp.cos(ang).reshape(shape)
    sin = jnp.sin(ang).reshape(shape)
    xf = x.astype(jnp.float32)
    x1 = xf[..., :half]
    x2 = xf[..., half:rot]
    out = jnp.concatenate([x1 * cos - x2 * sin, x2 * cos + x1 * sin, xf[..., rot:]], axis=-1)
    return out.astype(x.dtype)

def causal_conv(u, w, b):
    ch = u.shape[-1]
    out = lax.conv_general_dilated(u, w.astype(u.dtype)[:, None, :], window_strides=(1,), padding=[(CONV_WIDTH - 1, 0)], dimension_numbers=("NWC", "WIO", "NWC"), feature_group_count=ch)
    return out + b.astype(u.dtype)

def mlstm_chunkwise(q, k, v, i_pre, f_pre):
    B, S, H, Dh = q.shape
    NC = S // CHUNK
    f32 = jnp.float32

    def chunks(a):
        a = a.astype(f32).reshape((B, NC, CHUNK) + a.shape[2:])
        return jnp.moveaxis(jnp.moveaxis(a, 1, 0), 3, 2)

    qc = chunks(q)
    kc = chunks(k) * (Dh ** -0.5)
    vc = chunks(v)
    ic = chunks(i_pre)
    lfc = jax.nn.log_sigmoid(chunks(f_pre))
    tril = jnp.tril(jnp.ones((CHUNK, CHUNK), dtype=bool))

    def step(carry, inp):
        C, n, m = carry
        qb, kb, vb, ib, lfb = inp
        b = jnp.cumsum(lfb, axis=-1)
        logD = b[..., :, None] - b[..., None, :] + ib[..., None, :]
        logD = jnp.where(tril, logD, -jnp.inf)
        m_inter = b + m[..., None]
        m_t = jnp.maximum(m_inter, jnp.max(logD, axis=-1))
        dmat = jnp.exp(logD - m_t[..., None])
        s_qk = jnp.einsum("bhtd,bhsd->bhts", qb, kb) * dmat
        inter = jnp.exp(m_inter - m_t)
        num = jnp.einsum("bhts,bhsd->bhtd", s_qk, vb) + inter[..., None] * jnp.einsum("bhvk,bhtk->bhtv", C, qb)
        den = jnp.sum(s_qk, axis=-1) + inter * jnp.einsum("bhk,bhtk->bht", n, qb)
        h = num / jnp.maximum(jnp.abs(den), jnp.exp(-m_t))[..., None]
        bL = b[..., -1]
        log_w = bL[..., None] - b + ib
        m_new = jnp.maximum(bL + m, jnp.max(log_w, axis=-1))
        w = jnp.exp(log_w - m_new[..., None])
        decay = jnp.exp(bL + m - m_new)
        C_new = decay[..., None, None] * C + jnp.einsum("bhsv,bhsk->bhvk", vb * w[..., None], kb)
        n_new = decay[..., None] * n + jnp.einsum("bhs,bhsk->bhk", w, kb)
        return (C_new, n_new, m_new), h

    init = (jnp.zeros((B, H, Dh, Dh), f32), jnp.zeros((B, H, Dh), f32), jnp.full((B, H), STAB_INIT, f32))
    _, hs = lax.scan(step, init, (qc, kc, vc, ic, lfc))
    return hs.transpose(1, 0, 3, 2, 4).reshape(B, S, H, Dh)

def dsa_attention(aq, ak, av, iq, ik, iw):
    B, S, H, Dh = aq.shape
    k_top = min(TOPK_KEYS_MAX, S // 4)
    nqb = S // Q_BLOCK
    key_chunk = jnp.arange(S) // CHUNK
    scale = Dh ** -0.5

    def block(args):
        qb, iqb, iwb, qpos = args
        q_chunk = qpos // CHUNK
        rel = jax.nn.relu(jnp.einsum("bqhd,bsd->bqhs", iqb, ik))
        score = jnp.einsum("bqh,bqhs->bqs", iwb, rel).astype(jnp.float32)
        admissible = key_chunk[None, :] <= q_chunk[:, None]
        score = jnp.where(admissible[None], score, -jnp.inf)
        _, idx = lax.top_k(score, k_top)
        valid = (idx // CHUNK) <= q_chunk[None, :, None]
        kg = jax.vmap(lambda kk, ii: kk[ii])(ak, idx)
        vg = jax.vmap(lambda vv, ii: vv[ii])(av, idx)
        logits = jnp.einsum("bqhd,bqkd->bhqk", qb, kg).astype(jnp.float32) * scale
        logits = jnp.where(valid[:, None], logits, -jnp.inf)
        p = jax.nn.softmax(logits, axis=-1).astype(vg.dtype)
        return jnp.einsum("bhqk,bqkd->bqhd", p, vg)

    def qblocks(a):
        return jnp.moveaxis(a.reshape((B, nqb, Q_BLOCK) + a.shape[2:]), 1, 0)

    out = lax.map(block, (qblocks(aq), qblocks(iq), qblocks(iw), jnp.arange(S).reshape(nqb, Q_BLOCK)))
    return jnp.moveaxis(out, 0, 1).reshape(B, S, H, Dh)

def moe_ffn(h, w_router, b_router, w_gate, w_up, w_down, ws_gate, ws_up, ws_down):
    B, S, D = h.shape
    T = B * S
    hf = h.reshape(T, D)
    scores = jax.nn.sigmoid(hf.astype(jnp.float32) @ w_router.astype(jnp.float32))
    sel = scores + b_router.astype(jnp.float32)
    grp = sel.reshape(T, N_GROUPS, N_EXPERTS // N_GROUPS)
    grp_score = jnp.sum(lax.top_k(grp, 2)[0], axis=-1)
    _, top_g = lax.top_k(grp_score, TOPK_GROUPS)
    gmask = jnp.any(top_g[..., None] == jnp.arange(N_GROUPS), axis=-2)
    emask = jnp.repeat(gmask, N_EXPERTS // N_GROUPS, axis=-1)
    _, eidx = lax.top_k(jnp.where(emask, sel, -jnp.inf), TOPK_EXPERTS)
    gw = jnp.take_along_axis(scores, eidx, axis=-1)
    gw = gw / jnp.sum(gw, axis=-1, keepdims=True) * ROUTE_SCALE

    A = T * TOPK_EXPERTS
    e_flat = eidx.reshape(A)
    tok_flat = jnp.repeat(jnp.arange(T, dtype=jnp.int32), TOPK_EXPERTS)
    g_flat = gw.reshape(A)
    order = jnp.argsort(e_flat)
    se, st, sg = e_flat[order], tok_flat[order], g_flat[order]
    counts = jax.ops.segment_sum(jnp.ones_like(e_flat), e_flat, num_segments=N_EXPERTS)
    padded = (counts + EXPERT_BLOCK - 1) // EXPERT_BLOCK * EXPERT_BLOCK
    pad_end = jnp.cumsum(padded)
    pad_start = pad_end - padded
    start = jnp.cumsum(counts) - counts
    dest = pad_start[se] + jnp.arange(A, dtype=se.dtype) - start[se]
    nb = (A + EXPERT_BLOCK - 1) // EXPERT_BLOCK + N_EXPERTS
    rows = nb * EXPERT_BLOCK
    row_tok = jnp.zeros((rows,), jnp.int32).at[dest].set(st)
    row_g = jnp.zeros((rows,), hf.dtype).at[dest].set(sg.astype(hf.dtype))
    block_e = jnp.clip(jnp.searchsorted(pad_end, jnp.arange(nb, dtype=pad_end.dtype) * EXPERT_BLOCK, side="right"), 0, N_EXPERTS - 1)

    def body(y, args):
        tok_b, g_b, e_b = args
        xb = hf[tok_b]
        u = jax.nn.silu(xb @ w_gate[e_b]) * (xb @ w_up[e_b])
        yb = (u @ w_down[e_b]) * g_b[:, None]
        return y.at[tok_b].add(yb), None

    routed, _ = lax.scan(body, jnp.zeros((T, D), hf.dtype), (row_tok.reshape(nb, EXPERT_BLOCK), row_g.reshape(nb, EXPERT_BLOCK), block_e))
    shared = (jax.nn.silu(hf @ ws_gate) * (hf @ ws_up)) @ ws_down
    return (routed + shared).reshape(B, S, D)

def setup_inputs(seed: int = 0) -> dict:
    key = jax.random.key(seed)
    ks = jax.random.split(key, 32)
    L, D = DEPTH, D_MODEL

    def nrm(k, shape, scale):
        return jax.random.normal(k, shape, jnp.float32) * scale

    def gain(k, shape):
        return 1.0 + 0.02 * jax.random.normal(k, shape, jnp.float32)

    return {
        "x": nrm(ks[0], (BATCH, SEQ, D), 1.0),
        "c": nrm(ks[1], (BATCH, D), 1.0),
        "w_ada": nrm(ks[2], (L, D, 6 * D), 0.3 * D ** -0.5),
        "b_ada": nrm(ks[3], (L, 6 * D), 0.02),
        "g_mix_pre": gain(ks[4], (L, D)),
        "g_mix_post": gain(ks[5], (L, D)),
        "g_ffn_pre": gain(ks[6], (L, D)),
        "g_ffn_post": gain(ks[7], (L, D)),
        "w_in": nrm(ks[8], (L, D, IN_DIM), D ** -0.5),
        "conv_w": nrm(ks[9], (L, CONV_WIDTH, 2 * M_WIDTH), CONV_WIDTH ** -0.5),
        "conv_b": nrm(ks[10], (L, 2 * M_WIDTH), 0.02),
        "b_igate": nrm(ks[11], (L, M_HEADS), 0.1),
        "b_fgate": jnp.linspace(3.0, 6.0, M_HEADS, dtype=jnp.float32)[None, :] + nrm(ks[12], (L, M_HEADS), 0.02),
        "g_mlstm_head": gain(ks[13], (L, M_WIDTH)),
        "g_idx_k": gain(ks[14], (L, IDX_DIM)),
        "b_idx_k": nrm(ks[15], (L, IDX_DIM), 0.02),
        "w_out": nrm(ks[16], (L, MIX_WIDTH, D), MIX_WIDTH ** -0.5),
        "w_router": nrm(ks[17], (L, D, N_EXPERTS), D ** -0.5),
        "b_router": nrm(ks[18], (L, N_EXPERTS), 0.01),
        "w_exp_gate": nrm(ks[19], (L, N_EXPERTS, D, D_EXPERT), D ** -0.5),
        "w_exp_up": nrm(ks[20], (L, N_EXPERTS, D, D_EXPERT), D ** -0.5),
        "w_exp_down": nrm(ks[21], (L, N_EXPERTS, D_EXPERT, D), D_EXPERT ** -0.5),
        "w_sh_gate": nrm(ks[22], (L, D, D_SHARED), D ** -0.5),
        "w_sh_up": nrm(ks[23], (L, D, D_SHARED), D ** -0.5),
        "w_sh_down": nrm(ks[24], (L, D_SHARED, D), D_SHARED ** -0.5),
    }

def reference(x, c, w_ada, b_ada, g_mix_pre, g_mix_post, g_ffn_pre, g_ffn_post, w_in, conv_w, conv_b, b_igate, b_fgate, g_mlstm_head, g_idx_k, b_idx_k, w_out, w_router, b_router, w_exp_gate, w_exp_up, w_exp_down, w_sh_gate, w_sh_up, w_sh_down):
    B, S, D = x.shape
    pos = jnp.arange(S)
    offsets = np.cumsum(SPLIT_SIZES)[:-1].tolist()
    idx_w_scale = (IDX_HEADS ** -0.5) * (IDX_DIM ** -0.5)
    for l in range(DEPTH):
        mod = jax.nn.silu(c) @ w_ada[l] + b_ada[l]
        sh1, sc1, gt1, sh2, sc2, gt2 = jnp.split(mod[:, None, :], 6, axis=-1)

        h = rms_norm(x, g_mix_pre[l]) * (1.0 + sc1) + sh1
        proj = h @ w_in[l]
        mq, mk, mv, mo, mi, mf, aq, ak, av, iq, ik, iw = jnp.split(proj, offsets, axis=-1)

        qk = jax.nn.silu(causal_conv(jnp.concatenate([mq, mk], axis=-1), conv_w[l], conv_b[l]))
        mq, mk = jnp.split(qk, 2, axis=-1)
        hm = mlstm_chunkwise(mq.reshape(B, S, M_HEADS, M_HEAD_DIM), mk.reshape(B, S, M_HEADS, M_HEAD_DIM), mv.reshape(B, S, M_HEADS, M_HEAD_DIM), mi + b_igate[l], mf + b_fgate[l])
        hm = head_rms_norm(hm, g_mlstm_head[l]).reshape(B, S, M_WIDTH)
        hm = (jax.nn.sigmoid(mo.astype(jnp.float32)) * hm).astype(x.dtype)

        aq = partial_rope(aq.reshape(B, S, A_HEADS, A_HEAD_DIM), pos)
        ak = partial_rope(ak, pos)
        iq = partial_rope(iq.reshape(B, S, IDX_HEADS, IDX_DIM), pos)
        ik = partial_rope(layer_norm(ik, g_idx_k[l], b_idx_k[l]), pos)
        ha = dsa_attention(aq, ak, av, iq, ik, iw * idx_w_scale).reshape(B, S, A_WIDTH)

        y = jnp.concatenate([hm, ha], axis=-1) @ w_out[l]
        x = x + gt1 * rms_norm(y, g_mix_post[l])

        h2 = rms_norm(x, g_ffn_pre[l]) * (1.0 + sc2) + sh2
        y2 = moe_ffn(h2, w_router[l], b_router[l], w_exp_gate[l], w_exp_up[l], w_exp_down[l], w_sh_gate[l], w_sh_up[l], w_sh_down[l])
        x = x + gt2 * rms_norm(y2, g_ffn_post[l])
    return x


_drawn_inputs = setup_inputs


def setup_inputs(seed=0):
    import zlib

    import numpy as np

    out = dict(_drawn_inputs(seed))
    spreads = {}
    factors = {'g_mix_pre': 4.184,
     'g_mix_post': 6.293,
     'g_ffn_pre': 2.804,
     'g_ffn_post': 8.0,
     'conv_b': 8.0,
     'b_igate': 8.0,
     'g_mlstm_head': 7.945,
     'g_idx_k': 6.413,
     'b_idx_k': 6.936}
    for name, (base, spread) in spreads.items():
        noise = np.random.default_rng([zlib.crc32(name.encode()), seed]).standard_normal(out[name].shape)
        drawn = base * np.exp(spread * noise) if base else spread * noise
        out[name] = __import__('jax').numpy.asarray(drawn.astype(out[name].dtype))
    for name, factor in factors.items():
        out[name] = (out[name] * factor).astype(out[name].dtype)
    return out
```

```python
from contextlib import ExitStack

import numpy as np

import concourse.bass as bass
from concourse import mybir

F32 = mybir.dt.float32
I32 = mybir.dt.int32
ALU = mybir.AluOpType
ACT = mybir.ActivationFunctionType
AX = mybir.AxisListType

P = 128
SEQ = 512
D = 1024
NT = SEQ // P
KC = D // P
CHUNK = 64
HEADS = 4
DH = 128
IH = 4
IDIM = 64
CONV = 4
TOPK = 128
THETA = 500000.0
E_N = 64
E_GROUPS = 8
E_PER = E_N // E_GROUPS
E_TOPG = 4
DE = 256
FC = DE // P
ROUTE_SCALE = 2.5
EPS = 1e-6
NEG = -1e30
FMIN = -3.4028234e38
FMASK = -3.0e38
CAP = 104
MAX_EXTRA = SEQ * 8 // CAP
STEPS = (SEQ - 1) // CAP
E_PAD = E_N + 3

QK_W = 2 * HEADS * DH
V0 = 0
O0 = V0 + HEADS * DH
I0 = O0 + HEADS * DH
F0 = I0 + HEADS
AQ0 = F0 + HEADS
AK0 = AQ0 + HEADS * DH
AV0 = AK0 + DH
IQ0 = AV0 + DH
IK0 = IQ0 + IH * IDIM
IW0 = IK0 + IDIM
NAT_W = IW0 + IH
ROT_A = DH // 4 // 2
ROT_I = IDIM // 4 // 2

K_ID = 0
K_TRI = K_ID + P
K_STRICT = K_TRI + P
K_ONES = K_STRICT + P
K_IOTA = K_ONES + P
K_SEL = K_IOTA + P
K_CAUSAL = K_SEL + HEADS * P
K_TOK = K_CAUSAL + P
K_PADROW = K_TOK + NT
K_PART = K_PADROW + 1
K_COSA = K_PART + 1
K_SINA = K_COSA + NT * ROT_A
K_COSI = K_SINA + NT * ROT_A
K_SINI = K_COSI + NT * ROT_I
K_W = K_SINI + NT * ROT_I


def constants():
    k = np.zeros((P, K_W), np.float32)
    i = np.arange(P)
    k[:, K_ID:K_ID + P] = np.eye(P)
    k[:, K_TRI:K_TRI + P] = np.where(i[:, None] <= i[None, :], 0.0, NEG)
    k[:, K_STRICT:K_STRICT + P] = i[:, None] < i[None, :]
    k[:, K_ONES:K_ONES + P] = 1.0
    k[:, K_IOTA:K_IOTA + P] = i[None, :]
    for h in range(HEADS):
        k[h, K_SEL + h * P:K_SEL + (h + 1) * P] = 1.0
    k[:, K_CAUSAL:K_CAUSAL + P] = np.where(i[None, :] // CHUNK <= i[:, None] // CHUNK, 0.0, NEG)
    k[:, K_TOK:K_TOK + NT] = i[:, None] + P * np.arange(NT)[None, :] + 1
    k[:, K_PADROW] = SEQ + 1 + i
    k[:, K_PART] = i
    for half, at_cos, at_sin in ((ROT_A, K_COSA, K_SINA), (ROT_I, K_COSI, K_SINI)):
        inv = np.exp(-np.log(np.float32(THETA)) * np.arange(half, dtype=np.float32) * np.float32(1.0 / half))
        ang = np.arange(SEQ, dtype=np.float32)[:, None] * inv.astype(np.float32)[None, :]
        for at, f in ((at_cos, np.cos), (at_sin, np.sin)):
            k[:, at:at + NT * half] = f(ang).reshape(NT, P, half).transpose(1, 0, 2).reshape(P, NT * half)
    return k


class Chain:

    def __init__(self, eng, sem):
        self.eng, self.sem, self.n = eng, sem, 0

    def __call__(self, ins):
        self.n += 1
        ins.then_inc(self.sem, 1)
        self.eng.wait_ge(self.sem, self.n)


SLOTS = 4
NAT_PIECES = {"idx": (IQ0, NAT_W - IQ0), "v": (V0, 512), "o": (O0, 512), "g": (I0, 264), "r": (I0 + 264, 512)}
STREAM = [("ada", 0, 0), ("ada", 0, 1), ("ada", 1, 0), ("ada", 1, 1),
          ("nat", "idx", 0), ("nat", "v", 0), ("nat", "o", 0), ("qk", 0, 0),
          ("qk", 1, 0), ("row", 2, 0), ("row", 2, 1), ("nat", "g", 0),
          ("row", 3, 0), ("row", 3, 1), ("row", 4, 0), ("nat", "r", 0),
          ("row", 4, 1), ("row", 5, 0), ("row", 5, 1)]


def stage_in(nc, ctx, A, G):
    with ExitStack() as own:
        def sb(name, shape, dt=F32):
            return own.enter_context(nc.sbuf_tensor(name, shape, dt))

        G.used = []

        def sem(name):
            G.used.append(own.enter_context(nc.semaphore(name)))
            return G.used[-1]

        k, xt, nat, qkc, rows, maskb, cols = G.k, G.xt, G.nat, G.qkc, G.rows, G.maskb, G.cols
        ident = k[:, K_ID:K_ID + P]
        stage = sb("stage", [P, SLOTS, 4096])
        hT = sb("hT", [P, KC, SEQ])
        raw = sb("raw", [P, 4, SEQ + CONV - 1])
        tmp = sb("conv_tmp", [P, 2, SEQ])
        cT = sb("cT", [P, KC])
        cs = sb("cs", [P, KC])
        gpre = sb("gpre", [P, KC])
        bcol = sb("bcol", [P, 2, KC])
        modA = sb("modA", [P, KC])
        modB = sb("modB", [P, KC])
        colrows = sb("colrows", [44, P])
        gik = sb("gik", [P, IDIM])
        bik = sb("bik", [P, IDIM])
        ss = sb("ss", [P, 4 * NT])
        rs = sb("rs", [P, 4 * NT])
        iqT = raw[0:IDIM, :, CONV - 1:]
        ikT = sb("ikT", [IDIM, SEQ])
        iwS = sb("iwS", [P, NT, IH])
        lnb = sb("lnb", [P, NT, IDIM])
        ropet = sb("ropet", [P, 4, NT, HEADS, ROT_A])
        work = sb("work", [P, SEQ])
        relu = tmp
        top8 = sb("top8", [P, 8])
        ps = G.ps
        xn = qkc[:, :, :].rearrange("p a b -> p (a b)").rearrange("p (i d) -> p i d", i=NT)

        s_in = sem("in_small")
        s_x = sem("in_x")
        landed = [sem(f"piece_landed{i}") for i in range(SLOTS)]
        s_ada_used = sem("ada_piece_used")
        s_row_used = sem("row_piece_used")
        s_b = sem("in_bias_rows")
        dch, ach, pch = sem("dve_chain"), sem("act_chain"), sem("pool_chain")
        s_silu = sem("c_silu")
        s_ssq = sem("x_squares")
        s_ms = sem("x_mean_square")
        s_rt = sem("x_root")
        s_xn = sem("x_normed")
        s_cols = sem("cols_transposed")
        s_colsd = sem("cols_copied")
        s_modd = sem("mod_ready")
        s_xT = sem("x_transposed")
        s_hTv = sem("hT_from_dve")
        s_hTa = sem("hT_from_act")
        s_nat = sem("nat_tile_done")
        s_natd = sem("nat_tile_copied")
        s_raw = sem("raw_chunk_copied")
        s_conv = sem("conv_done")
        s_qk = sem("qk_activated")
        s_zero = sem("conv_pad_zero")
        s_acc0 = sem("row_acc_zeroed")
        s_lnv = sem("ik_variance")
        s_ln = sem("ik_rstd")
        s_lnr = sem("ik_root")
        s_rope = sem("indexer_rotated")
        s_iT = sem("indexer_transposed")
        s_iTd = sem("indexer_T_copied")
        s_rel = sem("indexer_products")
        s_relu = sem("indexer_relu")
        s_sc = sem("indexer_summed")
        s_iw = sem("indexer_weights")

        freed, count = [], {"ada": 0, "row": 0, "nat": 0, "qk": 0}
        for kind, a, _ in STREAM:
            count[kind] += 1
            if kind in ("row", "ada"):
                freed.append(({"row": s_row_used, "ada": s_ada_used}[kind], count[kind]))
            else:
                freed.append((s_nat, NT * (count["nat"] + count["qk"])))
        place = {piece: n for n, piece in enumerate(STREAM)}

        def arrived(eng, piece):
            n = place[piece]
            eng.wait_ge(landed[n % SLOTS], 16 * (n // SLOTS + 1))
            return n % SLOTS

        block = own.enter_context(nc.Block())

        @block.sync
        def _(sp):
            sp.dma_start(k[:, :], A["consts"]).then_inc(s_in, 16)
            sp.dma_start(cT[:, :], A["c"].rearrange("a (p c) -> (a p) c", c=KC)).then_inc(s_in, 16)
            sp.dma_start(xt[:, :, :], A["x"][0].rearrange("(i p) d -> p i d", p=P)).then_inc(s_x, 16)
            w_ada = A["w_ada"][0].rearrange("(p c) n -> p c n", c=KC)
            w_in = A["w_in"][0].rearrange("(p c) n -> p c n", c=KC)
            for n, (kind, a, b) in enumerate(STREAM):
                if n >= SLOTS:
                    sp.wait_ge(*freed[n - SLOTS])
                if kind in ("ada", "row"):
                    dst = stage[:, n % SLOTS, :].rearrange("p (c n) -> p c n", c=4)
                    src = w_ada[:, 4 * b:4 * b + 4, a * D:(a + 1) * D]
                else:
                    c0, w = (a * 512, 512) if kind == "qk" else (QK_W + NAT_PIECES[a][0], NAT_PIECES[a][1])
                    dst = stage[:, n % SLOTS, 0:KC * w].rearrange("p (c n) -> p c n", c=KC)
                    src = w_in[:, :, c0:c0 + w]
                sp.dma_start(dst, src).then_inc(landed[n % SLOTS], 16)

        @block.gpsimd
        def _(pool):
            step = Chain(pool, pch)
            nc.gpsimd.memset(raw[:, :, 0:CONV - 1], 0.0).then_inc(s_zero, 1)
            nc.gpsimd.memset(rows[:, :, :], 0.0).then_inc(s_acc0, 1)
            pool.wait_ge(s_in, 16 * 9)
            pool.wait_ge(s_natd, NT)
            ik = nat[:, :, IK0:IK0 + IDIM]

            def wide(c, n=IDIM):
                return rs[:, c * NT:(c + 1) * NT].rearrange("p (i o) -> p i o", o=1).broadcast_to([P, NT, n])

            nc.gpsimd.tensor_scalar(iwS[:, :, :], nat[:, :, IW0:IW0 + IH], (IH ** -0.5) * (IDIM ** -0.5), None,
                                    ALU.mult).then_inc(s_iw, 1)
            pool.wait_ge(s_ln, 1)
            gk = gik[:, :].rearrange("p (o d) -> p o d", o=1).broadcast_to([P, NT, IDIM])
            bk = bik[:, :].rearrange("p (o d) -> p o d", o=1).broadcast_to([P, NT, IDIM])
            step(nc.gpsimd.tensor_tensor(lnb[:, :, :], lnb[:, :, :], wide(2), ALU.mult))
            step(nc.gpsimd.tensor_tensor(lnb[:, :, :], lnb[:, :, :], gk, ALU.mult))
            step(nc.gpsimd.tensor_tensor(ik, lnb[:, :, :], bk, ALU.add))

            def rope(at, heads, dim, half, cos_at, sin_at, last):
                v = nat[:, :, at:at + heads * dim].rearrange("p i (h d) -> p i h d", h=heads)
                x1, x2 = v[:, :, :, 0:half], v[:, :, :, half:2 * half]

                def table(c):
                    t = k[:, c:c + NT * half].rearrange("p (i o d) -> p i o d", i=NT, o=1)
                    return t.broadcast_to([P, NT, heads, half])

                t = [ropet[:, n, :, 0:heads, 0:half] for n in range(4)]
                nc.gpsimd.tensor_tensor(t[0], x1, table(cos_at), ALU.mult)
                nc.gpsimd.tensor_tensor(t[1], x2, table(sin_at), ALU.mult)
                nc.gpsimd.tensor_tensor(t[2], x2, table(cos_at), ALU.mult)
                step(nc.gpsimd.tensor_tensor(t[3], x1, table(sin_at), ALU.mult))
                nc.gpsimd.tensor_tensor(x1, t[0], t[1], ALU.subtract)
                ins = nc.gpsimd.tensor_tensor(x2, t[2], t[3], ALU.add)
                step(ins) if last is None else ins.then_inc(last, 1)

            rope(IK0, 1, IDIM, ROT_I, K_COSI, K_SINI, None)
            rope(IQ0, IH, IDIM, ROT_I, K_COSI, K_SINI, s_rope)
            pool.wait_ge(s_natd, 5 * NT + 8)
            rope(AK0, 1, DH, ROT_A, K_COSA, K_SINA, None)
            rope(AQ0, HEADS, DH, ROT_A, K_COSA, K_SINA, G.s_roped)

        @block.scalar
        def _(act):
            step = Chain(act, ach)
            act.dma_start(gpre[:, :], A["g_mix_pre"].rearrange("a (p c) -> (a p) c", c=KC)).then_inc(s_in, 16)
            act.dma_start(bcol[:, :, :], A["b_ada"][0, 0:2 * D].rearrange("(s p c) -> p s c", s=2, c=KC)).then_inc(s_in, 16)
            act.dma_start(colrows[0:32, :], A["conv_w"][0].rearrange("j (n p) -> (j n) p", p=P)).then_inc(s_in, 16)
            act.dma_start(colrows[32:40, :], A["conv_b"][0].rearrange("(n p) -> n p", p=P)).then_inc(s_in, 16)
            act.dma_start(colrows[40:44, :], A["g_mlstm_head"][0].rearrange("(n p) -> n p", p=P)).then_inc(s_in, 16)
            act.dma_start(gik[:, :], A["g_idx_k"].broadcast_to([P, IDIM])).then_inc(s_in, 16)
            act.dma_start(bik[:, :], A["b_idx_k"].broadcast_to([P, IDIM])).then_inc(s_in, 16)
            act.wait_ge(s_acc0, 1)
            act.dma_start(rows[0:1, :, :], A["b_ada"][:, 2 * D:6 * D].rearrange("a (s n) -> a s n", s=4)).then_inc(s_b, 16)
            act.wait_ge(s_in, 16 * 9)
            nc.scalar.activation(cs[:, :], cT[:, :], ACT.Silu).then_inc(s_silu, 1)
            act.wait_ge(s_x, 16)
            for i in range(NT):
                nc.scalar.activation(hT[:, 2 * i:2 * i + 2, :], xt[:, i, :].rearrange("p (a b) -> p a b", a=2), ACT.Square,
                                     accum_out=ss[:, i:i + 1]).then_inc(s_ssq, 1)
            act.wait_ge(s_ms, 1)
            nc.scalar.activation(rs[:, 0:NT], ss[:, NT:2 * NT], ACT.Sqrt).then_inc(s_rt, 1)
            act.wait_ge(s_modd, 1)
            for c in range(1, KC, 2):
                act.wait_ge(s_xT, c + 1)
                nc.scalar.activation(hT[:, c, :], ps[:, c, :], ACT.Identity, bias=modB[:, c:c + 1],
                                     scale=modA[:, c:c + 1]).then_inc(s_hTa, 1)

            def copy_nat(n, first, w):
                for i in range(NT):
                    act.wait_ge(s_nat, n + i + 1)
                    nc.scalar.activation(nat[:, i, first:first + w], ps[:, (n + i) % 4, 0:w], ACT.Copy).then_inc(s_natd, 1)

            copy_nat(0, *NAT_PIECES["idx"])
            act.wait_ge(s_lnv, 1)
            nc.scalar.activation(rs[:, NT:2 * NT], ss[:, 2 * NT:3 * NT], ACT.Sqrt).then_inc(s_lnr, 1)
            copy_nat(NT, *NAT_PIECES["v"])
            for t in range(NT):
                act.wait_ge(s_iT, t + 1)
                nc.scalar.activation(iqT[:, :, t * P:(t + 1) * P],
                                     ps[0:IDIM, 4 + t % 2, :].rearrange("p (h t) -> p h t", h=IH), ACT.Copy).then_inc(s_iTd, 1)
            act.wait_ge(s_iT, NT + 1)
            nc.scalar.activation(ikT[:, :], ps[0:IDIM, 6, :], ACT.Copy).then_inc(s_iTd, 1)

            def relus(i):
                for h in range(IH):
                    u = (i - 1) * IH + h
                    act.wait_ge(s_rel, u + 1)
                    if u >= 2:
                        act.wait_ge(s_sc, u - 1)
                    w = P * (i + 1)
                    nc.scalar.activation(relu[:, u % 2, 0:w], ps[:, 4 + u % 4, 0:w], ACT.Relu).then_inc(s_relu, 1)

            for i in range(1, NT):
                relus(i)
            copy_nat(2 * NT, *NAT_PIECES["o"])

            def silu_qk(c):
                act.wait_ge(s_conv, c + 1)
                nc.scalar.activation(qkc[:, c, :], tmp[:, c % 2, :], ACT.Silu,
                                     bias=cols[:, 32 + c:33 + c]).then_inc(s_qk, 1)

            act.wait_ge(s_zero, 1)
            act.wait_ge(s_colsd, 1)
            for c in range(2 * HEADS):
                n = 3 * NT + c
                act.wait_ge(s_nat, n + 1)
                if c >= 4:
                    act.wait_ge(s_conv, c - 3)
                nc.scalar.activation(raw[:, c % 4, CONV - 1:], ps[:, n % 4, :], ACT.Copy).then_inc(s_natd, 1)
                if c >= 2:
                    silu_qk(c - 2)
            silu_qk(6)
            silu_qk(7)
            copy_nat(3 * NT + 8, *NAT_PIECES["g"])
            copy_nat(4 * NT + 8, *NAT_PIECES["r"])
            act.wait_ge(s_natd, 5 * NT + 8)

        @block.vector
        def _(dve):
            step = Chain(dve, dch)
            dve.wait_ge(s_ssq, NT)
            nc.vector.tensor_scalar(ss[:, NT:2 * NT], ss[:, 0:NT], 1.0 / D, EPS, ALU.mult, ALU.add).then_inc(s_ms, 1)
            dve.wait_ge(s_rt, 1)
            step(nc.vector.reciprocal(rs[:, 0:NT], rs[:, 0:NT]))
            for i in range(NT):
                nc.vector.tensor_scalar(xn[:, i, :], xt[:, i, :], rs[:, i:i + 1], None, ALU.mult).then_inc(s_xn, 1)
            dve.wait_ge(s_cols, 1)
            nc.vector.tensor_copy(cols[:, 0:44], ps[:, 6, 0:44]).then_inc(s_colsd, 1)
            dve.wait_ge(s_ada_used, 4)
            dve.wait_ge(s_in, 16 * 9)
            step(nc.vector.tensor_tensor(modB[:, :], ps[:, 7, 0:KC], bcol[:, 0, :], ALU.add))
            step(nc.vector.scalar_tensor_tensor(modA[:, :], ps[:, 7, KC:2 * KC], 1.0, bcol[:, 1, :], ALU.add, ALU.add))
            nc.vector.tensor_tensor(modA[:, :], modA[:, :], gpre[:, :], ALU.mult).then_inc(s_modd, 1)
            dve.wait_ge(s_modd, 1)
            for c in range(0, KC, 2):
                dve.wait_ge(s_xT, c + 1)
                nc.vector.tensor_scalar(hT[:, c, :], ps[:, c, :], modA[:, c:c + 1], modB[:, c:c + 1],
                                        ALU.mult, ALU.add).then_inc(s_hTv, 1)
            dve.wait_ge(s_natd, NT)
            ik = nat[:, :, IK0:IK0 + IDIM]
            mean = rs[:, 3 * NT:4 * NT]
            step(nc.vector.tensor_reduce(mean, ik, AX.X, ALU.add))
            step(nc.vector.tensor_scalar(mean, mean, 1.0 / IDIM, None, ALU.mult))
            step(nc.vector.tensor_tensor(lnb[:, :, :], ik,
                                         mean.rearrange("p (i o) -> p i o", o=1).broadcast_to([P, NT, IDIM]), ALU.subtract))
            sq = work[:, 0:NT * IDIM].rearrange("p (i d) -> p i d", i=NT)
            step(nc.vector.tensor_tensor(sq, lnb[:, :, :], lnb[:, :, :], ALU.mult))
            step(nc.vector.tensor_reduce(ss[:, 3 * NT:4 * NT], sq, AX.X, ALU.add))
            nc.vector.tensor_scalar(ss[:, 2 * NT:3 * NT], ss[:, 3 * NT:4 * NT], 1.0 / IDIM, EPS, ALU.mult, ALU.add).then_inc(s_lnv, 1)
            dve.wait_ge(s_lnr, 1)
            nc.vector.reciprocal(rs[:, 2 * NT:3 * NT], rs[:, NT:2 * NT]).then_inc(s_ln, 1)

            dve.wait_ge(s_iw, 1)
            for i in range(1, NT):
                w = P * (i + 1)
                sc = maskb[:, i, 0:w]
                for h in range(IH):
                    u = (i - 1) * IH + h
                    dve.wait_ge(s_relu, u + 1)
                    if h:
                        dve.wait_ge(s_sc, u)
                        nc.vector.scalar_tensor_tensor(sc, relu[:, u % 2, 0:w], iwS[:, i, h:h + 1], sc,
                                                       ALU.mult, ALU.add).then_inc(s_sc, 1)
                    else:
                        nc.vector.tensor_scalar(sc, relu[:, u % 2, 0:w], iwS[:, i, h:h + 1], None, ALU.mult).then_inc(s_sc, 1)
            dve.wait_ge(s_sc, (NT - 1) * IH)
            for i in range(1, NT):
                w = P * (i + 1)
                sc, wk = maskb[:, i, 0:w], work[:, 0:w]
                step(nc.vector.memset(sc[0:CHUNK, w - CHUNK:w], FMASK))
                for r in range(TOPK // 8):
                    src = sc if r == 0 else wk
                    step(nc.vector.max(top8[:, :], src))
                    step(nc.vector.match_replace(wk, top8[:, :], src, FMIN))
                step(nc.vector.tensor_tensor(wk, wk, sc, ALU.is_equal))
                step(nc.vector.tensor_scalar(sc, wk, NEG, None, ALU.mult))
            nc.vector.tensor_copy(maskb[:, 0, 0:P], k[:, K_CAUSAL:K_CAUSAL + P])

            def modulation_rows(s, half):
                slot = arrived(dve, ("row", s, half))
                w = stage[:, slot, :].rearrange("p (c n) -> p c n", c=4)
                for c in range(4):
                    ins = nc.vector.scalar_tensor_tensor(rows[:, s - 2, :], w[:, c, :], cs[:, 4 * half + c:4 * half + c + 1],
                                                         rows[:, s - 2, :], ALU.mult, ALU.add)
                    if c < 3:
                        step(ins)
                    else:
                        ins.then_inc(s_row_used, 1)
                dve.wait_ge(s_row_used, 2 * (s - 2) + half + 1)

            def conv(c):
                dve.wait_ge(s_natd, 3 * NT + c + 1)
                if c >= 2:
                    dve.wait_ge(s_qk, c - 1)
                o = tmp[:, c % 2, :]
                r = raw[:, c % 4, :]
                step(nc.vector.tensor_scalar(o, r[:, 0:SEQ], cols[:, c:c + 1], None, ALU.mult))
                for j in range(1, CONV):
                    w = cols[:, 8 * j + c:8 * j + c + 1]
                    ins = nc.vector.scalar_tensor_tensor(o, r[:, j:j + SEQ], w, o, ALU.mult, ALU.add)
                    if j < CONV - 1:
                        step(ins)
                    else:
                        ins.then_inc(s_conv, 1)

            dve.wait_ge(s_b, 16)
            for c in range(4):
                conv(c)
            modulation_rows(2, 0)
            modulation_rows(2, 1)
            for c in range(4, 8):
                conv(c)
            for s, half in ((3, 0), (3, 1), (4, 0), (4, 1), (5, 0), (5, 1)):
                modulation_rows(s, half)

        @block.tensor
        def _(pe):
            pe.wait_ge(s_in, 16 * 9)
            nc.tensor.transpose(ps[:, 6, 0:44], colrows[:, :], ident[0:44, 0:44]).then_inc(s_cols, 1)
            pe.wait_ge(s_silu, 1)
            for s in range(2):
                sl = [arrived(pe, ("ada", s, half)) for half in range(2)]
                for c in range(KC):
                    for q in range(KC):
                        w = stage[:, sl[q // 4], :].rearrange("p (c n) -> p c n", c=4)
                        ins = nc.tensor.matmul(ps[:, 7, s * KC + c:s * KC + c + 1], w[:, q % 4, c:D:KC], cs[:, q:q + 1],
                                               start=q == 0, stop=q == KC - 1)
                        if c == KC - 1 and q >= KC - 2:
                            ins.then_inc(s_ada_used, 1)
            pe.wait_ge(s_xn, NT)
            pe.wait_ge(s_colsd, 1)
            pe.wait_ge(s_modd, 1)
            for c in range(KC):
                for i in range(NT):
                    ins = nc.tensor.transpose(ps[:, c, i * P:(i + 1) * P], xn[:, i, c:D:KC], ident)
                ins.then_inc(s_xT, 1)
            pe.wait_ge(s_hTv, KC // 2)
            pe.wait_ge(s_hTa, KC // 2)

            def project_nat(n, name):
                slot = arrived(pe, ("nat", name, 0))
                w = NAT_PIECES[name][1]
                wt = stage[:, slot, 0:KC * w].rearrange("p (c n) -> p c n", c=KC)
                for i in range(NT):
                    if n + i >= 4:
                        pe.wait_ge(s_natd, n + i - 3)
                    for c in range(KC):
                        ins = nc.tensor.matmul(ps[:, (n + i) % 4, 0:w], hT[:, c, i * P:(i + 1) * P], wt[:, c, :],
                                               start=c == 0, stop=c == KC - 1)
                    ins.then_inc(s_nat, 1)

            def project_qk(a):
                slot = arrived(pe, ("qk", a, 0))
                wt = stage[:, slot, :].rearrange("p (c n) -> p c n", c=KC)
                for j in range(4):
                    n = 3 * NT + 4 * a + j
                    pe.wait_ge(s_natd, n - 3)
                    for c in range(KC):
                        ins = nc.tensor.matmul(ps[:, n % 4, :], wt[:, c, j * P:(j + 1) * P], hT[:, c, :],
                                               start=c == 0, stop=c == KC - 1)
                    ins.then_inc(s_nat, 1)

            project_nat(0, "idx")
            project_nat(NT, "v")
            pe.wait_ge(s_rope, 1)
            for i in range(NT):
                if i >= 2:
                    pe.wait_ge(s_iTd, i - 1)
                for h in range(IH):
                    ins = nc.tensor.transpose(ps[0:IDIM, 4 + i % 2, h * P:(h + 1) * P],
                                              nat[:, i, IQ0 + h * IDIM:IQ0 + (h + 1) * IDIM], ident)
                ins.then_inc(s_iT, 1)
            for i in range(NT):
                ins = nc.tensor.transpose(ps[0:IDIM, 6, i * P:(i + 1) * P], nat[:, i, IK0:IK0 + IDIM], ident)
            ins.then_inc(s_iT, 1)
            pe.wait_ge(s_iTd, NT + 1)
            for i in range(1, NT):
                for h in range(IH):
                    u = (i - 1) * IH + h
                    if u >= 4:
                        pe.wait_ge(s_relu, u - 3)
                    nc.tensor.matmul(ps[:, 4 + u % 4, 0:P * (i + 1)], iqT[:, h, i * P:(i + 1) * P], ikT[:, 0:P * (i + 1)],
                                     start=True, stop=True).then_inc(s_rel, 1)
            project_nat(2 * NT, "o")
            project_qk(0)
            project_qk(1)
            project_nat(3 * NT + 8, "g")
            project_nat(4 * NT + 8, "r")


def stage_attention(nc, A, G):
    with ExitStack() as own:
        def sb(name, shape, dt=F32):
            return own.enter_context(nc.sbuf_tensor(name, shape, dt))

        G.used = []

        def sem(name):
            G.used.append(own.enter_context(nc.semaphore(name)))
            return G.used[-1]

        k, nat, qkc, rows, maskb, cols, ps = G.k, G.nat, G.qkc, G.rows, G.maskb, G.cols, G.ps
        catT, wout, arena = G.catT, G.wout, G.arena
        ident = k[:, K_ID:K_ID + P]
        TRI = [0, 512, 896, 1152]
        TRI_W = 1280
        stT = arena[:, 0:2 * TRI_W].rearrange("p (b n) -> p b n", b=2)
        dm = arena[:, 2 * TRI_W:4 * TRI_W].rearrange("p (b n) -> p b n", b=2)
        md = arena[:, 4 * TRI_W:4 * TRI_W + 8 * P].rearrange("p (b n) -> p b n", b=8)
        aqT = arena[:, 0:2048].rearrange("p (h t) -> p h t", h=HEADS)
        akT = arena[:, 2048:2560]
        lg = arena[:, 2560:3584].rearrange("p (b n) -> p b n", b=2)
        pr = arena[:, 3584:5120].rearrange("p (b n) -> p b n", b=3)
        prT = arena[:, 5120:6144].rearrange("p (b n) -> p b n", b=2)
        vext = sb("vext", [P, NT, HEADS, DH + 1])
        hall = sb("hall", [P, NT, HEADS * DH])
        gains = sb("gains", [P, 3, D])
        gb = sb("gate_bias", [HEADS, 2])
        ga = sb("gate_a", [HEADS, SEQ])
        gf = sb("gate_f", [HEADS, SEQ])
        gt = sb("gate_t", [HEADS, SEQ])
        aN = sb("gates_nat", [P, 2, NT, HEADS])
        den = sb("den", [P, NT])
        var = sb("var", [P, HEADS, NT])
        rstd = sb("rstd", [P, HEADS, NT])
        mx = sb("mx", [P, 2])
        nm = sb("nm", [P, 2])
        rsum = sb("rsum", [P, 2])
        rinv = sb("rinv", [P, 2])
        sqb = sb("sqb", [P, NT, DH])

        s_in = sem("att_small_in")
        dch, ach, pch = sem("dve_chain"), sem("act_chain"), sem("pool_chain")
        s_gT = sem("gates_transposed")
        s_row = sem("row_broadcast")
        s_rowd = sem("row_ready")
        s_absf = sem("gate_abs")
        s_lse = sem("gate_log")
        s_em = sem("gate_m")
        s_emd = sem("gate_exp_m")
        s_an = sem("gates_back")
        s_and = sem("gates_nat_ready")
        s_bc = sem("negM_broadcast")
        s_md = sem("diag_masked")
        s_dm = sem("decay_ready")
        s_sT = sem("scores_T")
        s_sTd = sem("scores_T_weighted")
        s_num = sem("numerator")
        s_numd = sem("numerator_read")
        s_sig = sem("out_gate")
        s_vext = sem("v_extended")
        s_hsq = sem("head_var")
        s_hrt = sem("head_root")
        s_hr = sem("head_rstd")
        s_hn = sem("head_normed")
        s_hT = sem("head_transposed")
        s_hTd = sem("head_T_copied")
        s_qT = sem("aq_transposed")
        s_qTd = sem("aq_T_copied")
        s_lg = sem("logits")
        s_lgd = sem("logits_masked")
        s_nm = sem("neg_max")
        s_ex = sem("exps")
        s_ri = sem("sum_inverse")
        s_pn = sem("probs_normed")
        s_pT = sem("probs_transposed")
        s_pTd = sem("probs_T_copied")
        s_o = sem("attended")
        s_od = sem("attended_copied")
        UNITS = [(h, i) for h in range(HEADS) for i in range(NT)]
        SCALE = DH ** -0.5
        block = own.enter_context(nc.Block())

        @block.sync
        def _(sp):
            sp.dma_start(gb[:, 0:1], A["b_igate"].rearrange("a h -> h a")).then_inc(s_in, 16)
            sp.dma_start(gb[:, 1:2], A["b_fgate"].rearrange("a h -> h a")).then_inc(s_in, 16)
            for n, name in enumerate(("g_mix_post", "g_ffn_pre", "g_ffn_post")):
                sp.dma_start(gains[:, n, :], A[name].broadcast_to([P, D])).then_inc(s_in, 16)
            sp.dma_start(wout[:, :, :], A["w_out"][0].rearrange("(f p) n -> p f n", p=P)).then_inc(G.s_wout, 16)

        @block.gpsimd
        def _(pool):
            nc.gpsimd.memset(vext[:, :, :, DH:DH + 1], 1.0)
            nc.gpsimd.tensor_copy(vext[:, :, :, 0:DH], nat[:, :, V0:V0 + 512].rearrange("p i (h d) -> p i h d", h=HEADS)).then_inc(s_vext, 1)
            pool.wait_ge(s_hr, 1)
            pool.wait_ge(s_sig, 1)
            for h in range(HEADS):
                hv = hall[:, :, h * DH:(h + 1) * DH]
                r = rstd[:, h, :].rearrange("p (i o) -> p i o", o=1).broadcast_to([P, NT, DH])
                nc.gpsimd.tensor_tensor(hv, hv, r, ALU.mult).then_inc(s_hn, 1)
                pool.wait_ge(s_hn, 2 * h + 1)
                nc.gpsimd.tensor_tensor(hv, hv, nat[:, :, O0 + h * DH:O0 + (h + 1) * DH], ALU.mult).then_inc(s_hn, 1)
            for u, (h, i) in enumerate(UNITS):
                pool.wait_ge(s_ri, u + 1)
                w = P * (i + 1)
                nc.gpsimd.tensor_scalar(pr[:, u % 3, 0:w], pr[:, u % 3, 0:w], rinv[:, u % 2:u % 2 + 1], None,
                                        ALU.mult).then_inc(s_pn, 1)

        @block.scalar
        def _(act):
            step = Chain(act, ach)
            nc.scalar.activation(nat[:, :, O0:O0 + 512], nat[:, :, O0:O0 + 512], ACT.Sigmoid).then_inc(s_sig, 1)
            act.wait_ge(s_absf, 1)
            step(nc.scalar.activation(gt[:, :], gt[:, :], ACT.Exp, scale=-1.0))
            nc.scalar.activation(gt[:, :], gt[:, :], ACT.Ln, bias=1.0).then_inc(s_lse, 1)
            act.wait_ge(s_em, 1)
            nc.scalar.activation(gt[:, :], gt[:, :], ACT.Exp, scale=-1.0).then_inc(s_emd, 1)
            act.wait_ge(s_and, 1)
            for h in range(HEADS):
                if h >= 2:
                    act.wait_ge(s_sTd, NT * (h - 1))
                act.wait_ge(s_md, NT * (h + 1))
                for j in range(NT):
                    w = SEQ - P * j
                    bias = aN[:, 0, j, h:h + 1]
                    ins = nc.scalar.activation(dm[:, h % 2, TRI[j]:TRI[j] + P], md[:, NT * (h % 2) + j, :], ACT.Exp, bias=bias)
                    if w > P:
                        ins = nc.scalar.activation(dm[:, h % 2, TRI[j] + P:TRI[j] + w], ps[:, h % 2, P * (j + 1):SEQ],
                                                   ACT.Exp, bias=bias)
                    ins.then_inc(s_dm, 1)
            act.wait_ge(s_hsq, 1)
            nc.scalar.activation(rstd[:, :, :], var[:, :, :], ACT.Sqrt).then_inc(s_hrt, 1)
            act.wait_ge(s_num, HEADS)
            for h in range(HEADS + 1):
                act.wait_ge(s_qT, h + 1)
                dst = aqT[:, h, :] if h < HEADS else akT
                nc.scalar.activation(dst, ps[:, h, :], ACT.Copy).then_inc(s_qTd, 1)

            def exp_unit(u):
                w = P * (UNITS[u][1] + 1)
                act.wait_ge(s_nm, u + 1)
                if u >= 3:
                    act.wait_ge(s_pT, u - 2)
                nc.scalar.activation(pr[:, u % 3, 0:w], lg[:, u % 2, 0:w], ACT.Exp, bias=nm[:, u % 2:u % 2 + 1], scale=SCALE,
                                     accum_out=rsum[:, u % 2:u % 2 + 1]).then_inc(s_ex, 1)

            def copy_pT(u):
                w = P * (UNITS[u][1] + 1)
                act.wait_ge(s_pT, u + 1)
                if u >= 2:
                    act.wait_ge(s_o, u - 1)
                nc.scalar.activation(prT[:, u % 2, 0:w], ps[:, 3 + u % 3, 0:w], ACT.Copy).then_inc(s_pTd, 1)

            for u in range(len(UNITS)):
                exp_unit(u)
                if u:
                    copy_pT(u - 1)
            copy_pT(len(UNITS) - 1)

        @block.vector
        def _(dve):
            step = Chain(dve, dch)
            dve.wait_ge(s_in, 16 * 5)
            dve.wait_ge(s_gT, 2)
            step(nc.vector.tensor_scalar(gf[:, :], ps[0:HEADS, 1, :], gb[:, 1:2], None, ALU.add))
            step(nc.vector.tensor_scalar(gt[:, :], gf[:, :], -1.0, None, ALU.mult))
            nc.vector.tensor_tensor(gt[:, :], gf[:, :], gt[:, :], ALU.max).then_inc(s_absf, 1)
            step(nc.vector.tensor_scalar(gf[:, :], gf[:, :], 0.0, None, ALU.min))
            step(nc.vector.tensor_scalar(ga[:, :], ps[0:HEADS, 0, :], gb[:, 0:1], None, ALU.add))
            dve.wait_ge(s_lse, 1)
            step(nc.vector.tensor_tensor(gf[:, :], gf[:, :], gt[:, :], ALU.subtract))
            one = k[0:HEADS, K_ONES:K_ONES + 1].broadcast_to([HEADS, SEQ])
            step(nc.vector.tensor_tensor_scan(gt[:, :], one, gf[:, :], 0.0, ALU.mult, ALU.add))
            step(nc.vector.tensor_tensor(ga[:, :], ga[:, :], gt[:, :], ALU.subtract))
            step(nc.vector.tensor_tensor_scan(gf[:, :], one, ga[:, :], NEG, ALU.mult, ALU.max))
            nc.vector.tensor_tensor(gt[:, :], gt[:, :], gf[:, :], ALU.add).then_inc(s_em, 1)
            step(nc.vector.tensor_scalar(gf[:, :], gf[:, :], -1.0, None, ALU.mult))
            for r in range(8):
                s, c = r // 2, slice(512 * (r % 2), 512 * (r % 2 + 1))
                dve.wait_ge(s_row, r + 1)
                src, dst = ps[:, 2 + r % 6, :], rows[:, s, c]
                if s == 1:
                    ins = nc.vector.tensor_copy(dst, src)
                elif s == 2:
                    ins = nc.vector.scalar_tensor_tensor(dst, src, 1.0, gains[:, 1, c], ALU.add, ALU.mult)
                else:
                    ins = nc.vector.tensor_tensor(dst, src, gains[:, 0 if s == 0 else 2, c], ALU.mult)
                ins.then_inc(s_rowd, 1)
            dve.wait_ge(s_an, 1)
            nc.vector.tensor_copy(aN[:, :, :, :], ps[:, 0, 0:2 * NT * HEADS].rearrange("p (a i h) -> p a i h", a=2, i=NT)).then_inc(s_and, 1)

            def diagonals(h):
                dve.wait_ge(s_bc, h + 1)
                if h >= 2:
                    dve.wait_ge(s_dm, NT * (h - 1))
                for j in range(NT):
                    nc.vector.tensor_tensor(md[:, NT * (h % 2) + j, :], ps[:, h % 2, j * P:(j + 1) * P],
                                            k[:, K_TRI:K_TRI + P], ALU.add).then_inc(s_md, 1)

            def weigh(h):
                for j in range(NT):
                    u, w = NT * h + j, SEQ - P * j
                    dve.wait_ge(s_sT, u + 1)
                    dve.wait_ge(s_dm, u + 1)
                    if h >= 2:
                        dve.wait_ge(s_num, h - 1)
                    nc.vector.scalar_tensor_tensor(stT[:, h % 2, TRI[j]:TRI[j] + w], ps[:, 2 + u % 2, 0:w], SCALE,
                                                   dm[:, h % 2, TRI[j]:TRI[j] + w], ALU.mult, ALU.mult).then_inc(s_sTd, 1)

            def read_head(h):
                dve.wait_ge(s_num, h + 1)
                b = 4 + 2 * (h % 2)
                v = ps[:, b:b + 2, :].rearrange("p b (t n) -> p (b t) n", n=256)
                hv = hall[:, :, h * DH:(h + 1) * DH]
                dv = den[:, :].rearrange("p (i o) -> p i o", o=1)
                step(nc.vector.scalar_tensor_tensor(dv, v[:, :, DH:DH + 1], -1.0, aN[:, 1, :, h:h + 1], ALU.mult, ALU.max))
                step(nc.vector.tensor_tensor(dv, dv, v[:, :, DH:DH + 1], ALU.max))
                step(nc.vector.reciprocal(den[:, :], den[:, :]))
                nc.vector.tensor_tensor(hv, v[:, :, 0:DH], den[:, :].rearrange("p (i o) -> p i o", o=1).broadcast_to([P, NT, DH]),
                                        ALU.mult).then_inc(s_numd, 1)
                dve.wait_ge(s_numd, h + 1)
                step(nc.vector.tensor_tensor(sqb[:, :, :], hv, hv, ALU.mult))
                step(nc.vector.tensor_reduce(var[:, h, :], sqb[:, :, :], AX.X, ALU.add))

            diagonals(0)
            for h in range(HEADS):
                if h + 1 < HEADS:
                    diagonals(h + 1)
                weigh(h)
                if h:
                    read_head(h - 1)
            read_head(HEADS - 1)
            nc.vector.tensor_scalar(var[:, :, :], var[:, :, :], 1.0 / DH, EPS, ALU.mult, ALU.add).then_inc(s_hsq, 1)
            dve.wait_ge(s_hrt, 1)
            nc.vector.reciprocal(rstd[:, :, :], rstd[:, :, :]).then_inc(s_hr, 1)

            def mask_unit(u):
                h, i = UNITS[u]
                w = P * (i + 1)
                dve.wait_ge(s_lg, u + 1)
                if u >= 2:
                    dve.wait_ge(s_ex, u - 1)
                nc.vector.tensor_tensor_reduce(out=lg[:, u % 2, 0:w], in0=ps[:, u % 3, 0:w], in1=maskb[:, i, 0:w], scale=1.0,
                                               scalar=FMIN, op0=ALU.add, op1=ALU.max,
                                               accum_out=mx[:, u % 2:u % 2 + 1]).then_inc(s_lgd, 1)
                dve.wait_ge(s_lgd, u + 1)
                nc.vector.tensor_scalar(nm[:, u % 2:u % 2 + 1], mx[:, u % 2:u % 2 + 1], -SCALE, None, ALU.mult).then_inc(s_nm, 1)

            def invert(u):
                dve.wait_ge(s_ex, u + 1)
                if u >= 2:
                    dve.wait_ge(s_pn, u - 1)
                nc.vector.reciprocal(rinv[:, u % 2:u % 2 + 1], rsum[:, u % 2:u % 2 + 1]).then_inc(s_ri, 1)

            def copy_out(h):
                dve.wait_ge(s_o, NT * (h + 1))
                nc.vector.tensor_copy(catT[:, HEADS + h, :], ps[:, 6 + h % 2, :]).then_inc(s_od, 1)

            def copy_head(h):
                dve.wait_ge(s_hT, h + 1)
                nc.vector.tensor_scalar(catT[:, h, :], ps[:, 6 + h % 2, :], cols[:, 40 + h:41 + h], None, ALU.mult).then_inc(s_hTd, 1)

            for h in range(HEADS):
                copy_head(h)
            for u in range(len(UNITS)):
                mask_unit(u)
                if u:
                    invert(u - 1)
                if u >= NT + 2 and (u - 2) % NT == 0:
                    copy_out((u - 2) // NT - 1)
            invert(len(UNITS) - 1)
            copy_out(HEADS - 1)

        @block.tensor
        def _(pe):
            for b, at in ((0, I0), (1, F0)):
                for i in range(NT):
                    ins = nc.tensor.transpose(ps[0:HEADS, b, i * P:(i + 1) * P], nat[:, i, at:at + HEADS], ident)
                ins.then_inc(s_gT, 1)
            for r in range(8):
                if r >= 6:
                    pe.wait_ge(s_rowd, r - 5)
                nc.tensor.matmul(ps[:, 2 + r % 6, :], k[:, K_ONES:K_ONES + P], rows[:, r // 2, 512 * (r % 2):512 * (r % 2 + 1)],
                                 start=True, stop=True).then_inc(s_row, 1)
            pe.wait_ge(s_emd, 1)
            for a, src in enumerate((ga, gt)):
                for i in range(NT):
                    at = (a * NT + i) * HEADS
                    ins = nc.tensor.transpose(ps[:, 0, at:at + HEADS], src[:, i * P:(i + 1) * P], ident[0:HEADS, 0:HEADS])
            ins.then_inc(s_an, 1)
            pe.wait_ge(s_and, 1)
            pe.wait_ge(s_rowd, 8)
            pe.wait_ge(s_vext, 1)

            def broadcast(h):
                if h >= 2:
                    pe.wait_ge(s_dm, NT * (h - 1))
                nc.tensor.matmul(ps[:, h % 2, :], k[0:HEADS, K_SEL + h * P:K_SEL + (h + 1) * P], gf[:, :],
                                 start=True, stop=True).then_inc(s_bc, 1)

            def scores(h):
                for j in range(NT):
                    u = NT * h + j
                    if u >= 2:
                        pe.wait_ge(s_sTd, u - 1)
                    nc.tensor.matmul(ps[:, 2 + u % 2, 0:SEQ - P * j], qkc[:, HEADS + h, j * P:(j + 1) * P], qkc[:, h, j * P:SEQ],
                                     start=True, stop=True).then_inc(s_sT, 1)

            def numerators(h):
                if h >= 2:
                    pe.wait_ge(s_numd, h - 1)
                pe.wait_ge(s_sTd, NT * (h + 1))
                for i in range(NT):
                    for j in range(i + 1):
                        ins = nc.tensor.matmul(ps[:, 4 + 2 * (h % 2) + i // 2, 256 * (i % 2):256 * (i % 2) + DH + 1],
                                               stT[:, h % 2, TRI[j] + P * (i - j):TRI[j] + P * (i - j + 1)], vext[:, j, h, :],
                                               start=j == 0, stop=j == i)
                ins.then_inc(s_num, 1)

            broadcast(0)
            for h in range(HEADS):
                if h + 1 < HEADS:
                    broadcast(h + 1)
                scores(h)
                if h:
                    numerators(h - 1)
            numerators(HEADS - 1)
            pe.wait_ge(G.s_roped, 1)
            pe.wait_ge(s_dm, NT * HEADS)
            pe.wait_ge(s_sTd, NT * HEADS)
            pe.wait_ge(s_numd, HEADS)
            for h in range(HEADS + 1):
                for i in range(NT):
                    at = AQ0 + h * DH
                    ins = nc.tensor.transpose(ps[:, h, i * P:(i + 1) * P], nat[:, i, at:at + DH], ident)
                ins.then_inc(s_qT, 1)
            for h in range(HEADS):
                pe.wait_ge(s_hn, 2 * (h + 1))
                if h >= 2:
                    pe.wait_ge(s_hTd, h - 1)
                for i in range(NT):
                    ins = nc.tensor.transpose(ps[:, 6 + h % 2, i * P:(i + 1) * P], hall[:, i, h * DH:(h + 1) * DH], ident)
                ins.then_inc(s_hT, 1)
            pe.wait_ge(s_qTd, HEADS + 1)
            pe.wait_ge(s_hTd, HEADS)

            def logits(u):
                h, i = UNITS[u]
                if u >= 3:
                    pe.wait_ge(s_lgd, u - 2)
                nc.tensor.matmul(ps[:, u % 3, 0:P * (i + 1)], aqT[:, h, i * P:(i + 1) * P], akT[:, 0:P * (i + 1)],
                                 start=True, stop=True).then_inc(s_lg, 1)

            def turn(u):
                h, i = UNITS[u]
                pe.wait_ge(s_pn, u + 1)
                if u >= 3:
                    pe.wait_ge(s_pTd, u - 2)
                for j in range(i + 1):
                    ins = nc.tensor.transpose(ps[:, 3 + u % 3, j * P:(j + 1) * P], pr[:, u % 3, j * P:(j + 1) * P], ident)
                ins.then_inc(s_pT, 1)

            def attend(u):
                h, i = UNITS[u]
                pe.wait_ge(s_pTd, u + 1)
                if h >= 2 and i == 0:
                    pe.wait_ge(s_od, h - 1)
                for j in range(i + 1):
                    ins = nc.tensor.matmul(ps[:, 6 + h % 2, i * P:(i + 1) * P], nat[:, j, AV0:AV0 + DH],
                                           prT[:, u % 2, j * P:(j + 1) * P], start=j == 0, stop=j == i)
                ins.then_inc(s_o, 1)

            logits(0)
            logits(1)
            for u in range(len(UNITS)):
                if u + 2 < len(UNITS):
                    logits(u + 2)
                turn(u)
                if u:
                    attend(u - 1)
            attend(len(UNITS) - 1)


def stage_route(nc, A, G):
    with ExitStack() as own:
        def sb(name, shape, dt=F32):
            return own.enter_context(nc.sbuf_tensor(name, shape, dt))

        G.used = []

        def sem(name):
            G.used.append(own.enter_context(nc.semaphore(name)))
            return G.used[-1]

        k, rows, xt, ps, catT, wout = G.k, G.rows, G.xt, G.ps, G.catT, G.wout
        posm, gt = G.posm, G.gt
        ident = k[:, K_ID:K_ID + P]
        ones = k[:, K_ONES:K_ONES + P]
        flat = G.nat[:, :, :].rearrange("p i n -> p (i n)")
        h2n = flat[:, 0:NT * D].rearrange("p (i d) -> p i d", i=NT)
        wg = flat[:, 4096:4096 + KC * DE].rearrange("p (c f) -> p c f", c=KC)
        wu = flat[:, 6144:6144 + KC * DE].rearrange("p (c f) -> p c f", c=KC)
        h2T = G.qkc
        wd = G.arena[:, 0:FC * D].rearrange("p (f n) -> p f n", f=FC)
        wr = G.arena[:, 2048:2048 + KC * E_N].rearrange("p (c e) -> p c e", c=KC)
        sg = G.arena[:, 2560:3584].rearrange("p (f t) -> p f t", f=FC)
        uT = G.arena[:, 3584:4608].rearrange("p (f t) -> p f t", f=FC)
        tmp = G.arena[:, 4608:5632]
        ysh = sb("shared_out", [P, 2, D])
        br = sb("b_router", [P, E_N])
        ssq = sb("ssq", [P, NT, 4])
        ms = sb("ms", [P, NT, 2])
        rt = sb("rt", [P, NT, 2])
        sco = sb("scores", [P, NT, E_N])
        sel = sb("sel", [P, NT, E_N])
        top2 = sb("top2", [P, NT * E_GROUPS, 8])
        gs = sb("group_score", [P, NT, E_GROUPS])
        cmp1 = sb("cmp1", [P, NT, E_GROUPS, E_GROUPS])
        cmp2 = sb("cmp2", [P, NT, E_GROUPS, E_GROUPS])
        gm = sb("group_mask", [P, NT, E_GROUPS])
        t8 = sb("top8e", [P, NT, 8])
        em = sb("expert_mask", [P, NT, E_N])
        wk = sb("sel_left", [P, NT, E_N])
        gsum = sb("gate_sum", [P, NT])
        cnt = sb("counts", [P, 4, E_N])
        tab = sb("tab", [P, 4])
        diag = sb("diag", [P, 2, P])

        s_in = sem("route_in")
        s_wsh = sem("shared_weights")
        dch, ach = sem("dve_chain"), sem("act_chain")
        s_y = sem("y_projected")
        s_sq = sem("squares")
        s_ms = sem("mean_squares")
        s_rt = sem("roots")
        s_yr = sem("y_read")
        s_x2 = sem("x2_ready")
        s_h2 = sem("h2_ready")
        s_h2T = sem("h2_transposed")
        s_h2Td = sem("h2_T_copied")
        s_lg = sem("router_logits")
        s_sco = sem("scores_ready")
        s_gu = sem("shared_gate_up")
        s_sg = sem("shared_silu")
        s_u = sem("shared_u")
        s_dn = sem("shared_down")
        s_dnd = sem("shared_copied")
        s_em = sem("expert_mask_ready")
        s_pos = sem("positions")
        s_dg = sem("diagonals_ready")
        s_tab = sem("table_rows")
        s_hw = sem("h2_stored")
        s_yw = [sem(f"shared_stored{i}") for i in range(2)]
        s_init = sem("tables_cleared")
        s_tabd = sem("tables_ready")
        block = own.enter_context(nc.Block())

        @block.sync
        def _(sp):
            sp.dma_start(br[:, :], A["b_router"].broadcast_to([P, E_N])).then_inc(s_in, 16)
            sp.dma_start(wr, A["w_router"][0].rearrange("(p c) e -> p c e", c=KC)).then_inc(s_in, 16)
            sp.dma_start(wg, A["w_sh_gate"][0].rearrange("(p c) f -> p c f", c=KC)).then_inc(s_wsh, 16)
            sp.dma_start(wu, A["w_sh_up"][0].rearrange("(p c) f -> p c f", c=KC)).then_inc(s_wsh, 16)
            sp.dma_start(wd, A["w_sh_down"][0].rearrange("(f p) n -> p f n", p=P)).then_inc(s_wsh, 16)
            for i in range(NT):
                sp.wait_ge(s_h2, i + 1)
                sp.dma_start(G.h2_rows[i * P:(i + 1) * P, :], h2n[:, i, :]).then_inc(s_hw, 16)
            for i in range(NT):
                sp.wait_ge(s_dnd, i + 1)
                sp.dma_start(G.y_rows[i * P:(i + 1) * P, :], ysh[:, i % 2, :]).then_inc(s_yw[i % 2], 16)
            sp.wait_ge(s_hw, 16 * NT)
            sp.wait_ge(s_yw[0], 16 * (NT // 2))
            sp.wait_ge(s_yw[1], 16 * (NT // 2))

        @block.gpsimd
        def _(pool):
            nc.gpsimd.memset(posm[:, :], -1.0).then_inc(s_init, 1)
            nc.gpsimd.memset(gt[:, :, :, :], 0.0).then_inc(s_init, 1)

        @block.scalar
        def _(act):
            def squares(i, n):
                if n == 0:
                    act.wait_ge(s_y, i + 1)
                    if i:
                        act.wait_ge(s_h2, i)
                    src = ps[:, 2 * i:2 * i + 2, :]
                else:
                    act.wait_ge(s_x2, i + 1)
                    src = xt[:, i, :].rearrange("p (a b) -> p a b", a=2)
                nc.scalar.activation(tmp.rearrange("p (a b) -> p a b", a=2), src, ACT.Square,
                                     accum_out=ssq[:, i, n:n + 1]).then_inc(s_sq, 1)
                act.wait_ge(s_ms, 2 * i + n + 1)
                nc.scalar.activation(rt[:, i, n:n + 1], ms[:, i, n:n + 1], ACT.Sqrt).then_inc(s_rt, 1)

            def copy_h2T(i):
                act.wait_ge(s_h2T, 2 * i + 2)
                nc.scalar.activation(h2T[:, 4:8, i * P:(i + 1) * P], ps[:, 2 * i + 1, :].rearrange("p (c t) -> p c t", c=4),
                                     ACT.Copy).then_inc(s_h2Td, 1)

            for i in range(NT):
                squares(i, 0)
                squares(i, 1)
                copy_h2T(i)
            for i in range(NT):
                act.wait_ge(s_lg, i + 1)
                nc.scalar.activation(sco[:, i, :], ps[:, 6, i * E_N:(i + 1) * E_N], ACT.Sigmoid).then_inc(s_sco, 1)
            for f in range(FC):
                act.wait_ge(s_gu, f + 1)
                nc.scalar.activation(sg[:, f, :], ps[:, f, :], ACT.Silu).then_inc(s_sg, 1)
            for i in range(NT):
                act.wait_ge(s_dn, i + 1)
                if i >= 2:
                    act.wait_ge(s_yw[i % 2], 16 * (i // 2))
                nc.scalar.activation(ysh[:, i % 2, :], ps[:, 4 * (i % 2):4 * (i % 2) + 2, :].rearrange("p a b -> p (a b)"),
                                     ACT.Copy).then_inc(s_dnd, 1)

        @block.vector
        def _(dve):
            step = Chain(dve, dch)

            def root(i, n):
                dve.wait_ge(s_sq, 2 * i + n + 1)
                nc.vector.tensor_scalar(ms[:, i, n:n + 1], ssq[:, i, n:n + 1], 1.0 / D, EPS, ALU.mult, ALU.add).then_inc(s_ms, 1)
                dve.wait_ge(s_rt, 2 * i + n + 1)
                step(nc.vector.reciprocal(rt[:, i, n:n + 1], rt[:, i, n:n + 1]))

            for i in range(NT):
                root(i, 0)
                nc.vector.scalar_tensor_tensor(tmp, ps[:, 2 * i:2 * i + 2, :].rearrange("p a b -> p (a b)"), rt[:, i, 0:1],
                                               rows[:, 0, :], ALU.mult, ALU.mult).then_inc(s_yr, 1)
                dve.wait_ge(s_yr, i + 1)
                nc.vector.tensor_tensor(xt[:, i, :], xt[:, i, :], tmp, ALU.add).then_inc(s_x2, 1)
                root(i, 1)
                step(nc.vector.scalar_tensor_tensor(h2n[:, i, :], xt[:, i, :], rt[:, i, 1:2], rows[:, 2, :], ALU.mult, ALU.mult))
                nc.vector.tensor_tensor(h2n[:, i, :], h2n[:, i, :], rows[:, 1, :], ALU.add).then_inc(s_h2, 1)
                dve.wait_ge(s_h2T, 2 * i + 1)
                nc.vector.tensor_copy(h2T[:, 0:4, i * P:(i + 1) * P], ps[:, 2 * i, :].rearrange("p (c t) -> p c t", c=4)).then_inc(s_h2Td, 1)

            def bc(ap, shape):
                return ap.broadcast_to(shape)

            dve.wait_ge(s_in, 32)
            dve.wait_ge(s_sco, NT)
            step(nc.vector.tensor_tensor(sel[:, :, :], sco[:, :, :],
                                         bc(br[:, :].rearrange("p (o e) -> p o e", o=1), [P, NT, E_N]), ALU.add))
            for n in range(NT * E_GROUPS):
                i, g = n // E_GROUPS, n % E_GROUPS
                ins = nc.vector.max(top2[:, n, :], sel[:, i, g * E_PER:(g + 1) * E_PER])
            step(ins)
            step(nc.vector.tensor_tensor(gs[:, :, :].rearrange("p i g -> p (i g)").rearrange("p (n o) -> p n o", o=1),
                                         top2[:, :, 0:1], top2[:, :, 1:2], ALU.add))
            full = [P, NT, E_GROUPS, E_GROUPS]
            mine = bc(gs[:, :, :].rearrange("p i (g o) -> p i g o", o=1), full)
            other = bc(gs[:, :, :].rearrange("p i (o g) -> p i o g", o=1), full)
            nc.vector.tensor_tensor(cmp1[:, :, :, :], other, mine, ALU.is_gt)
            step(nc.vector.tensor_tensor(cmp2[:, :, :, :], other, mine, ALU.is_equal))
            for g in range(E_GROUPS):
                step(nc.vector.memset(cmp2[:, :, g, g:E_GROUPS], 0.0))
            step(nc.vector.tensor_tensor(cmp1[:, :, :, :], cmp1[:, :, :, :], cmp2[:, :, :, :], ALU.add))
            step(nc.vector.tensor_reduce(gm[:, :, :], cmp1[:, :, :, :], AX.X, ALU.add))
            step(nc.vector.tensor_scalar(gm[:, :, :], gm[:, :, :], float(E_TOPG), FMASK, ALU.is_ge, ALU.mult))
            step(nc.vector.tensor_tensor(
                sel[:, :, :].rearrange("p i (g m) -> p i g m", g=E_GROUPS), sel[:, :, :].rearrange("p i (g m) -> p i g m", g=E_GROUPS),
                bc(gm[:, :, :].rearrange("p i (g o) -> p i g o", o=1), [P, NT, E_GROUPS, E_PER]), ALU.add))
            for i in range(NT):
                ins = nc.vector.max(t8[:, i, :], sel[:, i, :])
            step(ins)
            for i in range(NT):
                ins = nc.vector.match_replace(wk[:, i, :], t8[:, i, :], sel[:, i, :], FMIN)
            step(ins)
            nc.vector.tensor_tensor(em[:, :, :], wk[:, :, :], sel[:, :, :], ALU.not_equal).then_inc(s_em, 1)
            dve.wait_ge(s_em, 1)
            step(nc.vector.tensor_tensor(wk[:, :, :], sco[:, :, :], em[:, :, :], ALU.mult))
            step(nc.vector.tensor_reduce(gsum[:, :], wk[:, :, :], AX.X, ALU.add))
            step(nc.vector.reciprocal(gsum[:, :], gsum[:, :]))
            dve.wait_ge(s_init, 2)
            gv = gt[:, 0:E_N, :, :].rearrange("p e i t -> p i e t")
            for i in range(NT):
                nc.vector.tensor_scalar(gv[:, i, :, 1], wk[:, i, :], gsum[:, i:i + 1], ROUTE_SCALE, ALU.mult, ALU.mult)
            for i in range(NT):
                ins = nc.vector.tensor_copy(gv[:, i, :, 0], bc(k[:, K_TOK + i:K_TOK + i + 1], [P, E_N]))
            step(ins)
            for f in range(FC):
                dve.wait_ge(s_sg, f + 1)
                nc.vector.tensor_tensor(uT[:, f, :], sg[:, f, :], ps[:, 2 + f, :], ALU.mult).then_inc(s_u, 1)
            dve.wait_ge(s_pos, 1)
            pp = ps[:, 6, 0:NT * E_N].rearrange("p (i e) -> p i e", i=NT)
            step(nc.vector.scalar_tensor_tensor(wk[:, :, :], pp, 1.0, em[:, :, :], ALU.add, ALU.mult))
            nc.vector.tensor_scalar(posm[:, 0:E_N * NT].rearrange("p (e i) -> p i e", i=NT), wk[:, :, :], -1.0, None, ALU.add)
            n_e, k_e, cum, at = (cnt[:, n, :] for n in range(4))
            step(nc.vector.tensor_copy(n_e, ps[:, 6, NT * E_N:(NT + 1) * E_N]))
            step(nc.vector.tensor_scalar(k_e, n_e, float(CAP), None, ALU.is_gt))
            for m in range(2, STEPS + 1):
                step(nc.vector.scalar_tensor_tensor(k_e, n_e, float(m * CAP), k_e, ALU.is_gt, ALU.add))
            step(nc.vector.tensor_tensor_scan(cum, k[:, K_ONES:K_ONES + E_N], k_e, 0.0, ALU.mult, ALU.add))
            step(nc.vector.tensor_scalar(at, cum, k[:, K_PART:K_PART + 1], None, ALU.is_le))
            step(nc.vector.tensor_reduce(tab[:, 0:1], at, AX.X, ALU.add))
            step(nc.vector.tensor_tensor(at, at, k_e, ALU.mult))
            step(nc.vector.tensor_reduce(tab[:, 1:2], at, AX.X, ALU.add))
            step(nc.vector.tensor_tensor(tab[:, 2:3], k[:, K_PART:K_PART + 1], tab[:, 1:2], ALU.subtract))
            step(nc.vector.tensor_scalar(tab[:, 2:3], tab[:, 2:3], 1.0, float(CAP), ALU.add, ALU.mult))
            step(nc.vector.tensor_scalar(diag[:, 0, :], ident, tab[:, 0:1], None, ALU.mult))
            nc.vector.tensor_scalar(diag[:, 1, :], ident, tab[:, 2:3], None, ALU.mult).then_inc(s_dg, 1)
            dve.wait_ge(s_tab, 1)
            step(nc.vector.tensor_copy(G.extra_base[:, :], ps[:, 7, P:2 * P]))
            step(nc.vector.tensor_copy(G.extra_tab[:, 0:P], ps[0:1, 7, 0:P]))
            nc.vector.tensor_copy(G.extra_tab[:, P:P + 1], cum[0:1, E_N - 1:E_N]).then_inc(s_tabd, 1)
            dve.wait_ge(s_tabd, 1)

        @block.tensor
        def _(pe):
            pe.wait_ge(G.s_wout, 16)
            for i in range(NT):
                for half in range(2):
                    for f in range(2 * HEADS):
                        ins = nc.tensor.matmul(ps[:, 2 * i + half, :], catT[:, f, i * P:(i + 1) * P],
                                               wout[:, f, 512 * half:512 * (half + 1)], start=f == 0, stop=f == 2 * HEADS - 1)
                ins.then_inc(s_y, 1)
            for i in range(NT):
                pe.wait_ge(s_h2, i + 1)
                for c in range(KC):
                    ins = nc.tensor.transpose(ps[:, 2 * i + c // 4, (c % 4) * P:(c % 4 + 1) * P], h2n[:, i, c:D:KC], ident)
                    if c % 4 == 3:
                        ins.then_inc(s_h2T, 1)
            pe.wait_ge(s_h2Td, 2 * NT)
            pe.wait_ge(s_in, 32)
            for i in range(NT):
                for c in range(KC):
                    ins = nc.tensor.matmul(ps[:, 6, i * E_N:(i + 1) * E_N], h2T[:, c, i * P:(i + 1) * P], wr[:, c, :],
                                           start=c == 0, stop=c == KC - 1)
                if i == NT - 1:
                    ins.then_inc(s_lg, NT)
            pe.wait_ge(s_wsh, 48)
            for f in range(FC):
                for b, w in ((f, wg), (2 + f, wu)):
                    for c in range(KC):
                        ins = nc.tensor.matmul(ps[:, b, :], w[:, c, f * P:(f + 1) * P], h2T[:, c, :], start=c == 0, stop=c == KC - 1)
                ins.then_inc(s_gu, 1)
            pe.wait_ge(s_em, 1)
            for i in range(NT):
                dst = ps[:, 6, i * E_N:(i + 1) * E_N]
                for n in range(i):
                    nc.tensor.matmul(dst, ones, em[:, n, :], start=n == 0, stop=False)
                nc.tensor.matmul(dst, k[:, K_STRICT:K_STRICT + P], em[:, i, :], start=i == 0, stop=True)
            for n in range(NT):
                ins = nc.tensor.matmul(ps[:, 6, NT * E_N:(NT + 1) * E_N], ones, em[:, n, :], start=n == 0, stop=n == NT - 1)
            ins.then_inc(s_pos, 1)
            pe.wait_ge(s_u, FC)
            for i in range(NT):
                b = 4 * (i % 2)
                if i >= 2:
                    pe.wait_ge(s_dnd, i - 1)
                for half in range(2):
                    for f in range(FC):
                        ins = nc.tensor.matmul(ps[:, b + half, :], uT[:, f, i * P:(i + 1) * P], wd[:, f, 512 * half:512 * (half + 1)],
                                               start=f == 0, stop=f == FC - 1)
                ins.then_inc(s_dn, 1)
            pe.wait_ge(s_dg, 1)
            for n in range(2):
                ins = nc.tensor.matmul(ps[:, 7, n * P:(n + 1) * P], ones, diag[:, n, :], start=True, stop=True)
            ins.then_inc(s_tab, 1)


RING = 4


def stage_experts(nc, A, G):
    with ExitStack() as own:
        def sb(name, shape, dt=F32):
            return own.enter_context(nc.sbuf_tensor(name, shape, dt))

        G.used = []

        def sem(name):
            G.used.append(own.enter_context(nc.semaphore(name)))
            return G.used[-1]

        k, ps, posm, gt = G.k, G.ps, G.posm, G.gt
        ident = k[:, K_ID:K_ID + P]
        wg = sb("wg", [P, RING, KC, DE])
        wu = sb("wu", [P, RING, KC, DE])
        wd = sb("wd", [P, RING, FC, D])
        pick = sb("pick", [P, 2, NT, CAP])
        found = sb("found", [CAP, 4, 2])
        gidx = sb("gather_rows", [CAP, 2], I32)
        sidx = sb("scatter_rows", [CAP, 4], I32)
        pad = sb("pad", [CAP, 2])
        xg = sb("xg", [CAP, 2, D])
        xT = sb("xT", [P, 2, KC, P])
        sg = sb("sg", [P, FC, P])
        uT = sb("uT", [P, 2, FC, P])
        yb = sb("yb", [CAP, 2, D])

        w_gate, w_up, w_down = A["w_exp_gate"][0], A["w_exp_up"][0], A["w_exp_down"][0]

        def load_weights(eng, e, slot, s_wgu, s_wd, before_down=None):
            eng.dma_start(wg[:, slot], w_gate[e].rearrange("(p c) f -> p c f", c=KC)).then_inc(s_wgu, 16)
            eng.dma_start(wu[:, slot], w_up[e].rearrange("(p c) f -> p c f", c=KC)).then_inc(s_wgu, 16)
            if before_down is not None:
                eng.wait_ge(*before_down)
            eng.dma_start(wd[:, slot], w_down[e].rearrange("(f p) n -> p f n", p=P)).then_inc(s_wd, 16)

        def pick_rows(q, n):
            step = q
            f = found[:, n, 0:1]
            step(nc.vector.tensor_scalar(gidx[:, n % 2:n % 2 + 1], f, -1.0, 0.0, ALU.add, ALU.max))
            step(nc.vector.tensor_scalar(pad[:, 0:1], f, 0.0, k[0:CAP, K_PADROW:K_PADROW + 1], ALU.is_equal, ALU.mult))
            return nc.vector.scalar_tensor_tensor(sidx[:, n:n + 1], f, -1.0, pad[:, 0:1], ALU.add, ALU.add)

        with ExitStack() as inner:
            def isem(name):
                return inner.enter_context(nc.semaphore(name))

            s_wgu = [isem(f"gate_up_landed{n}") for n in range(RING)]
            s_wd = [isem(f"down_landed{n}") for n in range(RING)]
            dch = isem("dve_chain")
            s_pick = isem("pick_built")
            s_find = isem("rows_found")
            s_idx = isem("row_numbers")
            s_g = [isem(f"gathered{n}") for n in range(2)]
            s_xp = isem("x_transposed")
            s_xd = isem("xT_low_copied")
            s_xa = isem("xT_high_copied")
            s_gu = isem("gate_up_done")
            s_sg = isem("silu_done")
            s_u = isem("u_ready")
            s_dn = isem("down_done")
            s_ya = isem("y_low_ready")
            s_yd = isem("y_high_ready")
            s_sc = isem("scattered")
            s_passed = isem("pool_waits_passed")
            block = inner.enter_context(nc.Block())

            @block.sync
            def _(sp):
                for e in range(RING):
                    load_weights(sp, e, e, s_wgu[e], s_wd[e])
                with sp.Fori(0, E_N // RING - 1) as t:
                    for n in range(RING):
                        sp.wait_ge(s_gu, RING * t + n + 1)
                        load_weights(sp, RING * t + (n + RING), n, s_wgu[n], s_wd[n],
                                     (s_dn, RING * t + n + 1))

            @block.gpsimd
            def _(pool):
                def gather(n, slot):
                    pool.indirect_dma_start(out=xg[:, slot, :], out_offset=None, in_=G.h2_rows,
                                            in_offset=bass.IndirectOffsetOnAxis(ap=gidx[:, slot:slot + 1], axis=0)).then_inc(s_g[slot], 16)

                for n in range(2):
                    pool.dma_start(G.y_rows[SEQ + n * 64:SEQ + (n + 1) * 64, :], G.xt[0:64, 0, :]).then_inc(s_sc, 16)
                for n in range(2):
                    pool.wait_ge(s_idx, n + 1)
                    gather(n, n)
                with pool.Fori(0, E_N // RING) as t:
                    for n in range(RING):
                        e = RING * t + n
                        pool.wait_ge(s_idx, e + 3)
                        pool.wait_ge(s_xp, e + 1)
                        pool.sem_inc(s_passed, 1)
                        gather(n, n % 2)
                        pool.wait_ge(s_ya, e + 2)
                        pool.wait_ge(s_yd, e + 2)
                        pool.wait_ge(s_sc, 16 * e + 32)
                        pool.sem_inc(s_passed, 1)
                        pool.indirect_dma_start(out=G.y_rows, out_offset=bass.IndirectOffsetOnAxis(ap=sidx[:, n:n + 1], axis=0),
                                                in_=yb[:, n % 2, :], in_offset=None, compute_op=ALU.add).then_inc(s_sc, 16)
                pool.wait_ge(s_sc, 16 * E_N + 32)
                pool.wait_ge(s_g[0], 16 * (E_N // 2 + 1))
                pool.wait_ge(s_g[1], 16 * (E_N // 2 + 1))

            @block.scalar
            def _(act):
                def copy_xT(slot, e1):
                    act.wait_ge(s_xp, e1)
                    nc.scalar.activation(xT[:, slot, 4:8, 0:CAP], ps[:, 1, :].rearrange("p (c t) -> p c t", c=4)[:, :, 0:CAP],
                                         ACT.Copy).then_inc(s_xa, 1)

                act.sem_inc(s_ya, 1)
                copy_xT(0, 1)
                with act.Fori(0, E_N // RING) as t:
                    for n in range(RING):
                        e = RING * t + n
                        act.wait_ge(s_gu, e + 1)
                        act.wait_ge(s_u, e + 1)
                        gate = ps[:, 2 + n % 2, 0:2 * P].rearrange("p (f t) -> p f t", f=FC)
                        nc.scalar.activation(sg[:, :, 0:CAP], gate[:, :, 0:CAP], ACT.Silu).then_inc(s_sg, 1)
                        copy_xT((n + 1) % 2, e + 2)
                        act.wait_ge(s_dn, e + 1)
                        act.wait_ge(s_sc, 16 * e + 16)
                        nc.scalar.activation(yb[:, n % 2, 0:512], ps[0:CAP, 4, :], ACT.Copy,
                                             scale=found[:, n, 1:2]).then_inc(s_ya, 1)

            @block.vector
            def _(dve):
                step = Chain(dve, dch)
                LINKS = 2 + 1
                count = [0]

                def build_pick(e, slot):
                    for i in range(NT):
                        ins = nc.vector.tensor_scalar(pick[:, slot, i, :], k[:, K_IOTA:K_IOTA + CAP],
                                                      posm[:, bass.ds(NT * e + i, 1)], None, ALU.is_equal)
                    ins.then_inc(s_pick, 1)

                def link(base):
                    def q(ins):
                        count[0] += 1
                        ins.then_inc(dch, 1)
                        dve.wait_ge(dch, base + count[0])
                    return q

                def read_found(e1, n, base):
                    dve.wait_ge(s_find, e1)
                    q = link(base)
                    q(nc.vector.tensor_copy(found[:, n, :], ps[0:CAP, 6 + n % 2, 0:2]))
                    pick_rows(q, n).then_inc(s_idx, 1)

                def copy_xT(slot, e1):
                    dve.wait_ge(s_xp, e1)
                    nc.vector.tensor_copy(xT[:, slot, 0:4, 0:CAP],
                                          ps[:, 0, :].rearrange("p (c t) -> p c t", c=4)[:, :, 0:CAP]).then_inc(s_xd, 1)

                dve.sem_inc(s_u, 1)
                dve.sem_inc(s_yd, 1)
                build_pick(0, 0)
                build_pick(1, 1)
                read_found(1, 0, 0)
                read_found(2, 1, 0)
                build_pick(2, 0)
                copy_xT(0, 1)
                first = count[0]
                with dve.Fori(0, E_N // RING) as t:
                    count[0] = 0
                    for n in range(RING):
                        e = RING * t + n
                        dve.wait_ge(s_sg, e + 1)
                        up = ps[:, 2 + n % 2, 2 * P:4 * P].rearrange("p (f t) -> p f t", f=FC)
                        nc.vector.tensor_tensor(uT[:, n % 2, :, 0:CAP], sg[:, :, 0:CAP], up[:, :, 0:CAP], ALU.mult).then_inc(s_u, 1)
                        dve.wait_ge(s_sc, 16 * e + 16)
                        read_found(e + 3, (n + 2) % RING, 3 * RING * t + first)
                        copy_xT((n + 1) % 2, e + 2)
                        dve.wait_ge(s_dn, e + 1)
                        nc.vector.tensor_scalar(yb[:, n % 2, 512:D], ps[0:CAP, 5, :], found[:, n, 1:2], None,
                                                ALU.mult).then_inc(s_yd, 1)
                        build_pick(e + 3, (n + 1) % 2)
                    assert count[0] == 3 * RING

            @block.tensor
            def _(pe):
                def find(e, n, slot):
                    pe.wait_ge(s_pick, e + 1)
                    for i in range(NT):
                        ins = nc.tensor.matmul(ps[0:CAP, 6 + slot, 0:2], pick[:, slot, i, :],
                                               gt[:, bass.ds(e, 1), i, :].rearrange("p o t -> p (o t)"), start=i == 0, stop=i == NT - 1)
                    ins.then_inc(s_find, 1)

                def transpose_x(slot, count):
                    pe.wait_ge(s_g[slot], count)
                    for c in range(KC):
                        ins = nc.tensor.transpose(ps[:, c // 4, (c % 4) * P:(c % 4) * P + CAP], xg[:, slot, c:D:KC], ident[0:CAP, 0:CAP])
                    ins.then_inc(s_xp, 1)

                find(0, 0, 0)
                find(1, 1, 1)
                transpose_x(0, 16)
                with pe.Fori(0, E_N // RING) as t:
                    for n in range(RING):
                        e = RING * t + n
                        pe.wait_ge(s_wgu[n], 32 * t + 32)
                        pe.wait_ge(s_xd, e + 1)
                        pe.wait_ge(s_xa, e + 1)
                        for m, w in ((0, wg), (1, wu)):
                            for f in range(FC):
                                at = (2 * m + f) * P
                                for c in range(KC):
                                    ins = nc.tensor.matmul(ps[:, 2 + n % 2, at:at + CAP], w[:, n, c, f * P:(f + 1) * P],
                                                           xT[:, n % 2, c, 0:CAP], start=c == 0, stop=c == KC - 1)
                        ins.then_inc(s_gu, 1)
                        pe.wait_ge(s_idx, e + 1)
                        find(e + 2, n, n % 2)
                        transpose_x((n + 1) % 2, 32 * t + 16 * ((n + 1) // 2) + 16)
                        pe.wait_ge(s_wd[n], 16 * t + 16)
                        pe.wait_ge(s_u, e + 2)
                        pe.wait_ge(s_ya, e + 1)
                        pe.wait_ge(s_yd, e + 1)
                        for half in range(2):
                            for f in range(FC):
                                ins = nc.tensor.matmul(ps[0:CAP, 4 + half, :], uT[:, n % 2, f, 0:CAP],
                                                       wd[:, n, f, 512 * half:512 * (half + 1)], start=f == 0, stop=f == FC - 1)
                        ins.then_inc(s_dn, 1)

        with ExitStack() as inner:
            def isem(name):
                return inner.enter_context(nc.semaphore(name))

            s_wgu, s_wd = isem("x_gate_up_landed"), isem("x_down_landed")
            dch = isem("dve_chain")
            s_pick, s_find, s_idx, s_g = isem("x_pick_built"), isem("x_rows_found"), isem("x_row_numbers"), isem("x_gathered")
            s_xp, s_xd, s_xa = isem("x_x_transposed"), isem("x_xT_low_copied"), isem("x_xT_high_copied")
            s_gu, s_sg, s_u, s_dn = isem("x_gate_up_done"), isem("x_silu_done"), isem("x_u_ready"), isem("x_down_done")
            s_ya, s_yd, s_sc = isem("x_y_low_ready"), isem("x_y_high_ready"), isem("x_scattered")
            s_added, s_passed = isem("x_tile_added"), isem("x_pool_waits_passed")
            block = inner.enter_context(nc.Block())

            def extra_tiles(eng, body):
                total = eng.value_load(G.extra_tab[0:1, P:P + 1], min_val=0, max_val=MAX_EXTRA)
                with eng.If(total > 0):
                    with eng.Fori(0, MAX_EXTRA) as j:
                        with eng.If(total > j):
                            body(j)

            def expert_of(eng, j):
                return eng.value_load(G.extra_tab[0:1, bass.ds(j, 1)], min_val=0, max_val=E_N - 1)

            @block.sync
            def _(sp):
                def body(j):
                    sp.wait_ge(s_dn, j + 1)
                    load_weights(sp, expert_of(sp, j), 0, s_wgu, s_wd)

                sp.sem_inc(s_dn, 1)
                extra_tiles(sp, body)

            @block.gpsimd
            def _(pool):
                def body(j):
                    pool.wait_ge(s_idx, j + 1)
                    pool.sem_inc(s_passed, 1)
                    pool.indirect_dma_start(out=xg[:, 0, :], out_offset=None, in_=G.h2_rows,
                                            in_offset=bass.IndirectOffsetOnAxis(ap=gidx[:, 0:1], axis=0)).then_inc(s_g, 16)
                    pool.wait_ge(s_ya, j + 1)
                    pool.wait_ge(s_yd, j + 1)
                    pool.sem_inc(s_passed, 1)
                    pool.indirect_dma_start(out=G.y_rows, out_offset=bass.IndirectOffsetOnAxis(ap=sidx[:, 0:1], axis=0),
                                            in_=yb[:, 0, :], in_offset=None, compute_op=ALU.add).then_inc(s_sc, 16)
                    pool.wait_ge(s_sc, 16 * j + 16)
                    pool.sem_inc(s_added, 1)

                pool.sem_inc(s_added, 1)
                extra_tiles(pool, body)

            @block.scalar
            def _(act):
                def body(j):
                    act.wait_ge(s_xp, j + 1)
                    nc.scalar.activation(xT[:, 0, 4:8, 0:CAP], ps[:, 1, :].rearrange("p (c t) -> p c t", c=4)[:, :, 0:CAP],
                                         ACT.Copy).then_inc(s_xa, 1)
                    act.wait_ge(s_gu, j + 1)
                    gate = ps[:, 2, 0:2 * P].rearrange("p (f t) -> p f t", f=FC)
                    nc.scalar.activation(sg[:, :, 0:CAP], gate[:, :, 0:CAP], ACT.Silu).then_inc(s_sg, 1)
                    act.wait_ge(s_dn, j + 2)
                    nc.scalar.activation(yb[:, 0, 0:512], ps[0:CAP, 4, :], ACT.Copy, scale=found[:, 0, 1:2]).then_inc(s_ya, 1)

                extra_tiles(act, body)

            @block.vector
            def _(dve):
                def body(j):
                    e = expert_of(dve, j)
                    dve.wait_ge(s_added, j + 1)
                    for i in range(NT):
                        ins = nc.vector.tensor_scalar(pick[:, 0, i, :], k[:, K_IOTA:K_IOTA + CAP], G.extra_base[:, bass.ds(j, 1)],
                                                      posm[:, bass.ds(NT * e + i, 1)], ALU.add, ALU.is_equal)
                    ins.then_inc(s_pick, 1)
                    dve.wait_ge(s_find, j + 1)
                    count = [0]

                    def q(ins):
                        count[0] += 1
                        ins.then_inc(dch, 1)
                        dve.wait_ge(dch, 3 * j + count[0])

                    q(nc.vector.tensor_copy(found[:, 0, :], ps[0:CAP, 6, 0:2]))
                    pick_rows(q, 0).then_inc(s_idx, 1)
                    dve.wait_ge(s_xp, j + 1)
                    nc.vector.tensor_copy(xT[:, 0, 0:4, 0:CAP], ps[:, 0, :].rearrange("p (c t) -> p c t", c=4)[:, :, 0:CAP]).then_inc(s_xd, 1)
                    dve.wait_ge(s_sg, j + 1)
                    up = ps[:, 2, 2 * P:4 * P].rearrange("p (f t) -> p f t", f=FC)
                    nc.vector.tensor_tensor(uT[:, 0, :, 0:CAP], sg[:, :, 0:CAP], up[:, :, 0:CAP], ALU.mult).then_inc(s_u, 1)
                    dve.wait_ge(s_dn, j + 2)
                    nc.vector.tensor_scalar(yb[:, 0, 512:D], ps[0:CAP, 5, :], found[:, 0, 1:2], None, ALU.mult).then_inc(s_yd, 1)

                extra_tiles(dve, body)

            @block.tensor
            def _(pe):
                def body(j):
                    e = expert_of(pe, j)
                    pe.wait_ge(s_pick, j + 1)
                    for i in range(NT):
                        ins = nc.tensor.matmul(ps[0:CAP, 6, 0:2], pick[:, 0, i, :],
                                               gt[:, bass.ds(e, 1), i, :].rearrange("p o t -> p (o t)"), start=i == 0, stop=i == NT - 1)
                    ins.then_inc(s_find, 1)
                    pe.wait_ge(s_g, 16 * j + 16)
                    for c in range(KC):
                        ins = nc.tensor.transpose(ps[:, c // 4, (c % 4) * P:(c % 4) * P + CAP], xg[:, 0, c:D:KC], ident[0:CAP, 0:CAP])
                    ins.then_inc(s_xp, 1)
                    pe.wait_ge(s_wgu, 32 * j + 32)
                    pe.wait_ge(s_xd, j + 1)
                    pe.wait_ge(s_xa, j + 1)
                    for m, w in ((0, wg), (1, wu)):
                        for f in range(FC):
                            at = (2 * m + f) * P
                            for c in range(KC):
                                ins = nc.tensor.matmul(ps[:, 2, at:at + CAP], w[:, 0, c, f * P:(f + 1) * P], xT[:, 0, c, 0:CAP],
                                                       start=c == 0, stop=c == KC - 1)
                    ins.then_inc(s_gu, 1)
                    pe.wait_ge(s_wd, 16 * j + 16)
                    pe.wait_ge(s_u, j + 1)
                    for half in range(2):
                        for f in range(FC):
                            ins = nc.tensor.matmul(ps[0:CAP, 4 + half, :], uT[:, 0, f, 0:CAP], wd[:, 0, f, 512 * half:512 * (half + 1)],
                                                   start=f == 0, stop=f == FC - 1)
                    ins.then_inc(s_dn, 1)

                extra_tiles(pe, body)

        stage_final(nc, A, G)


def stage_final(nc, A, G):
    with ExitStack() as own:
        def sb(name, shape, dt=F32):
            return own.enter_context(nc.sbuf_tensor(name, shape, dt))

        G.used = []

        def sem(name):
            G.used.append(own.enter_context(nc.semaphore(name)))
            return G.used[-1]

        xt, rows = G.xt, G.rows
        y = sb("y_final", [P, NT, D])
        sq = sb("sq_final", [P, 2, D])
        ss = sb("ss_final", [P, NT])
        rt = sb("rt_final", [P, NT])
        s_in = [sem(f"y_landed{i}") for i in range(NT)]
        s_sq, s_ms, s_rt, s_o, s_out = sem("y_squares"), sem("y_mean_square"), sem("y_root"), sem("out_ready"), sem("out_stored")
        dch = sem("dve_chain")
        block = own.enter_context(nc.Block())

        @block.sync
        def _(sp):
            for i in range(NT):
                sp.dma_start(y[:, i, :], G.y_rows[i * P:(i + 1) * P, :]).then_inc(s_in[i], 16)
            for i in range(NT):
                sp.wait_ge(s_o, i + 1)
                sp.dma_start(G.out[0, i * P:(i + 1) * P, :], xt[:, i, :]).then_inc(s_out, 16)
            sp.wait_ge(s_out, 16 * NT)

        @block.scalar
        def _(act):
            for i in range(NT):
                act.wait_ge(s_in[i], 16)
                nc.scalar.activation(sq[:, i % 2, :], y[:, i, :], ACT.Square, accum_out=ss[:, i:i + 1]).then_inc(s_sq, 1)
                act.wait_ge(s_ms, i + 1)
                nc.scalar.activation(rt[:, i:i + 1], ss[:, i:i + 1], ACT.Sqrt).then_inc(s_rt, 1)

        @block.vector
        def _(dve):
            step = Chain(dve, dch)
            for i in range(NT):
                dve.wait_ge(s_sq, i + 1)
                nc.vector.tensor_scalar(ss[:, i:i + 1], ss[:, i:i + 1], 1.0 / D, EPS, ALU.mult, ALU.add).then_inc(s_ms, 1)
                dve.wait_ge(s_rt, i + 1)
                step(nc.vector.reciprocal(rt[:, i:i + 1], rt[:, i:i + 1]))
                step(nc.vector.scalar_tensor_tensor(y[:, i, :], y[:, i, :], rt[:, i:i + 1], rows[:, 3, :], ALU.mult, ALU.mult))
                nc.vector.tensor_tensor(xt[:, i, :], xt[:, i, :], y[:, i, :], ALU.add).then_inc(s_o, 1)


def clear_semaphores(nc, sems):
    with nc.Block() as block:
        @block.gpsimd
        def _(pool):
            for s in sems:
                pool.sem_clear(s)


class Shared:
    pass


def build(nc, A, out):
    with ExitStack() as ctx:
        def sb(name, shape, dt=F32):
            return ctx.enter_context(nc.sbuf_tensor(name, shape, dt))

        G = Shared()
        G.ps = ctx.enter_context(nc.psum_tensor("ps", [P, 8, 512], F32))
        G.k = sb("consts", [P, K_W])
        G.cols = sb("cols", [P, 44])
        G.rows = sb("rows", [P, 4, D])
        G.maskb = sb("maskb", [P, NT, SEQ])
        G.xt = sb("xt", [P, NT, D])
        G.s_roped = ctx.enter_context(nc.semaphore("attention_rotated"))
        G.s_wout = ctx.enter_context(nc.semaphore("w_out_landed"))
        G.posm = sb("place_in_expert", [P, E_PAD * NT])
        G.gt = sb("gate_and_token", [P, E_PAD, NT, 2])
        G.extra_base = sb("extra_base", [P, P])
        G.extra_tab = sb("extra_tab", [1, P + 1], I32)
        G.h2_rows = nc.dram_tensor("h2_rows", (SEQ, D), F32, kind="Internal").ap()
        G.y_rows = nc.dram_tensor("y_rows", (SEQ + P, D), F32, kind="Internal").ap()
        G.out = out
        with ExitStack() as mid:
            G.nat = mid.enter_context(nc.sbuf_tensor("nat", [P, NT, NAT_W], F32))
            G.qkc = mid.enter_context(nc.sbuf_tensor("qkc", [P, 2 * HEADS, SEQ], F32))
            stage_in(nc, ctx, A, G)
            clear_semaphores(nc, G.used)
            G.catT = mid.enter_context(nc.sbuf_tensor("catT", [P, 2 * HEADS, SEQ], F32))
            G.wout = mid.enter_context(nc.sbuf_tensor("wout", [P, 2 * HEADS, D], F32))
            G.arena = mid.enter_context(nc.sbuf_tensor("arena", [P, 6144], F32))
            stage_attention(nc, A, G)
            clear_semaphores(nc, G.used)
            stage_route(nc, A, G)
        stage_experts(nc, A, G)


INS = ["x", "c", "w_ada", "b_ada", "g_mix_pre", "g_mix_post", "g_ffn_pre", "g_ffn_post", "w_in", "conv_w", "conv_b",
       "b_igate", "b_fgate", "g_mlstm_head", "g_idx_k", "b_idx_k", "w_out", "w_router", "b_router", "w_exp_gate",
       "w_exp_up", "w_exp_down", "w_sh_gate", "w_sh_up", "w_sh_down"]


def kernel(**inputs):
    import concourse.bacc as bacc
    from concourse.bass_utils import run_bass_kernel_spmd

    nc = bacc.Bacc("TRN2", target_bir_lowering=False, num_devices=1)
    arrays = {f"in_{n}": np.ascontiguousarray(inputs[n]) for n in INS}
    arrays["in_consts"] = constants()
    A = {n[3:]: nc.dram_tensor(n, a.shape, mybir.dt.from_np(a.dtype), kind="ExternalInput").ap() for n, a in arrays.items()}
    out = nc.dram_tensor("out_y", (1, SEQ, D), F32, kind="ExternalOutput").ap()
    build(nc, A, out)
    return run_bass_kernel_spmd(nc, [arrays], core_ids=[0]).results[0]["out_y"]
```

```python
from contextlib import ExitStack

import numpy as np

import concourse.bass as bass
from concourse import mybir

F32 = mybir.dt.float32
FR = mybir.dt.float32r
BF16 = mybir.dt.bfloat16
I32 = mybir.dt.int32
ALU = mybir.AluOpType
ACT = mybir.ActivationFunctionType
AX = mybir.AxisListType

P = 128
SEQ = 512
D = 1024
NT = SEQ // P
KC = D // P
CHUNK = 64
HEADS = 4
DH = 128
IH = 4
IDIM = 64
CONV = 4
TOPK = 128
THETA = 500000.0
E_N = 64
E_GROUPS = 8
E_PER = E_N // E_GROUPS
E_TOPG = 4
DE = 256
FC = DE // P
ROUTE_SCALE = 2.5
EPS = 1e-6
NEG = -1e30
FMIN = -3.4028234e38
FMASK = -3.0e38
CAP = 104
MAX_EXTRA = SEQ * 8 // CAP
STEPS = (SEQ - 1) // CAP
E_PAD = E_N + 3

QK_W = 2 * HEADS * DH
V0 = 0
O0 = V0 + HEADS * DH
I0 = O0 + HEADS * DH
F0 = I0 + HEADS
AQ0 = F0 + HEADS
AK0 = AQ0 + HEADS * DH
AV0 = AK0 + DH
IQ0 = AV0 + DH
IK0 = IQ0 + IH * IDIM
IW0 = IK0 + IDIM
NAT_W = IW0 + IH
ROT_A = DH // 4 // 2
ROT_I = IDIM // 4 // 2

K_ID = 0
K_TRI = K_ID + P
K_STRICT = K_TRI + P
K_ONES = K_STRICT + P
K_IOTA = K_ONES + P
K_SEL = K_IOTA + P
K_CAUSAL = K_SEL + HEADS * P
K_TOKH = K_CAUSAL + P
K_TOKL = K_TOKH + NT
K_PADROW = K_TOKL + NT
K_PART = K_PADROW + 1
K_COSA = K_PART + 1
K_SINA = K_COSA + NT * ROT_A
K_COSI = K_SINA + NT * ROT_A
K_SINI = K_COSI + NT * ROT_I
K_W = K_SINI + NT * ROT_I


def constants():
    k = np.zeros((P, K_W), np.float32)
    i = np.arange(P)
    k[:, K_ID:K_ID + P] = np.eye(P)
    k[:, K_TRI:K_TRI + P] = np.where(i[:, None] <= i[None, :], 0.0, NEG)
    k[:, K_STRICT:K_STRICT + P] = i[:, None] < i[None, :]
    k[:, K_ONES:K_ONES + P] = 1.0
    k[:, K_IOTA:K_IOTA + P] = i[None, :]
    for h in range(HEADS):
        k[h, K_SEL + h * P:K_SEL + (h + 1) * P] = 1.0
    k[:, K_CAUSAL:K_CAUSAL + P] = np.where(i[None, :] // CHUNK <= i[:, None] // CHUNK, 0.0, NEG)
    tok = i[:, None] + P * np.arange(NT)[None, :] + 1
    k[:, K_TOKH:K_TOKH + NT] = tok // 256 * 256
    k[:, K_TOKL:K_TOKL + NT] = tok % 256
    k[:, K_PADROW] = SEQ + 1 + i
    k[:, K_PART] = i
    for half, at_cos, at_sin in ((ROT_A, K_COSA, K_SINA), (ROT_I, K_COSI, K_SINI)):
        inv = np.exp(-np.log(np.float32(THETA)) * np.arange(half, dtype=np.float32) * np.float32(1.0 / half))
        ang = np.arange(SEQ, dtype=np.float32)[:, None] * inv.astype(np.float32)[None, :]
        for at, f in ((at_cos, np.cos), (at_sin, np.sin)):
            k[:, at:at + NT * half] = f(ang).reshape(NT, P, half).transpose(1, 0, 2).reshape(P, NT * half)
    return k


class Chain:

    def __init__(self, eng, sem):
        self.eng, self.sem, self.n = eng, sem, 0

    def __call__(self, ins):
        self.n += 1
        ins.then_inc(self.sem, 1)
        self.eng.wait_ge(self.sem, self.n)


SLOTS = 4
SLOT_W = 2176
NAT_PIECES = [(1852, 272), (1586, 266), (1320, 266), (1056, 264), (792, 264), (528, 264), (264, 264), (0, 264)]
QK_PIECES = 4
ADA = [("ada", s, q) for s in range(2) for q in range(4)]
ROWS = [("row", s, q) for s in range(2, 6) for q in range(4)]
ITEMS = [("nat", n, 0) for n in range(5)] + [("qk", n, 0) for n in range(QK_PIECES)] + [("nat", n, 0) for n in range(5, 8)]
STREAM = (ADA + ITEMS[0:2] + ROWS[0:2] + ITEMS[2:3] + ROWS[2:5] + ITEMS[3:5] + ROWS[5:7] + ITEMS[5:] + ROWS[7:])


def stage_in(nc, A, G):
    with ExitStack() as own:
        def sb(name, shape, dt=F32):
            return own.enter_context(nc.sbuf_tensor(name, shape, dt))

        G.used = []

        def sem(name):
            G.used.append(own.enter_context(nc.semaphore(name)))
            return G.used[-1]

        k, nat, qkc, rows, maskb, cols, ps = G.k, G.nat, G.qkc, G.rows, G.maskb, G.cols, G.ps
        ident = k[:, K_ID:K_ID + P]
        free = G.big[:, G.FREE:G.FREE + 10240]
        stage = free[:, 0:SLOTS * SLOT_W].rearrange("p (s n) -> p s n", s=SLOTS)
        tmp = free[:, SLOTS * SLOT_W:SLOTS * SLOT_W + 1024].rearrange("p (b n) -> p b n", b=2)
        work = free[:, SLOTS * SLOT_W + 1024:SLOTS * SLOT_W + 1536]
        x_in = G.big[:, 0:NT * D].rearrange("p (i d) -> p i d", i=NT)
        hf = G.big[:, 0:KC * SEQ].rearrange("p (c t) -> p c t", c=KC)
        xn = G.big[:, G.QKC:G.QKC + NT * D].rearrange("p (i d) -> p i d", i=NT)
        acc = maskb[:, :, :].rearrange("p i t -> p (i t)").rearrange("p (s n) -> p s n", s=2)
        hhi = sb("hT_hi", [P, KC, SEQ], FR)
        hlo = sb("hT_lo", [P, KC, SEQ], FR)
        whi = sb("w_hi", [P, 2, SLOT_W], FR)
        wlo = sb("w_lo", [P, 2, SLOT_W], FR)
        flat = G.xt[:, :, :].rearrange("p i d -> p (i d)")
        RAW = 4 * (SEQ + CONV - 1)
        raw = flat[:, 0:RAW].rearrange("p (b n) -> p b n", b=4)
        ropet = flat[:, RAW:RAW + 4 * NT * HEADS * ROT_A].rearrange("p (n i h d) -> p n i h d", n=4, i=NT, h=HEADS)
        ikT = flat[0:IDIM, 3200:3200 + SEQ]
        lnb = flat[:, 3712:3712 + NT * IDIM].rearrange("p (i d) -> p i d", i=NT)
        cT = sb("cT", [P, KC])
        cs = sb("cs", [P, KC])
        gpre = sb("gpre", [P, KC])
        bcol = sb("bcol", [P, 2, KC])
        modA = sb("modA", [P, KC])
        modB = sb("modB", [P, KC])
        colrows = sb("colrows", [44, P])
        gik = sb("gik", [P, IDIM])
        bik = sb("bik", [P, IDIM])
        ss = sb("ss", [P, 4 * NT])
        rs = sb("rs", [P, 4 * NT])
        iqT = raw[0:IDIM, :, CONV - 1:]
        iwS = flat[:, 3104:3104 + NT * IH].rearrange("p (i h) -> p i h", i=NT)
        relu = tmp
        top8 = flat[:, 3136:3144]

        s_in = sem("in_small")
        s_c = sem("c_landed")
        s_bias = sem("biases_landed")
        s_x = sem("in_x")
        landed = [sem(f"piece_landed{i}") for i in range(SLOTS)]
        s_ada_used = sem("ada_piece_used")
        s_row_used = sem("row_piece_used")
        dch, ach, pch = sem("dve_chain"), sem("act_chain"), sem("pool_chain")
        s_silu = sem("c_silu")
        s_ssq = sem("x_squares")
        s_ms = sem("x_mean_square")
        s_rt = sem("x_root")
        s_xn = sem("x_normed")
        s_cols = sem("cols_transposed")
        s_colsd = sem("cols_copied")
        s_mod = sem("mod_columns")
        s_modd = sem("mod_ready")
        s_xT = sem("x_transposed")
        s_hf = sem("h_modulated")
        s_hhi = sem("h_hi")
        s_hlo = sem("h_lo")
        s_whi = sem("w_hi_ready")
        s_wlo = sem("w_lo_ready")
        s_nat = sem("projected")
        s_natd = sem("projection_copied")
        s_conv = sem("conv_done")
        s_qk = sem("qk_activated")
        s_zero = sem("conv_pad_zero")
        s_lnv = sem("ik_variance")
        s_ln = sem("ik_normed")
        s_lnr = sem("ik_root")
        s_rope = sem("indexer_rotated")
        s_iT = sem("indexer_transposed")
        s_iTd = sem("indexer_T_copied")
        s_rel = sem("indexer_products")
        s_relu = sem("indexer_relu")
        s_sc = sem("indexer_summed")
        s_iw = sem("indexer_weights")

        first, n_out = [], 0
        for kind, _, _ in ITEMS:
            first.append(n_out)
            n_out += NT if kind == "nat" else 2
        QK_FIRST = first[5]
        IDX_DONE = first[2]
        freed, count = [], {"ada": 0, "row": 0}
        for piece in STREAM:
            if piece[0] in count:
                count[piece[0]] += 1
                freed.append(({"row": s_row_used, "ada": s_ada_used}[piece[0]], count[piece[0]]))
            else:
                freed.append((s_wlo, ITEMS.index(piece) + 1))
        place = {piece: n for n, piece in enumerate(STREAM)}

        def arrived(eng, piece):
            n = place[piece]
            eng.wait_ge(landed[n % SLOTS], 16 * (n // SLOTS + 1))
            return n % SLOTS

        def width(piece):
            return NAT_PIECES[piece[1]][1] if piece[0] == "nat" else 256

        block = own.enter_context(nc.Block())

        @block.sync
        def _(sp):
            sp.dma_start(cT[:, :], A["c"].rearrange("a (p c) -> (a p) c", c=KC)).then_inc(s_c, 16)
            w_ada = A["w_ada"][0].rearrange("(p c) n -> p c n", c=KC)
            w_in = A["w_in"][0].rearrange("(p c) n -> p c n", c=KC)
            for n, piece in enumerate(STREAM):
                kind, a, b = piece
                if n >= SLOTS:
                    sp.wait_ge(*freed[n - SLOTS])
                if kind in ("ada", "row"):
                    dst = stage[:, n % SLOTS, 0:2 * D].rearrange("p (c n) -> p c n", c=2)
                    src = w_ada[:, 2 * b:2 * b + 2, a * D:(a + 1) * D]
                else:
                    w = width(piece)
                    c0 = a * 256 if kind == "qk" else QK_W + NAT_PIECES[a][0]
                    dst = stage[:, n % SLOTS, 0:KC * w].rearrange("p (c n) -> p c n", c=KC)
                    src = w_in[:, :, c0:c0 + w]
                sp.dma_start(dst, src).then_inc(landed[n % SLOTS], 16)
                if n == 1:
                    sp.dma_start(x_in, A["x"][0].rearrange("(i p) d -> p i d", p=P)).then_inc(s_x, 16)

        @block.gpsimd
        def _(pool):
            step = Chain(pool, pch)
            nc.gpsimd.memset(rows[:, :, :], 0.0).then_inc(s_zero, 1)
            nc.gpsimd.memset(raw[:, :, 0:CONV - 1], 0.0).then_inc(s_zero, 1)

            def low_part(m):
                n = KC * width(ITEMS[m])
                pool.wait_ge(s_whi, m + 1)
                nc.gpsimd.tensor_tensor(wlo[:, m % 2, 0:n], stage[:, place[ITEMS[m]] % SLOTS, 0:n],
                                        whi[:, m % 2, 0:n].bitcast(F32), ALU.subtract).then_inc(s_wlo, 1)

            def rope(at, heads, dim, half, cos_at, sin_at, last):
                v = nat[:, :, at:at + heads * dim].rearrange("p i (h d) -> p i h d", h=heads)
                x1, x2 = v[:, :, :, 0:half], v[:, :, :, half:2 * half]

                def table(c):
                    t = k[:, c:c + NT * half].rearrange("p (i o d) -> p i o d", i=NT, o=1)
                    return t.broadcast_to([P, NT, heads, half])

                t = [ropet[:, n, :, 0:heads, 0:half] for n in range(4)]
                nc.gpsimd.tensor_tensor(t[0], x1, table(cos_at), ALU.mult)
                nc.gpsimd.tensor_tensor(t[1], x2, table(sin_at), ALU.mult)
                nc.gpsimd.tensor_tensor(t[2], x2, table(cos_at), ALU.mult)
                step(nc.gpsimd.tensor_tensor(t[3], x1, table(sin_at), ALU.mult))
                nc.gpsimd.tensor_tensor(x1, t[0], t[1], ALU.subtract)
                ins = nc.gpsimd.tensor_tensor(x2, t[2], t[3], ALU.add)
                step(ins) if last is None else ins.then_inc(last, 1)

            for m in range(3):
                low_part(m)
            pool.wait_ge(s_in, 16 * 8)
            pool.wait_ge(s_natd, IDX_DONE)
            nc.gpsimd.tensor_scalar(iwS[:, :, :], nat[:, :, IW0:IW0 + IH], (IH ** -0.5) * (IDIM ** -0.5), None,
                                    ALU.mult).then_inc(s_iw, 1)
            rope(IQ0, IH, IDIM, ROT_I, K_COSI, K_SINI, None)
            low_part(3)
            pool.wait_ge(s_ln, 1)
            rope(IK0, 1, IDIM, ROT_I, K_COSI, K_SINI, s_rope)
            for m in range(4, 7):
                low_part(m)
            pool.wait_ge(s_natd, first[5])
            rope(AK0, 1, DH, ROT_A, K_COSA, K_SINA, None)
            rope(AQ0, HEADS, DH, ROT_A, K_COSA, K_SINA, G.s_roped)
            for m in range(7, len(ITEMS)):
                low_part(m)

        @block.scalar
        def _(act):
            step = Chain(act, ach)
            act.dma_start(k[:, :], A["consts"]).then_inc(s_in, 16)
            act.dma_start(gpre[:, :], A["g_mix_pre"].rearrange("a (p c) -> (a p) c", c=KC)).then_inc(s_in, 16)
            act.dma_start(bcol[:, :, :], A["b_ada"][0, 0:2 * D].rearrange("(s p c) -> p s c", s=2, c=KC)).then_inc(s_in, 16)
            act.dma_start(colrows[0:32, :], A["conv_w"][0].rearrange("j (n p) -> (j n) p", p=P)).then_inc(s_in, 16)
            act.dma_start(colrows[32:40, :], A["conv_b"][0].rearrange("(n p) -> n p", p=P)).then_inc(s_in, 16)
            act.dma_start(colrows[40:44, :], A["g_mlstm_head"][0].rearrange("(n p) -> n p", p=P)).then_inc(s_in, 16)
            act.dma_start(gik[:, :], A["g_idx_k"].broadcast_to([P, IDIM])).then_inc(s_in, 16)
            act.dma_start(bik[:, :], A["b_idx_k"].broadcast_to([P, IDIM])).then_inc(s_in, 16)
            act.dma_start(G.gb[:, 0:1], A["b_igate"].rearrange("a h -> h a")).then_inc(s_bias, 16)
            act.dma_start(G.gb[:, 1:2], A["b_fgate"].rearrange("a h -> h a")).then_inc(s_bias, 16)
            act.wait_ge(s_zero, 1)
            act.dma_start(rows[0:1, :, :], A["b_ada"][:, 2 * D:6 * D].rearrange("a (s d) -> a s d", s=4)).then_inc(s_bias, 16)
            act.wait_ge(s_c, 16)
            nc.scalar.activation(cs[:, :], cT[:, :], ACT.Silu).then_inc(s_silu, 1)
            act.wait_ge(s_x, 16)
            for i in range(NT):
                nc.scalar.activation(xn[:, i, :], x_in[:, i, :], ACT.Square, accum_out=ss[:, i:i + 1]).then_inc(s_ssq, 1)
            act.wait_ge(s_ms, 1)
            step(nc.scalar.activation(rs[:, 0:NT], ss[:, NT:2 * NT], ACT.Sqrt))
            nc.scalar.activation(rs[:, NT:2 * NT], rs[:, 0:NT], ACT.Copy).then_inc(s_rt, 1)
            act.wait_ge(s_xn, 1)
            for i in range(NT):
                nc.scalar.activation(xn[:, i, :], x_in[:, i, :], ACT.Copy, scale=rs[:, i:i + 1]).then_inc(s_xn, 1)

            def high_part(m):
                n = KC * width(ITEMS[m])
                slot = arrived(act, ITEMS[m])
                if m >= 2:
                    act.wait_ge(s_nat, first[m - 1])
                nc.scalar.activation(whi[:, m % 2, 0:n], stage[:, slot, 0:n], ACT.Copy).then_inc(s_whi, 1)

            act.wait_ge(s_modd, 1)
            for c in range(KC):
                act.wait_ge(s_xT, c + 1)
                nc.scalar.activation(hf[:, c, :], ps[:, c, :], ACT.Identity, bias=modB[:, c:c + 1],
                                     scale=modA[:, c:c + 1]).then_inc(s_hf, 1)
                if c == 1:
                    high_part(0)
            high_part(1)

            def copy_nat(m):
                c0, w = NAT_PIECES[ITEMS[m][1]]
                for i in range(NT):
                    n = first[m] + i
                    act.wait_ge(s_nat, n + 1)
                    nc.scalar.activation(nat[:, i, c0:c0 + w], ps[:, n % 4, 0:w], ACT.Copy).then_inc(s_natd, 1)

            copy_nat(0)
            high_part(2)
            copy_nat(1)
            high_part(3)
            act.wait_ge(s_lnv, 1)
            nc.scalar.activation(rs[:, NT:2 * NT], ss[:, 2 * NT:3 * NT], ACT.Sqrt).then_inc(s_lnr, 1)
            copy_nat(2)
            for t in range(NT):
                act.wait_ge(s_iT, t + 1)
                nc.scalar.activation(iqT[:, :, t * P:(t + 1) * P],
                                     ps[0:IDIM, 4 + t % 2, :].rearrange("p (h t) -> p h t", h=IH), ACT.Copy).then_inc(s_iTd, 1)
            act.wait_ge(s_iT, NT + 1)
            nc.scalar.activation(ikT[:, :], ps[0:IDIM, 6, :], ACT.Copy).then_inc(s_iTd, 1)
            high_part(4)
            for i in range(1, NT):
                for h in range(IH):
                    u = (i - 1) * IH + h
                    act.wait_ge(s_rel, u + 1)
                    if u >= 2:
                        act.wait_ge(s_sc, u - 1)
                    w = P * (i + 1)
                    nc.scalar.activation(relu[:, u % 2, 0:w], ps[:, 4 + u % 4, 0:w], ACT.Relu).then_inc(s_relu, 1)
            copy_nat(3)
            high_part(5)
            copy_nat(4)
            high_part(6)

            def silu_qk(c):
                act.wait_ge(s_conv, c + 1)
                nc.scalar.activation(qkc[:, c, :], tmp[:, c % 2, :], ACT.Silu,
                                     bias=cols[:, 32 + c:33 + c]).then_inc(s_qk, 1)

            act.wait_ge(s_zero, 2)
            act.wait_ge(s_colsd, 1)
            for c in range(2 * HEADS):
                n = QK_FIRST + c
                act.wait_ge(s_nat, n + 1)
                if c >= 4:
                    act.wait_ge(s_conv, c - 3)
                nc.scalar.activation(raw[:, c % 4, CONV - 1:], ps[:, n % 4, :], ACT.Copy).then_inc(s_natd, 1)
                if c % 2:
                    high_part(7 + c // 2)
                if c >= 4:
                    silu_qk(c - 4)
            copy_nat(9)
            high_part(11)
            for c in range(4, 8):
                silu_qk(c)
            copy_nat(10)
            copy_nat(11)
            act.wait_ge(s_natd, n_out)

        @block.vector
        def _(dve):
            step = Chain(dve, dch)

            def modulation(piece, dst, s_done, n):
                _, s, q = piece
                slot = arrived(dve, piece)
                for c in range(2):
                    w, by = stage[:, slot, c * D:(c + 1) * D], cs[:, 2 * q + c:2 * q + c + 1]
                    if piece == ("ada", s, 0) and c == 0:
                        ins = nc.vector.tensor_scalar(dst, w, by, None, ALU.mult)
                    else:
                        ins = nc.vector.scalar_tensor_tensor(dst, w, by, dst, ALU.mult, ALU.add)
                    if c == 0:
                        step(ins)
                    else:
                        ins.then_inc(s_done, 1)
                dve.wait_ge(s_done, n + 1)

            dve.wait_ge(s_silu, 1)
            for n, piece in enumerate(ADA):
                modulation(piece, acc[:, piece[1], :], s_ada_used, n)
                if n == 3:
                    dve.wait_ge(s_cols, 1)
                    nc.vector.tensor_copy(cols[:, 0:44], ps[:, 6, 0:44]).then_inc(s_colsd, 1)
                    dve.wait_ge(s_ssq, NT)
                    nc.vector.tensor_scalar(ss[:, NT:2 * NT], ss[:, 0:NT], 1.0 / D, EPS, ALU.mult, ALU.add).then_inc(s_ms, 1)
                    dve.wait_ge(s_rt, 1)
                    nc.vector.reciprocal(rs[:, 0:NT], rs[:, NT:2 * NT]).then_inc(s_xn, 1)
            dve.wait_ge(s_mod, 1)
            step(nc.vector.tensor_tensor(modB[:, :], ps[:, 7, 0:KC], bcol[:, 0, :], ALU.add))
            step(nc.vector.scalar_tensor_tensor(modA[:, :], ps[:, 7, KC:2 * KC], 1.0, bcol[:, 1, :], ALU.add, ALU.add))
            nc.vector.tensor_tensor(modA[:, :], modA[:, :], gpre[:, :], ALU.mult).then_inc(s_modd, 1)
            for c in range(KC):
                dve.wait_ge(s_hf, c + 1)
                nc.vector.tensor_copy(hhi[:, c, :], hf[:, c, :]).then_inc(s_hhi, 1)
            for c in range(KC):
                dve.wait_ge(s_hhi, c + 1)
                nc.vector.tensor_tensor(hlo[:, c, :], hf[:, c, :], hhi[:, c, :].bitcast(F32), ALU.subtract).then_inc(s_hlo, 1)
            dve.wait_ge(s_bias, 48)
            for n, piece in enumerate(ROWS[0:5]):
                modulation(piece, rows[:, piece[1] - 2, :], s_row_used, n)
            dve.wait_ge(s_natd, IDX_DONE)
            ik = nat[:, :, IK0:IK0 + IDIM]
            mean = rs[:, 3 * NT:4 * NT]

            def wide(ap):
                return ap.rearrange("p (i o) -> p i o", o=1).broadcast_to([P, NT, IDIM])

            step(nc.vector.tensor_reduce(mean, ik, AX.X, ALU.add))
            step(nc.vector.tensor_scalar(mean, mean, 1.0 / IDIM, None, ALU.mult))
            step(nc.vector.tensor_tensor(lnb[:, :, :], ik, wide(mean), ALU.subtract))
            sq = work[:, 0:NT * IDIM].rearrange("p (i d) -> p i d", i=NT)
            step(nc.vector.tensor_tensor(sq, lnb[:, :, :], lnb[:, :, :], ALU.mult))
            step(nc.vector.tensor_reduce(ss[:, 3 * NT:4 * NT], sq, AX.X, ALU.add))
            nc.vector.tensor_scalar(ss[:, 2 * NT:3 * NT], ss[:, 3 * NT:4 * NT], 1.0 / IDIM, EPS, ALU.mult, ALU.add).then_inc(s_lnv, 1)
            dve.wait_ge(s_lnr, 1)
            step(nc.vector.reciprocal(rs[:, 2 * NT:3 * NT], rs[:, NT:2 * NT]))
            step(nc.vector.tensor_tensor(lnb[:, :, :], lnb[:, :, :], wide(rs[:, 2 * NT:3 * NT]), ALU.mult))
            gk = gik[:, :].rearrange("p (o d) -> p o d", o=1).broadcast_to([P, NT, IDIM])
            bk = bik[:, :].rearrange("p (o d) -> p o d", o=1).broadcast_to([P, NT, IDIM])
            step(nc.vector.tensor_tensor(lnb[:, :, :], lnb[:, :, :], gk, ALU.mult))
            nc.vector.tensor_tensor(ik, lnb[:, :, :], bk, ALU.add).then_inc(s_ln, 1)

            for n, piece in enumerate(ROWS[5:7]):
                modulation(piece, rows[:, piece[1] - 2, :], s_row_used, 5 + n)

            dve.wait_ge(s_iw, 1)
            for i in range(1, NT):
                w = P * (i + 1)
                sc = maskb[:, i, 0:w]
                for h in range(IH):
                    u = (i - 1) * IH + h
                    dve.wait_ge(s_relu, u + 1)
                    if h:
                        dve.wait_ge(s_sc, u)
                        nc.vector.scalar_tensor_tensor(sc, relu[:, u % 2, 0:w], iwS[:, i, h:h + 1], sc,
                                                       ALU.mult, ALU.add).then_inc(s_sc, 1)
                    else:
                        nc.vector.tensor_scalar(sc, relu[:, u % 2, 0:w], iwS[:, i, h:h + 1], None, ALU.mult).then_inc(s_sc, 1)
            def conv(c):
                dve.wait_ge(s_natd, QK_FIRST + c + 1)
                if c >= 2:
                    dve.wait_ge(s_qk, c - 1)
                o = tmp[:, c % 2, :]
                r = raw[:, c % 4, :]
                step(nc.vector.tensor_scalar(o, r[:, 0:SEQ], cols[:, c:c + 1], None, ALU.mult))
                for j in range(1, CONV):
                    w = cols[:, 8 * j + c:8 * j + c + 1]
                    ins = nc.vector.scalar_tensor_tensor(o, r[:, j:j + SEQ], w, o, ALU.mult, ALU.add)
                    if j < CONV - 1:
                        step(ins)
                    else:
                        ins.then_inc(s_conv, 1)

            conv_at = {(2, 12): 0, (3, 0): 1, (3, 3): 2, (3, 5): 3, (3, 8): 4, (3, 10): 5, (3, 13): 6, (3, 15): 7}
            dve.wait_ge(s_sc, (NT - 1) * IH)
            for i in range(1, NT):
                w = P * (i + 1)
                sc, wk = maskb[:, i, 0:w], work[:, 0:w]
                step(nc.vector.memset(sc[0:CHUNK, w - CHUNK:w], FMASK))
                for r in range(TOPK // 8):
                    if (i, r) in conv_at:
                        conv(conv_at[i, r])
                    src = sc if r == 0 else wk
                    step(nc.vector.max(top8[:, :], src))
                    step(nc.vector.match_replace(wk, top8[:, :], src, FMIN))
                step(nc.vector.tensor_tensor(wk, wk, sc, ALU.is_equal))
                step(nc.vector.tensor_scalar(sc, wk, NEG, None, ALU.mult))
            nc.vector.tensor_copy(maskb[:, 0, 0:P], k[:, K_CAUSAL:K_CAUSAL + P])
            for n, piece in enumerate(ROWS[7:16]):
                modulation(piece, rows[:, piece[1] - 2, :], s_row_used, 7 + n)


        @block.tensor
        def _(pe):
            pe.wait_ge(s_in, 16 * 8)
            nc.tensor.transpose(ps[:, 6, 0:44], colrows[:, :], ident[0:44, 0:44]).then_inc(s_cols, 1)
            pe.wait_ge(s_xn, NT + 1)
            pe.wait_ge(s_colsd, 1)
            for c in range(KC - 1):
                for i in range(NT):
                    ins = nc.tensor.transpose(ps[:, c, i * P:(i + 1) * P], xn[:, i, c:D:KC], ident)
                ins.then_inc(s_xT, 1)
            pe.wait_ge(s_ada_used, len(ADA))
            for s in range(2):
                for c in range(KC):
                    ins = nc.tensor.matmul(ps[:, 7, s * KC + c:s * KC + c + 1], acc[:, s, c:D:KC], k[:, K_ONES:K_ONES + 1],
                                           start=True, stop=True)
            ins.then_inc(s_mod, 1)
            pe.wait_ge(s_modd, 1)
            for i in range(NT):
                ins = nc.tensor.transpose(ps[:, KC - 1, i * P:(i + 1) * P], xn[:, i, KC - 1:D:KC], ident)
            ins.then_inc(s_xT, 1)
            PARTS = ((hhi, whi), (hlo, whi), (hhi, wlo))

            def project(m):
                kind, a, _ = ITEMS[m]
                w = width(ITEMS[m])
                pe.wait_ge(s_whi, m + 1)
                if m == 0:
                    for j, (hp, wp) in enumerate(PARTS):
                        wt = wp[:, 0, 0:KC * w].rearrange("p (c n) -> p c n", c=KC)
                        for i in range(NT):
                            for c in range(KC):
                                if i == 0:
                                    pe.wait_ge((s_hhi, s_hlo, s_wlo)[j], (c + 1, c + 1, 1)[j])
                                ins = nc.tensor.matmul(ps[:, i, 0:w], hp[:, c, i * P:(i + 1) * P], wt[:, c, :],
                                                       start=j == 0 and c == 0, stop=j == 2 and c == KC - 1)
                            if j == 2:
                                ins.then_inc(s_nat, 1)
                    return
                pe.wait_ge(s_wlo, m + 1)
                for i in range(NT if kind == "nat" else 2):
                    n = first[m] + i
                    if n >= 4:
                        pe.wait_ge(s_natd, n - 3)
                    for j, (hp, wp) in enumerate(PARTS):
                        wt = wp[:, m % 2, 0:KC * w].rearrange("p (c n) -> p c n", c=KC)
                        for c in range(KC):
                            lhsT = hp[:, c, i * P:(i + 1) * P] if kind == "nat" else wt[:, c, i * P:(i + 1) * P]
                            rhs = wt[:, c, :] if kind == "nat" else hp[:, c, :]
                            ins = nc.tensor.matmul(ps[:, n % 4, 0:w if kind == "nat" else SEQ], lhsT, rhs,
                                                   start=j == 0 and c == 0, stop=j == 2 and c == KC - 1)
                    ins.then_inc(s_nat, 1)

            pe.wait_ge(s_hf, KC)
            project(0)
            project(1)
            project(2)
            pe.wait_ge(s_rope, 1)
            for i in range(NT):
                if i >= 2:
                    pe.wait_ge(s_iTd, i - 1)
                for h in range(IH):
                    ins = nc.tensor.transpose(ps[0:IDIM, 4 + i % 2, h * P:(h + 1) * P],
                                              nat[:, i, IQ0 + h * IDIM:IQ0 + (h + 1) * IDIM], ident)
                ins.then_inc(s_iT, 1)
            for i in range(NT):
                ins = nc.tensor.transpose(ps[0:IDIM, 6, i * P:(i + 1) * P], nat[:, i, IK0:IK0 + IDIM], ident)
            ins.then_inc(s_iT, 1)
            pe.wait_ge(s_iTd, NT + 1)
            for i in range(1, NT):
                for h in range(IH):
                    u = (i - 1) * IH + h
                    if u >= 4:
                        pe.wait_ge(s_relu, u - 3)
                    nc.tensor.matmul(ps[:, 4 + u % 4, 0:P * (i + 1)], iqT[:, h, i * P:(i + 1) * P], ikT[:, 0:P * (i + 1)],
                                     start=True, stop=True).then_inc(s_rel, 1)
            for m in range(3, len(ITEMS)):
                project(m)


def stage_attention(nc, A, G):
    with ExitStack() as own:
        def sb(name, shape, dt=F32):
            return own.enter_context(nc.sbuf_tensor(name, shape, dt))

        G.used = []

        def sem(name):
            G.used.append(own.enter_context(nc.semaphore(name)))
            return G.used[-1]

        k, nat, qkc, rows, maskb, cols, ps = G.k, G.nat, G.qkc, G.rows, G.maskb, G.cols, G.ps
        catT, wout, arena = G.catT, G.wout, G.arena
        ident = k[:, K_ID:K_ID + P]
        TRI = [0, 512, 896, 1152]
        TRI_W = 1280
        stT = arena[:, 0:2 * TRI_W].rearrange("p (b n) -> p b n", b=2)
        dm = arena[:, 2 * TRI_W:4 * TRI_W].rearrange("p (b n) -> p b n", b=2)
        md = arena[:, 4 * TRI_W:4 * TRI_W + 8 * P].rearrange("p (b n) -> p b n", b=8)
        aqT = arena[:, 0:2048].rearrange("p (h t) -> p h t", h=HEADS)
        akT = arena[:, 2048:2560]
        lg = arena[:, 2560:3584].rearrange("p (b n) -> p b n", b=2)
        pr = arena[:, 3584:5120].rearrange("p (b n) -> p b n", b=3)
        prT = arena[:, 5120:6144].rearrange("p (b n) -> p b n", b=2)
        vext = sb("vext", [P, NT, HEADS, DH + 1])
        hall = sb("hall", [P, NT, HEADS * DH])
        gains = G.xt[:, 0:3, :]
        gb = G.gb
        ga = sb("gate_a", [HEADS, SEQ])
        gf = sb("gate_f", [HEADS, SEQ])
        gt = sb("gate_t", [HEADS, SEQ])
        aN = sb("gates_nat", [P, 2, NT, HEADS])
        den = sb("den", [P, NT])
        var = sb("var", [P, HEADS, NT])
        rstd = sb("rstd", [P, HEADS, NT])
        mx = sb("mx", [P, 2])
        nm = sb("nm", [P, 2])
        rsum = sb("rsum", [P, 2])
        rinv = sb("rinv", [P, 2])
        sqb = sb("sqb", [P, NT, DH])

        s_in = sem("att_small_in")
        dch, ach, pch = sem("dve_chain"), sem("act_chain"), sem("pool_chain")
        s_gT = sem("gates_transposed")
        s_row = sem("row_broadcast")
        s_rowd = sem("row_ready")
        s_absf = sem("gate_abs")
        s_lse = sem("gate_log")
        s_em = sem("gate_m")
        s_emd = sem("gate_exp_m")
        s_an = sem("gates_back")
        s_and = sem("gates_nat_ready")
        s_bc = sem("negM_broadcast")
        s_md = sem("diag_masked")
        s_dm = sem("decay_ready")
        s_sT = sem("scores_T")
        s_sTd = sem("scores_T_weighted")
        s_num = sem("numerator")
        s_numd = sem("numerator_read")
        s_sig = sem("out_gate")
        s_vext = sem("v_extended")
        s_hsq = sem("head_var")
        s_hrt = sem("head_root")
        s_hr = sem("head_rstd")
        s_hn = sem("head_normed")
        s_hT = sem("head_transposed")
        s_hTd = sem("head_T_copied")
        s_qT = sem("aq_transposed")
        s_qTd = sem("aq_T_copied")
        s_lg = sem("logits")
        s_lgd = sem("logits_masked")
        s_nm = sem("neg_max")
        s_ex = sem("exps")
        s_ri = sem("sum_inverse")
        s_pn = sem("probs_normed")
        s_pT = sem("probs_transposed")
        s_pTd = sem("probs_T_copied")
        s_o = sem("attended")
        s_od = sem("attended_copied")
        UNITS = [(h, i) for h in range(HEADS) for i in range(NT)]
        SCALE = DH ** -0.5
        ROW_BANK = [5, 0, 1, 2, 3, 4, 5, 0]
        block = own.enter_context(nc.Block())

        @block.sync
        def _(sp):
            for n, name in enumerate(("g_mix_post", "g_ffn_pre", "g_ffn_post")):
                sp.dma_start(gains[:, n, :], A[name].broadcast_to([P, D])).then_inc(s_in, 16)
            sp.dma_start(wout[:, :, :], A["w_out"][0].rearrange("(f p) n -> p f n", p=P)).then_inc(G.s_wout, 16)

        @block.gpsimd
        def _(pool):
            nc.gpsimd.memset(vext[:, :, :, DH:DH + 1], 1.0)
            nc.gpsimd.tensor_copy(vext[:, :, :, 0:DH], nat[:, :, V0:V0 + 512].rearrange("p i (h d) -> p i h d", h=HEADS)).then_inc(s_vext, 1)
            for u, (h, i) in enumerate(UNITS):
                pool.wait_ge(s_ri, u + 1)
                w = P * (i + 1)
                nc.gpsimd.tensor_scalar(pr[:, u % 3, 0:w], pr[:, u % 3, 0:w], rinv[:, u % 2:u % 2 + 1], None,
                                        ALU.mult).then_inc(s_pn, 1)

        @block.scalar
        def _(act):
            step = Chain(act, ach)
            act.wait_ge(s_absf, 1)
            step(nc.scalar.activation(gt[:, :], gt[:, :], ACT.Exp, scale=-1.0))
            nc.scalar.activation(gt[:, :], gt[:, :], ACT.Ln, bias=1.0).then_inc(s_lse, 1)
            act.wait_ge(s_em, 1)
            nc.scalar.activation(gt[:, :], gt[:, :], ACT.Exp, scale=-1.0).then_inc(s_emd, 1)
            act.wait_ge(s_and, 1)
            for h in range(HEADS):
                if h >= 2:
                    act.wait_ge(s_sTd, NT * (h - 1))
                act.wait_ge(s_md, NT * (h + 1))
                for j in range(NT):
                    w = SEQ - P * j
                    bias = aN[:, 0, j, h:h + 1]
                    ins = nc.scalar.activation(dm[:, h % 2, TRI[j]:TRI[j] + P], md[:, NT * (h % 2) + j, :], ACT.Exp, bias=bias)
                    if w > P:
                        ins = nc.scalar.activation(dm[:, h % 2, TRI[j] + P:TRI[j] + w], ps[:, h % 2, P * (j + 1):SEQ],
                                                   ACT.Exp, bias=bias)
                    ins.then_inc(s_dm, 1)
            nc.scalar.activation(nat[:, :, O0:O0 + 512], nat[:, :, O0:O0 + 512], ACT.Sigmoid).then_inc(s_sig, 1)
            act.wait_ge(s_hsq, 1)
            nc.scalar.activation(rstd[:, :, :], var[:, :, :], ACT.Sqrt).then_inc(s_hrt, 1)
            act.wait_ge(s_num, HEADS)
            for h in range(HEADS + 1):
                act.wait_ge(s_qT, h + 1)
                dst = aqT[:, h, :] if h < HEADS else akT
                nc.scalar.activation(dst, ps[:, h, :], ACT.Copy).then_inc(s_qTd, 1)

            def exp_unit(u):
                w = P * (UNITS[u][1] + 1)
                act.wait_ge(s_nm, u + 1)
                if u >= 3:
                    act.wait_ge(s_pT, u - 2)
                nc.scalar.activation(pr[:, u % 3, 0:w], lg[:, u % 2, 0:w], ACT.Exp, bias=nm[:, u % 2:u % 2 + 1], scale=SCALE,
                                     accum_out=rsum[:, u % 2:u % 2 + 1]).then_inc(s_ex, 1)

            def copy_pT(u):
                w = P * (UNITS[u][1] + 1)
                act.wait_ge(s_pT, u + 1)
                if u >= 2:
                    act.wait_ge(s_o, u - 1)
                nc.scalar.activation(prT[:, u % 2, 0:w], ps[:, 3 + u % 3, 0:w], ACT.Copy).then_inc(s_pTd, 1)

            for u in range(len(UNITS)):
                exp_unit(u)
                if u:
                    copy_pT(u - 1)
            copy_pT(len(UNITS) - 1)

        @block.vector
        def _(dve):
            step = Chain(dve, dch)
            dve.wait_ge(s_gT, 2)
            step(nc.vector.tensor_scalar(gf[:, :], ps[0:HEADS, 1, :], gb[:, 1:2], None, ALU.add))
            step(nc.vector.tensor_scalar(gt[:, :], gf[:, :], -1.0, None, ALU.mult))
            nc.vector.tensor_tensor(gt[:, :], gf[:, :], gt[:, :], ALU.max).then_inc(s_absf, 1)
            step(nc.vector.tensor_scalar(gf[:, :], gf[:, :], 0.0, None, ALU.min))
            step(nc.vector.tensor_scalar(ga[:, :], ps[0:HEADS, 0, :], gb[:, 0:1], None, ALU.add))
            dve.wait_ge(s_lse, 1)
            step(nc.vector.tensor_tensor(gf[:, :], gf[:, :], gt[:, :], ALU.subtract))
            one = k[0:HEADS, K_ONES:K_ONES + 1].broadcast_to([HEADS, SEQ])
            step(nc.vector.tensor_tensor_scan(gt[:, :], one, gf[:, :], 0.0, ALU.mult, ALU.add))
            step(nc.vector.tensor_tensor(ga[:, :], ga[:, :], gt[:, :], ALU.subtract))
            step(nc.vector.tensor_tensor_scan(gf[:, :], one, ga[:, :], NEG, ALU.mult, ALU.max))
            nc.vector.tensor_tensor(gt[:, :], gt[:, :], gf[:, :], ALU.add).then_inc(s_em, 1)
            step(nc.vector.tensor_scalar(gf[:, :], gf[:, :], -1.0, None, ALU.mult))
            dve.wait_ge(s_an, 1)
            nc.vector.tensor_copy(aN[:, :, :, :], ps[:, 0, 0:2 * NT * HEADS].rearrange("p (a i h) -> p a i h", a=2, i=NT)).then_inc(s_and, 1)

            def diagonals(h):
                dve.wait_ge(s_bc, h + 1)
                if h >= 2:
                    dve.wait_ge(s_dm, NT * (h - 1))
                for j in range(NT):
                    nc.vector.tensor_tensor(md[:, NT * (h % 2) + j, :], ps[:, h % 2, j * P:(j + 1) * P],
                                            k[:, K_TRI:K_TRI + P], ALU.add).then_inc(s_md, 1)

            def weigh(h):
                for j in range(NT):
                    u, w = NT * h + j, SEQ - P * j
                    dve.wait_ge(s_sT, u + 1)
                    dve.wait_ge(s_dm, u + 1)
                    if h >= 2:
                        dve.wait_ge(s_num, h - 1)
                    nc.vector.scalar_tensor_tensor(stT[:, h % 2, TRI[j]:TRI[j] + w], ps[:, 2 + u % 2, 0:w], SCALE,
                                                   dm[:, h % 2, TRI[j]:TRI[j] + w], ALU.mult, ALU.mult).then_inc(s_sTd, 1)

            def read_head(h):
                dve.wait_ge(s_num, h + 1)
                b = 4 + 2 * (h % 2)
                v = ps[:, b:b + 2, :].rearrange("p b (t n) -> p (b t) n", n=256)
                hv = hall[:, :, h * DH:(h + 1) * DH]
                dv = den[:, :].rearrange("p (i o) -> p i o", o=1)
                step(nc.vector.scalar_tensor_tensor(dv, v[:, :, DH:DH + 1], -1.0, aN[:, 1, :, h:h + 1], ALU.mult, ALU.max))
                step(nc.vector.tensor_tensor(dv, dv, v[:, :, DH:DH + 1], ALU.max))
                step(nc.vector.reciprocal(den[:, :], den[:, :]))
                nc.vector.tensor_tensor(hv, v[:, :, 0:DH], den[:, :].rearrange("p (i o) -> p i o", o=1).broadcast_to([P, NT, DH]),
                                        ALU.mult).then_inc(s_numd, 1)
                dve.wait_ge(s_numd, h + 1)
                step(nc.vector.tensor_tensor(sqb[:, :, :], hv, hv, ALU.mult))
                step(nc.vector.tensor_reduce(var[:, h, :], sqb[:, :, :], AX.X, ALU.add))

            diagonals(0)
            for h in range(HEADS):
                if h + 1 < HEADS:
                    diagonals(h + 1)
                weigh(h)
                if h:
                    read_head(h - 1)
            read_head(HEADS - 1)
            nc.vector.tensor_scalar(var[:, :, :], var[:, :, :], 1.0 / DH, EPS, ALU.mult, ALU.add).then_inc(s_hsq, 1)
            dve.wait_ge(s_hrt, 1)
            nc.vector.reciprocal(rstd[:, :, :], rstd[:, :, :]).then_inc(s_hr, 1)
            dve.wait_ge(s_hr, 1)
            dve.wait_ge(s_sig, 1)
            for h in range(HEADS):
                for i in range(NT):
                    c = slice(h * DH, (h + 1) * DH)
                    ins = nc.vector.scalar_tensor_tensor(hall[:, i, c], hall[:, i, c], rstd[:, h, i:i + 1],
                                                         nat[:, i, O0 + h * DH:O0 + (h + 1) * DH], ALU.mult, ALU.mult)
                ins.then_inc(s_hn, 1)
            dve.wait_ge(s_in, 16 * 3)
            for r in range(8):
                s, c = r // 2, slice(512 * (r % 2), 512 * (r % 2 + 1))
                dve.wait_ge(s_row, r + 1)
                src, dst = ps[:, ROW_BANK[r], :], rows[:, s, c]
                if s == 1:
                    ins = nc.vector.tensor_copy(dst, src)
                elif s == 2:
                    ins = nc.vector.scalar_tensor_tensor(dst, src, 1.0, gains[:, 1, c], ALU.add, ALU.mult)
                else:
                    ins = nc.vector.tensor_tensor(dst, src, gains[:, 0 if s == 0 else 2, c], ALU.mult)
                ins.then_inc(s_rowd, 1)

            def mask_unit(u):
                h, i = UNITS[u]
                w = P * (i + 1)
                dve.wait_ge(s_lg, u + 1)
                if u >= 2:
                    dve.wait_ge(s_ex, u - 1)
                nc.vector.tensor_tensor_reduce(out=lg[:, u % 2, 0:w], in0=ps[:, u % 3, 0:w], in1=maskb[:, i, 0:w], scale=1.0,
                                               scalar=FMIN, op0=ALU.add, op1=ALU.max,
                                               accum_out=mx[:, u % 2:u % 2 + 1]).then_inc(s_lgd, 1)
                dve.wait_ge(s_lgd, u + 1)
                nc.vector.tensor_scalar(nm[:, u % 2:u % 2 + 1], mx[:, u % 2:u % 2 + 1], -SCALE, None, ALU.mult).then_inc(s_nm, 1)

            def invert(u):
                dve.wait_ge(s_ex, u + 1)
                if u >= 2:
                    dve.wait_ge(s_pn, u - 1)
                nc.vector.reciprocal(rinv[:, u % 2:u % 2 + 1], rsum[:, u % 2:u % 2 + 1]).then_inc(s_ri, 1)

            def copy_out(h):
                dve.wait_ge(s_o, NT * (h + 1))
                nc.vector.tensor_copy(catT[:, HEADS + h, :], ps[:, 6 + h % 2, :]).then_inc(s_od, 1)

            def copy_head(h):
                dve.wait_ge(s_hT, h + 1)
                nc.vector.tensor_scalar(catT[:, h, :], ps[:, 6 + h % 2, :], cols[:, 40 + h:41 + h], None, ALU.mult).then_inc(s_hTd, 1)

            for h in range(HEADS):
                copy_head(h)
            for u in range(len(UNITS)):
                mask_unit(u)
                if u:
                    invert(u - 1)
                if u >= NT + 2 and (u - 2) % NT == 0:
                    copy_out((u - 2) // NT - 1)
            invert(len(UNITS) - 1)
            copy_out(HEADS - 1)

        @block.tensor
        def _(pe):
            for b, at in ((0, I0), (1, F0)):
                for i in range(NT):
                    ins = nc.tensor.transpose(ps[0:HEADS, b, i * P:(i + 1) * P], nat[:, i, at:at + HEADS], ident)
                ins.then_inc(s_gT, 1)
            pe.wait_ge(s_emd, 1)
            for a, src in enumerate((ga, gt)):
                for i in range(NT):
                    at = (a * NT + i) * HEADS
                    ins = nc.tensor.transpose(ps[:, 0, at:at + HEADS], src[:, i * P:(i + 1) * P], ident[0:HEADS, 0:HEADS])
            ins.then_inc(s_an, 1)
            pe.wait_ge(s_and, 1)

            def broadcast(h):
                if h >= 2:
                    pe.wait_ge(s_dm, NT * (h - 1))
                nc.tensor.matmul(ps[:, h % 2, :], k[0:HEADS, K_SEL + h * P:K_SEL + (h + 1) * P], gf[:, :],
                                 start=True, stop=True).then_inc(s_bc, 1)

            def scores(h):
                for j in range(NT):
                    u = NT * h + j
                    if u >= 2:
                        pe.wait_ge(s_sTd, u - 1)
                    nc.tensor.matmul(ps[:, 2 + u % 2, 0:SEQ - P * j], qkc[:, HEADS + h, j * P:(j + 1) * P], qkc[:, h, j * P:SEQ],
                                     start=True, stop=True).then_inc(s_sT, 1)

            def numerators(h):
                if h == 0:
                    pe.wait_ge(s_vext, 1)
                if h >= 2:
                    pe.wait_ge(s_numd, h - 1)
                pe.wait_ge(s_sTd, NT * (h + 1))
                for i in range(NT):
                    for j in range(i + 1):
                        ins = nc.tensor.matmul(ps[:, 4 + 2 * (h % 2) + i // 2, 256 * (i % 2):256 * (i % 2) + DH + 1],
                                               stT[:, h % 2, TRI[j] + P * (i - j):TRI[j] + P * (i - j + 1)], vext[:, j, h, :],
                                               start=j == 0, stop=j == i)
                ins.then_inc(s_num, 1)

            broadcast(0)
            for h in range(HEADS):
                if h + 1 < HEADS:
                    broadcast(h + 1)
                scores(h)
                if h:
                    numerators(h - 1)
            numerators(HEADS - 1)
            pe.wait_ge(G.s_roped, 1)
            pe.wait_ge(s_dm, NT * HEADS)
            pe.wait_ge(s_sTd, NT * HEADS)
            pe.wait_ge(s_numd, HEADS)
            for h in range(HEADS + 1):
                for i in range(NT):
                    at = AQ0 + h * DH
                    ins = nc.tensor.transpose(ps[:, h, i * P:(i + 1) * P], nat[:, i, at:at + DH], ident)
                ins.then_inc(s_qT, 1)
            for r in range(8):
                if ROW_BANK[r] < 5:
                    pe.wait_ge(s_qTd, ROW_BANK[r] + 1)
                if r >= 6:
                    pe.wait_ge(s_rowd, r - 5)
                nc.tensor.matmul(ps[:, ROW_BANK[r], :], k[:, K_ONES:K_ONES + P], rows[:, r // 2, 512 * (r % 2):512 * (r % 2 + 1)],
                                 start=True, stop=True).then_inc(s_row, 1)
            for h in range(HEADS):
                pe.wait_ge(s_hn, h + 1)
                if h >= 2:
                    pe.wait_ge(s_hTd, h - 1)
                for i in range(NT):
                    ins = nc.tensor.transpose(ps[:, 6 + h % 2, i * P:(i + 1) * P], hall[:, i, h * DH:(h + 1) * DH], ident)
                ins.then_inc(s_hT, 1)
            pe.wait_ge(s_qTd, HEADS + 1)
            pe.wait_ge(s_rowd, 8)
            pe.wait_ge(s_hTd, HEADS)

            def logits(u):
                h, i = UNITS[u]
                if u >= 3:
                    pe.wait_ge(s_lgd, u - 2)
                nc.tensor.matmul(ps[:, u % 3, 0:P * (i + 1)], aqT[:, h, i * P:(i + 1) * P], akT[:, 0:P * (i + 1)],
                                 start=True, stop=True).then_inc(s_lg, 1)

            def turn(u):
                h, i = UNITS[u]
                pe.wait_ge(s_pn, u + 1)
                if u >= 3:
                    pe.wait_ge(s_pTd, u - 2)
                for j in range(i + 1):
                    ins = nc.tensor.transpose(ps[:, 3 + u % 3, j * P:(j + 1) * P], pr[:, u % 3, j * P:(j + 1) * P], ident)
                ins.then_inc(s_pT, 1)

            def attend(u):
                h, i = UNITS[u]
                pe.wait_ge(s_pTd, u + 1)
                if h >= 2 and i == 0:
                    pe.wait_ge(s_od, h - 1)
                for j in range(i + 1):
                    ins = nc.tensor.matmul(ps[:, 6 + h % 2, i * P:(i + 1) * P], nat[:, j, AV0:AV0 + DH],
                                           prT[:, u % 2, j * P:(j + 1) * P], start=j == 0, stop=j == i)
                ins.then_inc(s_o, 1)

            logits(0)
            logits(1)
            for u in range(len(UNITS)):
                if u + 2 < len(UNITS):
                    logits(u + 2)
                turn(u)
                if u:
                    attend(u - 1)
            attend(len(UNITS) - 1)


def stage_route(nc, A, G):
    with ExitStack() as own:
        def sb(name, shape, dt=F32):
            return own.enter_context(nc.sbuf_tensor(name, shape, dt))

        G.used = []

        def sem(name):
            G.used.append(own.enter_context(nc.semaphore(name)))
            return G.used[-1]

        k, rows, xt, ps, catT, wout = G.k, G.rows, G.xt, G.ps, G.catT, G.wout
        posm, gt = G.posm, G.gt
        ident = k[:, K_ID:K_ID + P]
        ones = k[:, K_ONES:K_ONES + P]
        flat = G.nat[:, :, :].rearrange("p i n -> p (i n)")
        h2n = flat[:, 0:NT * D].rearrange("p (i d) -> p i d", i=NT)
        wg = flat[:, 4096:4096 + KC * DE].rearrange("p (c f) -> p c f", c=KC)
        wu = flat[:, 6144:6144 + KC * DE].rearrange("p (c f) -> p c f", c=KC)
        h2T = G.qkc
        wd = G.arena[:, 0:FC * D].rearrange("p (f n) -> p f n", f=FC)
        wr = G.arena[:, 2048:2048 + KC * E_N].rearrange("p (c e) -> p c e", c=KC)
        sg = G.arena[:, 2560:3584].rearrange("p (f t) -> p f t", f=FC)
        uT = G.arena[:, 3584:4608].rearrange("p (f t) -> p f t", f=FC)
        tmp = G.arena[:, 4608:5632]
        ysh = sb("shared_out", [P, 2, D])
        br = sb("b_router", [P, E_N])
        ssq = sb("ssq", [P, NT, 4])
        ms = sb("ms", [P, NT, 2])
        rt = sb("rt", [P, NT, 2])
        sco = sb("scores", [P, NT, E_N])
        sel = sb("sel", [P, NT, E_N])
        top2 = sb("top2", [P, NT * E_GROUPS, 8])
        gs = sb("group_score", [P, NT, E_GROUPS])
        cmp1 = sb("cmp1", [P, NT, E_GROUPS, E_GROUPS])
        cmp2 = sb("cmp2", [P, NT, E_GROUPS, E_GROUPS])
        gm = sb("group_mask", [P, NT, E_GROUPS])
        t8 = sb("top8e", [P, NT, 8])
        em = sb("expert_mask", [P, NT, E_N])
        wk = sb("sel_left", [P, NT, E_N])
        gsum = sb("gate_sum", [P, NT])
        cnt = sb("counts", [P, 4, E_N])
        tab = sb("tab", [P, 4])
        diag = sb("diag", [P, 2, P])

        s_in = sem("route_in")
        s_wsh = sem("shared_weights")
        s_xin = sem("x_again")
        dch, ach = sem("dve_chain"), sem("act_chain")
        s_y = sem("y_projected")
        s_sq = sem("squares")
        s_ms = sem("mean_squares")
        s_rt = sem("roots")
        s_yr = sem("y_read")
        s_x2 = sem("x2_ready")
        s_h2 = sem("h2_ready")
        s_h2T = sem("h2_transposed")
        s_h2Td = sem("h2_T_copied")
        s_lg = sem("router_logits")
        s_sco = sem("scores_ready")
        s_gu = sem("shared_gate_up")
        s_sg = sem("shared_silu")
        s_u = sem("shared_u")
        s_dn = sem("shared_down")
        s_dnd = sem("shared_copied")
        s_em = sem("expert_mask_ready")
        s_pos = sem("positions")
        s_dg = sem("diagonals_ready")
        s_tab = sem("table_rows")
        s_hw = sem("h2_stored")
        s_yw = [sem(f"shared_stored{i}") for i in range(2)]
        s_init = sem("tables_cleared")
        s_tabd = sem("tables_ready")
        block = own.enter_context(nc.Block())

        @block.sync
        def _(sp):
            sp.dma_start(xt[:, :, :], A["x"][0].rearrange("(i p) d -> p i d", p=P)).then_inc(s_xin, 16)
            sp.dma_start(br[:, :], A["b_router"].broadcast_to([P, E_N])).then_inc(s_in, 16)
            sp.dma_start(wr, A["w_router"][0].rearrange("(p c) e -> p c e", c=KC)).then_inc(s_in, 16)
            sp.dma_start(wg, A["w_sh_gate"][0].rearrange("(p c) f -> p c f", c=KC)).then_inc(s_wsh, 16)
            sp.dma_start(wu, A["w_sh_up"][0].rearrange("(p c) f -> p c f", c=KC)).then_inc(s_wsh, 16)
            sp.dma_start(wd, A["w_sh_down"][0].rearrange("(f p) n -> p f n", p=P)).then_inc(s_wsh, 16)
            sp.wait_ge(s_y, NT)
            for e in range(2):
                for m, name in enumerate(("w_exp_gate", "w_exp_up")):
                    sp.dma_start(G.w_gate_up[e][:, m], A[name][0, e].rearrange("(p c) f -> p c f", c=KC)).then_inc(G.s_wgu[e], 16)
                sp.dma_start(G.w_down[e], A["w_exp_down"][0, e].rearrange("(f p) n -> p f n", p=P)).then_inc(G.s_wd[e], 16)
            for i in range(NT):
                sp.wait_ge(s_h2, i + 1)
                sp.dma_start(G.h2_rows[i * P:(i + 1) * P, :], h2n[:, i, :]).then_inc(s_hw, 16)
            for i in range(NT):
                sp.wait_ge(s_dnd, i + 1)
                sp.dma_start(G.y_rows[i * P:(i + 1) * P, :], ysh[:, i % 2, :]).then_inc(s_yw[i % 2], 16)
            sp.wait_ge(s_hw, 16 * NT)
            sp.wait_ge(s_yw[0], 16 * (NT // 2))
            sp.wait_ge(s_yw[1], 16 * (NT // 2))

        @block.gpsimd
        def _(pool):
            nc.gpsimd.memset(posm[:, :], -1.0).then_inc(s_init, 1)
            nc.gpsimd.memset(gt[:, :, :, :], 0.0).then_inc(s_init, 1)

        @block.scalar
        def _(act):
            def squares(i, n):
                if n == 0:
                    act.wait_ge(s_y, i + 1)
                    if i:
                        act.wait_ge(s_h2, i)
                    src = ps[:, 2 * i:2 * i + 2, :]
                else:
                    act.wait_ge(s_x2, i + 1)
                    src = xt[:, i, :].rearrange("p (a b) -> p a b", a=2)
                nc.scalar.activation(tmp.rearrange("p (a b) -> p a b", a=2), src, ACT.Square,
                                     accum_out=ssq[:, i, n:n + 1]).then_inc(s_sq, 1)
                act.wait_ge(s_ms, 2 * i + n + 1)
                nc.scalar.activation(rt[:, i, n:n + 1], ms[:, i, n:n + 1], ACT.Sqrt).then_inc(s_rt, 1)

            def copy_h2T(i):
                act.wait_ge(s_h2T, 2 * i + 2)
                nc.scalar.activation(h2T[:, 4:8, i * P:(i + 1) * P], ps[:, 2 * i + 1, :].rearrange("p (c t) -> p c t", c=4),
                                     ACT.Copy).then_inc(s_h2Td, 1)

            for i in range(NT):
                squares(i, 0)
                if i:
                    copy_h2T(i - 1)
                squares(i, 1)
            copy_h2T(NT - 1)
            act.wait_ge(s_lg, 1)
            nc.scalar.activation(sco[:, :, :], ps[:, 4, 0:NT * E_N].rearrange("p (i e) -> p i e", i=NT), ACT.Sigmoid).then_inc(s_sco, 1)
            for f in range(FC):
                act.wait_ge(s_gu, f + 1)
                nc.scalar.activation(sg[:, f, :], ps[:, f, :], ACT.Silu).then_inc(s_sg, 1)
            for i in range(NT):
                act.wait_ge(s_dn, i + 1)
                if i >= 2:
                    act.wait_ge(s_yw[i % 2], 16 * (i // 2))
                nc.scalar.activation(ysh[:, i % 2, :], ps[:, 4 * (i % 2):4 * (i % 2) + 2, :].rearrange("p a b -> p (a b)"),
                                     ACT.Copy).then_inc(s_dnd, 1)

        @block.vector
        def _(dve):
            step = Chain(dve, dch)

            def root(i, n):
                dve.wait_ge(s_sq, 2 * i + n + 1)
                nc.vector.tensor_scalar(ms[:, i, n:n + 1], ssq[:, i, n:n + 1], 1.0 / D, EPS, ALU.mult, ALU.add).then_inc(s_ms, 1)
                dve.wait_ge(s_rt, 2 * i + n + 1)
                step(nc.vector.reciprocal(rt[:, i, n:n + 1], rt[:, i, n:n + 1]))

            dve.wait_ge(s_xin, 16)
            def copy_h2T(i):
                dve.wait_ge(s_h2T, 2 * i + 1)
                nc.vector.tensor_copy(h2T[:, 0:4, i * P:(i + 1) * P], ps[:, 2 * i, :].rearrange("p (c t) -> p c t", c=4)).then_inc(s_h2Td, 1)

            for i in range(NT):
                root(i, 0)
                nc.vector.scalar_tensor_tensor(tmp, ps[:, 2 * i:2 * i + 2, :].rearrange("p a b -> p (a b)"), rt[:, i, 0:1],
                                               rows[:, 0, :], ALU.mult, ALU.mult).then_inc(s_yr, 1)
                if i:
                    copy_h2T(i - 1)
                dve.wait_ge(s_yr, i + 1)
                nc.vector.tensor_tensor(xt[:, i, :], xt[:, i, :], tmp, ALU.add).then_inc(s_x2, 1)
                root(i, 1)
                step(nc.vector.scalar_tensor_tensor(h2n[:, i, :], xt[:, i, :], rt[:, i, 1:2], rows[:, 2, :], ALU.mult, ALU.mult))
                nc.vector.tensor_tensor(h2n[:, i, :], h2n[:, i, :], rows[:, 1, :], ALU.add).then_inc(s_h2, 1)
            copy_h2T(NT - 1)

            def bc(ap, shape):
                return ap.broadcast_to(shape)

            dve.wait_ge(s_in, 32)
            dve.wait_ge(s_sco, 1)
            step(nc.vector.tensor_tensor(sel[:, :, :], sco[:, :, :],
                                         bc(br[:, :].rearrange("p (o e) -> p o e", o=1), [P, NT, E_N]), ALU.add))
            for n in range(NT * E_GROUPS):
                i, g = n // E_GROUPS, n % E_GROUPS
                ins = nc.vector.max(top2[:, n, :], sel[:, i, g * E_PER:(g + 1) * E_PER])
            step(ins)
            step(nc.vector.tensor_tensor(gs[:, :, :].rearrange("p i g -> p (i g)").rearrange("p (n o) -> p n o", o=1),
                                         top2[:, :, 0:1], top2[:, :, 1:2], ALU.add))
            full = [P, NT, E_GROUPS, E_GROUPS]
            mine = bc(gs[:, :, :].rearrange("p i (g o) -> p i g o", o=1), full)
            other = bc(gs[:, :, :].rearrange("p i (o g) -> p i o g", o=1), full)
            nc.vector.tensor_tensor(cmp1[:, :, :, :], other, mine, ALU.is_gt)
            step(nc.vector.tensor_tensor(cmp2[:, :, :, :], other, mine, ALU.is_equal))
            for g in range(E_GROUPS):
                step(nc.vector.memset(cmp2[:, :, g, g:E_GROUPS], 0.0))
            step(nc.vector.tensor_tensor(cmp1[:, :, :, :], cmp1[:, :, :, :], cmp2[:, :, :, :], ALU.add))
            step(nc.vector.tensor_reduce(gm[:, :, :], cmp1[:, :, :, :], AX.X, ALU.add))
            step(nc.vector.tensor_scalar(gm[:, :, :], gm[:, :, :], float(E_TOPG), FMASK, ALU.is_ge, ALU.mult))
            step(nc.vector.tensor_tensor(
                sel[:, :, :].rearrange("p i (g m) -> p i g m", g=E_GROUPS), sel[:, :, :].rearrange("p i (g m) -> p i g m", g=E_GROUPS),
                bc(gm[:, :, :].rearrange("p i (g o) -> p i g o", o=1), [P, NT, E_GROUPS, E_PER]), ALU.add))
            for i in range(NT):
                ins = nc.vector.max(t8[:, i, :], sel[:, i, :])
            step(ins)
            for i in range(NT):
                ins = nc.vector.match_replace(wk[:, i, :], t8[:, i, :], sel[:, i, :], FMIN)
            step(ins)
            nc.vector.tensor_tensor(em[:, :, :], wk[:, :, :], sel[:, :, :], ALU.not_equal).then_inc(s_em, 1)
            dve.wait_ge(s_em, 1)
            for f in range(FC):
                dve.wait_ge(s_sg, f + 1)
                nc.vector.tensor_tensor(uT[:, f, :], sg[:, f, :], ps[:, 2 + f, :], ALU.mult).then_inc(s_u, 1)
            step(nc.vector.tensor_tensor(wk[:, :, :], sco[:, :, :], em[:, :, :], ALU.mult))
            step(nc.vector.tensor_reduce(gsum[:, :], wk[:, :, :], AX.X, ALU.add))
            step(nc.vector.reciprocal(gsum[:, :], gsum[:, :]))
            dve.wait_ge(s_init, 2)
            gv = gt[:, 0:E_N, :, :].rearrange("p e i t -> p i e t")
            for i in range(NT):
                ins = nc.vector.tensor_scalar(wk[:, i, :], wk[:, i, :], gsum[:, i:i + 1], ROUTE_SCALE, ALU.mult, ALU.mult)
            step(ins)
            for n, at in enumerate((K_TOKH, K_TOKL)):
                for i in range(NT):
                    nc.vector.tensor_copy(gv[:, i, :, n], bc(k[:, at + i:at + i + 1], [P, E_N]))
            for n in range(3):
                step(nc.vector.tensor_copy(gv[:, :, :, 3 + n], wk[:, :, :]))
                if n < 2:
                    step(nc.vector.tensor_tensor(wk[:, :, :], wk[:, :, :], gv[:, :, :, 3 + n], ALU.subtract))
            dve.wait_ge(s_pos, 1)
            pp = ps[:, 7, 0:NT * E_N].rearrange("p (i e) -> p i e", i=NT)
            step(nc.vector.scalar_tensor_tensor(wk[:, :, :], pp, 1.0, em[:, :, :], ALU.add, ALU.mult))
            nc.vector.tensor_scalar(posm[:, 0:E_N * NT].rearrange("p (e i) -> p i e", i=NT), wk[:, :, :], -1.0, None, ALU.add)
            n_e, k_e, cum, at = (cnt[:, n, :] for n in range(4))
            step(nc.vector.tensor_copy(n_e, ps[:, 7, NT * E_N:(NT + 1) * E_N]))
            step(nc.vector.tensor_scalar(k_e, n_e, float(CAP), None, ALU.is_gt))
            for m in range(2, STEPS + 1):
                step(nc.vector.scalar_tensor_tensor(k_e, n_e, float(m * CAP), k_e, ALU.is_gt, ALU.add))
            step(nc.vector.tensor_tensor_scan(cum, k[:, K_ONES:K_ONES + E_N], k_e, 0.0, ALU.mult, ALU.add))
            step(nc.vector.tensor_scalar(at, cum, k[:, K_PART:K_PART + 1], None, ALU.is_le))
            step(nc.vector.tensor_reduce(tab[:, 0:1], at, AX.X, ALU.add))
            step(nc.vector.tensor_tensor(at, at, k_e, ALU.mult))
            step(nc.vector.tensor_reduce(tab[:, 1:2], at, AX.X, ALU.add))
            step(nc.vector.tensor_tensor(tab[:, 2:3], k[:, K_PART:K_PART + 1], tab[:, 1:2], ALU.subtract))
            step(nc.vector.tensor_scalar(tab[:, 2:3], tab[:, 2:3], 1.0, float(CAP), ALU.add, ALU.mult))
            step(nc.vector.tensor_scalar(diag[:, 0, :], ident, tab[:, 0:1], None, ALU.mult))
            nc.vector.tensor_scalar(diag[:, 1, :], ident, tab[:, 2:3], None, ALU.mult).then_inc(s_dg, 1)
            dve.wait_ge(s_tab, 1)
            step(nc.vector.tensor_copy(G.extra_base[:, :], ps[:, 6, P:2 * P]))
            step(nc.vector.tensor_copy(G.extra_tab[:, 0:P], ps[0:1, 6, 0:P]))
            nc.vector.tensor_copy(G.extra_tab[:, P:P + 1], cum[0:1, E_N - 1:E_N]).then_inc(s_tabd, 1)
            dve.wait_ge(s_tabd, 1)

        @block.tensor
        def _(pe):
            def project_out(i):
                for half in range(2):
                    for f in range(2 * HEADS):
                        ins = nc.tensor.matmul(ps[:, 2 * i + half, :], catT[:, f, i * P:(i + 1) * P],
                                               wout[:, f, 512 * half:512 * (half + 1)], start=f == 0, stop=f == 2 * HEADS - 1)
                ins.then_inc(s_y, 1)

            def turn(i):
                pe.wait_ge(s_h2, i + 1)
                for c in range(KC):
                    ins = nc.tensor.transpose(ps[:, 2 * i + c // 4, (c % 4) * P:(c % 4 + 1) * P], h2n[:, i, c:D:KC], ident)
                    if c % 4 == 3:
                        ins.then_inc(s_h2T, 1)

            def router(i):
                for c in range(KC):
                    ins = nc.tensor.matmul(ps[:, 4, i * E_N:(i + 1) * E_N], h2T[:, c, i * P:(i + 1) * P], wr[:, c, :],
                                           start=c == 0, stop=c == KC - 1)
                if i == NT - 1:
                    ins.then_inc(s_lg, 1)

            def shared(f, t0, t1):
                for b, w in ((f, wg), (2 + f, wu)):
                    for c in range(KC):
                        ins = nc.tensor.matmul(ps[:, b, t0:t1], w[:, c, f * P:(f + 1) * P], h2T[:, c, t0:t1], start=c == 0, stop=c == KC - 1)
                if t1 == SEQ:
                    ins.then_inc(s_gu, 1)

            pe.wait_ge(G.s_wout, 16)
            project_out(0)
            for i in range(1, NT):
                project_out(i)
                turn(i - 1)
            pe.wait_ge(s_h2Td, 2 * (NT - 1))
            pe.wait_ge(s_in, 32)
            pe.wait_ge(s_wsh, 48)
            for i in range(NT - 1):
                router(i)
            shared(0, 0, (NT - 1) * P)
            turn(NT - 1)
            pe.wait_ge(s_h2Td, 2 * NT)
            router(NT - 1)
            shared(0, (NT - 1) * P, SEQ)
            shared(1, 0, SEQ)
            def places():
                pe.wait_ge(s_em, 1)
                for i in range(NT):
                    dst = ps[:, 7, i * E_N:(i + 1) * E_N]
                    for n in range(i):
                        nc.tensor.matmul(dst, ones, em[:, n, :], start=n == 0, stop=False)
                    nc.tensor.matmul(dst, k[:, K_STRICT:K_STRICT + P], em[:, i, :], start=i == 0, stop=True)
                for n in range(NT):
                    ins = nc.tensor.matmul(ps[:, 7, NT * E_N:(NT + 1) * E_N], ones, em[:, n, :], start=n == 0, stop=n == NT - 1)
                ins.then_inc(s_pos, 1)

            def shared_down(i):
                b = 4 * (i % 2)
                if i >= 2:
                    pe.wait_ge(s_dnd, i - 1)
                for half in range(2):
                    for f in range(FC):
                        ins = nc.tensor.matmul(ps[:, b + half, :], uT[:, f, i * P:(i + 1) * P], wd[:, f, 512 * half:512 * (half + 1)],
                                               start=f == 0, stop=f == FC - 1)
                ins.then_inc(s_dn, 1)

            places()
            pe.wait_ge(s_u, FC)
            for i in range(NT):
                shared_down(i)
            pe.wait_ge(s_dg, 1)
            for n in range(2):
                ins = nc.tensor.matmul(ps[:, 6, n * P:(n + 1) * P], ones, diag[:, n, :], start=True, stop=True)
            ins.then_inc(s_tab, 1)


RING = 4


def stage_experts(nc, A, G):
    with ExitStack() as own:
        def sb(name, shape, dt=F32):
            return own.enter_context(nc.sbuf_tensor(name, shape, dt))

        G.used = []

        def sem(name):
            G.used.append(own.enter_context(nc.semaphore(name)))
            return G.used[-1]

        k, ps, posm, gt = G.k, G.ps, G.posm, G.gt
        ident = k[:, K_ID:K_ID + P]
        wgu, wd = G.w_gate_up, G.w_down
        pick = sb("pick", [P, 2, NT, CAP], BF16)
        found = sb("found", [CAP, 4, 2])
        sidx = sb("row_numbers", [CAP, 4], I32)
        pad = sb("pad", [CAP, 2])
        xg = sb("xg", [CAP, 2, D])
        xT = sb("xT", [P, 2, KC, P])
        sg = sb("sg", [P, FC, P])
        uT = sb("uT", [P, 2, FC, P])
        yb = sb("yb", [CAP, 2, D])

        w_gate, w_up, w_down = A["w_exp_gate"][0], A["w_exp_up"][0], A["w_exp_down"][0]

        def load_weights(eng, e, slot, s_wgu, s_wd, before_down=None):
            eng.dma_start(wgu[slot][:, 0], w_gate[e].rearrange("(p c) f -> p c f", c=KC)).then_inc(s_wgu, 16)
            eng.dma_start(wgu[slot][:, 1], w_up[e].rearrange("(p c) f -> p c f", c=KC)).then_inc(s_wgu, 16)
            if before_down is not None:
                eng.wait_ge(*before_down)
            eng.dma_start(wd[slot], w_down[e].rearrange("(f p) n -> p f n", p=P)).then_inc(s_wd, 16)

        def pick_rows(q, n, bank):
            q(nc.vector.tensor_reduce(found[:, n, :], ps[0:CAP, bank, 0:6].rearrange("p (a b) -> p a b", a=2), AX.X, ALU.add))
            f = found[:, n, 0:1]
            q(nc.vector.tensor_scalar(pad[:, 0:1], f, 0.0, k[0:CAP, K_PADROW:K_PADROW + 1], ALU.is_equal, ALU.mult))
            return nc.vector.scalar_tensor_tensor(sidx[:, n:n + 1], f, -1.0, pad[:, 0:1], ALU.add, ALU.add)

        def gather_rows(pool, slot, n):
            return pool.indirect_dma_start(out=xg[:, slot, :], out_offset=None, in_=G.h2_rows,
                                           in_offset=bass.IndirectOffsetOnAxis(ap=sidx[:, n:n + 1], axis=0),
                                           bounds_check=SEQ - 1, oob_is_err=False)

        with ExitStack() as inner:
            def isem(name):
                return inner.enter_context(nc.semaphore(name))

            s_wgu, s_wd = G.s_wgu, G.s_wd
            dch = isem("dve_chain")
            s_pick = isem("pick_built")
            s_find = isem("rows_found")
            s_idx = isem("row_numbers")
            s_g = [isem(f"gathered{n}") for n in range(2)]
            s_xp = isem("x_transposed")
            s_xd = isem("xT_low_copied")
            s_xa = isem("xT_high_copied")
            s_gu = isem("gate_up_done")
            s_sg = isem("silu_done")
            s_u = isem("u_ready")
            s_dn = isem("down_done")
            s_ya = isem("y_low_ready")
            s_yd = isem("y_high_ready")
            s_sc = isem("scattered")
            s_passed = isem("pool_waits_passed")
            s_zero = isem("xg_zero")
            block = inner.enter_context(nc.Block())

            @block.sync
            def _(sp):
                for n in range(2):
                    sp.wait_ge(s_g[n], 16)
                for e in range(2, RING):
                    load_weights(sp, e, e, s_wgu[e], s_wd[e])
                with sp.Fori(0, E_N // RING - 1) as t:
                    for n in range(RING):
                        sp.wait_ge(s_gu, RING * t + n + 1)
                        load_weights(sp, RING * t + (n + RING), n, s_wgu[n], s_wd[n],
                                     (s_dn, RING * t + n + 1))

            @block.gpsimd
            def _(pool):
                nc.gpsimd.memset(xg[:, :, :], 0.0).then_inc(s_zero, 1)
                for n in range(2):
                    pool.dma_start(G.y_rows[SEQ + n * 64:SEQ + (n + 1) * 64, :], G.xt[0:64, 0, :]).then_inc(s_sc, 16)
                pool.wait_ge(s_zero, 1)
                for n in range(2):
                    pool.wait_ge(s_idx, n + 1)
                    gather_rows(pool, n, n).then_inc(s_g[n], 16)
                with pool.Fori(0, E_N // RING) as t:
                    for n in range(RING):
                        e = RING * t + n
                        pool.wait_ge(s_idx, e + 3)
                        pool.wait_ge(s_xp, e + 1)
                        pool.sem_inc(s_passed, 1)
                        gather_rows(pool, n % 2, (n + 2) % RING).then_inc(s_g[n % 2], 16)
                        pool.wait_ge(s_ya, e + 2)
                        pool.wait_ge(s_yd, e + 2)
                        pool.wait_ge(s_sc, 16 * e + 32)
                        pool.sem_inc(s_passed, 1)
                        pool.indirect_dma_start(out=G.y_rows, out_offset=bass.IndirectOffsetOnAxis(ap=sidx[:, n:n + 1], axis=0),
                                                in_=yb[:, n % 2, :], in_offset=None, compute_op=ALU.add).then_inc(s_sc, 16)
                pool.wait_ge(s_sc, 16 * E_N + 32)
                pool.wait_ge(s_g[0], 16 * (E_N // 2 + 1))
                pool.wait_ge(s_g[1], 16 * (E_N // 2 + 1))

            @block.scalar
            def _(act):
                def copy_xT(slot, e1):
                    act.wait_ge(s_xp, e1)
                    nc.scalar.activation(xT[:, slot, 4:8, 0:CAP], ps[:, 1, :].rearrange("p (c t) -> p c t", c=4)[:, :, 0:CAP],
                                         ACT.Copy).then_inc(s_xa, 1)

                act.sem_inc(s_ya, 1)
                copy_xT(0, 1)
                with act.Fori(0, E_N // RING) as t:
                    for n in range(RING):
                        e = RING * t + n
                        act.wait_ge(s_gu, e + 1)
                        act.wait_ge(s_u, e + 1)
                        gate = ps[:, 2 + n % 2, 0:2 * P].rearrange("p (f t) -> p f t", f=FC)
                        nc.scalar.activation(sg[:, :, 0:CAP], gate[:, :, 0:CAP], ACT.Silu).then_inc(s_sg, 1)
                        copy_xT((n + 1) % 2, e + 2)
                        act.wait_ge(s_dn, e + 1)
                        act.wait_ge(s_sc, 16 * e + 16)
                        nc.scalar.activation(yb[:, n % 2, 0:512], ps[0:CAP, 4, :], ACT.Copy,
                                             scale=found[:, n, 1:2]).then_inc(s_ya, 1)

            @block.vector
            def _(dve):
                step = Chain(dve, dch)
                count = [0]

                def build_pick(e, slot):
                    for i in range(NT):
                        ins = nc.vector.tensor_scalar(pick[:, slot, i, :], k[:, K_IOTA:K_IOTA + CAP],
                                                      posm[:, bass.ds(NT * e + i, 1)], None, ALU.is_equal)
                    ins.then_inc(s_pick, 1)

                def link(base):
                    def q(ins):
                        count[0] += 1
                        ins.then_inc(dch, 1)
                        dve.wait_ge(dch, base + count[0])
                    return q

                def read_found(e1, n, base):
                    dve.wait_ge(s_find, e1)
                    pick_rows(link(base), n, 6 + n % 2).then_inc(s_idx, 1)

                def copy_xT(slot, e1):
                    dve.wait_ge(s_xp, e1)
                    nc.vector.tensor_copy(xT[:, slot, 0:4, 0:CAP],
                                          ps[:, 0, :].rearrange("p (c t) -> p c t", c=4)[:, :, 0:CAP]).then_inc(s_xd, 1)

                dve.sem_inc(s_u, 1)
                dve.sem_inc(s_yd, 1)
                build_pick(0, 0)
                build_pick(1, 1)
                read_found(1, 0, 0)
                read_found(2, 1, 0)
                build_pick(2, 0)
                copy_xT(0, 1)
                first = count[0]
                with dve.Fori(0, E_N // RING) as t:
                    count[0] = 0
                    for n in range(RING):
                        e = RING * t + n
                        dve.wait_ge(s_sg, e + 1)
                        up = ps[:, 2 + n % 2, 2 * P:4 * P].rearrange("p (f t) -> p f t", f=FC)
                        nc.vector.tensor_tensor(uT[:, n % 2, :, 0:CAP], sg[:, :, 0:CAP], up[:, :, 0:CAP], ALU.mult).then_inc(s_u, 1)
                        dve.wait_ge(s_sc, 16 * e + 16)
                        read_found(e + 3, (n + 2) % RING, 2 * RING * t + first)
                        copy_xT((n + 1) % 2, e + 2)
                        dve.wait_ge(s_dn, e + 1)
                        nc.vector.tensor_scalar(yb[:, n % 2, 512:D], ps[0:CAP, 5, :], found[:, n, 1:2], None,
                                                ALU.mult).then_inc(s_yd, 1)
                        build_pick(e + 3, (n + 1) % 2)
                    assert count[0] == 2 * RING

            @block.tensor
            def _(pe):
                def find(e, n, slot):
                    pe.wait_ge(s_pick, e + 1)
                    for i in range(NT):
                        ins = nc.tensor.matmul(ps[0:CAP, 6 + slot, 0:6], pick[:, slot, i, :],
                                               gt[:, bass.ds(e, 1), i, :].rearrange("p o t -> p (o t)"), start=i == 0, stop=i == NT - 1)
                    ins.then_inc(s_find, 1)

                def transpose_x(slot, count):
                    pe.wait_ge(s_g[slot], count)
                    for c in range(KC):
                        ins = nc.tensor.transpose(ps[:, c // 4, (c % 4) * P:(c % 4) * P + CAP], xg[:, slot, c:D:KC], ident[0:CAP, 0:CAP])
                    ins.then_inc(s_xp, 1)

                find(0, 0, 0)
                find(1, 1, 1)
                transpose_x(0, 16)
                with pe.Fori(0, E_N // RING) as t:
                    for n in range(RING):
                        e = RING * t + n
                        pe.wait_ge(s_wgu[n], 32 * t + 32)
                        pe.wait_ge(s_xd, e + 1)
                        pe.wait_ge(s_xa, e + 1)
                        for m in range(2):
                            for f in range(FC):
                                at = (2 * m + f) * P
                                for c in range(KC):
                                    ins = nc.tensor.matmul(ps[:, 2 + n % 2, at:at + CAP], wgu[n][:, m, c, f * P:(f + 1) * P],
                                                           xT[:, n % 2, c, 0:CAP], start=c == 0, stop=c == KC - 1)
                        ins.then_inc(s_gu, 1)
                        pe.wait_ge(s_idx, e + 1)
                        find(e + 2, n, n % 2)
                        transpose_x((n + 1) % 2, 32 * t + 16 * ((n + 1) // 2) + 16)
                        pe.wait_ge(s_wd[n], 16 * t + 16)
                        pe.wait_ge(s_u, e + 2)
                        pe.wait_ge(s_ya, e + 1)
                        pe.wait_ge(s_yd, e + 1)
                        for half in range(2):
                            for f in range(FC):
                                ins = nc.tensor.matmul(ps[0:CAP, 4 + half, :], uT[:, n % 2, f, 0:CAP],
                                                       wd[n][:, f, 512 * half:512 * (half + 1)], start=f == 0, stop=f == FC - 1)
                        ins.then_inc(s_dn, 1)

        with ExitStack() as inner:
            def isem(name):
                return inner.enter_context(nc.semaphore(name))

            s_wgu, s_wd = isem("x_gate_up_landed"), isem("x_down_landed")
            dch = isem("dve_chain")
            s_pick, s_find, s_idx, s_g = isem("x_pick_built"), isem("x_rows_found"), isem("x_row_numbers"), isem("x_gathered")
            s_xp, s_xd, s_xa = isem("x_x_transposed"), isem("x_xT_low_copied"), isem("x_xT_high_copied")
            s_gu, s_sg, s_u, s_dn = isem("x_gate_up_done"), isem("x_silu_done"), isem("x_u_ready"), isem("x_down_done")
            s_ya, s_yd, s_sc = isem("x_y_low_ready"), isem("x_y_high_ready"), isem("x_scattered")
            s_added, s_passed = isem("x_tile_added"), isem("x_pool_waits_passed")
            block = inner.enter_context(nc.Block())

            def extra_tiles(eng, body):
                total = eng.value_load(G.extra_tab[0:1, P:P + 1], min_val=0, max_val=MAX_EXTRA)
                with eng.If(total > 0):
                    with eng.Fori(0, MAX_EXTRA) as j:
                        with eng.If(total > j):
                            body(j)

            def expert_of(eng, j):
                return eng.value_load(G.extra_tab[0:1, bass.ds(j, 1)], min_val=0, max_val=E_N - 1)

            @block.sync
            def _(sp):
                def body(j):
                    sp.wait_ge(s_dn, j + 1)
                    load_weights(sp, expert_of(sp, j), 0, s_wgu, s_wd)

                sp.sem_inc(s_dn, 1)
                extra_tiles(sp, body)

            @block.gpsimd
            def _(pool):
                def body(j):
                    pool.wait_ge(s_idx, j + 1)
                    pool.sem_inc(s_passed, 1)
                    gather_rows(pool, 0, 0).then_inc(s_g, 16)
                    pool.wait_ge(s_ya, j + 1)
                    pool.wait_ge(s_yd, j + 1)
                    pool.sem_inc(s_passed, 1)
                    pool.indirect_dma_start(out=G.y_rows, out_offset=bass.IndirectOffsetOnAxis(ap=sidx[:, 0:1], axis=0),
                                            in_=yb[:, 0, :], in_offset=None, compute_op=ALU.add).then_inc(s_sc, 16)
                    pool.wait_ge(s_sc, 16 * j + 16)
                    pool.sem_inc(s_added, 1)

                pool.sem_inc(s_added, 1)
                extra_tiles(pool, body)

            @block.scalar
            def _(act):
                def body(j):
                    act.wait_ge(s_xp, j + 1)
                    nc.scalar.activation(xT[:, 0, 4:8, 0:CAP], ps[:, 1, :].rearrange("p (c t) -> p c t", c=4)[:, :, 0:CAP],
                                         ACT.Copy).then_inc(s_xa, 1)
                    act.wait_ge(s_gu, j + 1)
                    gate = ps[:, 2, 0:2 * P].rearrange("p (f t) -> p f t", f=FC)
                    nc.scalar.activation(sg[:, :, 0:CAP], gate[:, :, 0:CAP], ACT.Silu).then_inc(s_sg, 1)
                    act.wait_ge(s_dn, j + 2)
                    nc.scalar.activation(yb[:, 0, 0:512], ps[0:CAP, 4, :], ACT.Copy, scale=found[:, 0, 1:2]).then_inc(s_ya, 1)

                extra_tiles(act, body)

            @block.vector
            def _(dve):
                def body(j):
                    e = expert_of(dve, j)
                    dve.wait_ge(s_added, j + 1)
                    for i in range(NT):
                        ins = nc.vector.tensor_scalar(pick[:, 0, i, :], k[:, K_IOTA:K_IOTA + CAP], G.extra_base[:, bass.ds(j, 1)],
                                                      posm[:, bass.ds(NT * e + i, 1)], ALU.add, ALU.is_equal)
                    ins.then_inc(s_pick, 1)
                    dve.wait_ge(s_find, j + 1)
                    count = [0]

                    def q(ins):
                        count[0] += 1
                        ins.then_inc(dch, 1)
                        dve.wait_ge(dch, 2 * j + count[0])

                    pick_rows(q, 0, 6).then_inc(s_idx, 1)
                    dve.wait_ge(s_xp, j + 1)
                    nc.vector.tensor_copy(xT[:, 0, 0:4, 0:CAP], ps[:, 0, :].rearrange("p (c t) -> p c t", c=4)[:, :, 0:CAP]).then_inc(s_xd, 1)
                    dve.wait_ge(s_sg, j + 1)
                    up = ps[:, 2, 2 * P:4 * P].rearrange("p (f t) -> p f t", f=FC)
                    nc.vector.tensor_tensor(uT[:, 0, :, 0:CAP], sg[:, :, 0:CAP], up[:, :, 0:CAP], ALU.mult).then_inc(s_u, 1)
                    dve.wait_ge(s_dn, j + 2)
                    nc.vector.tensor_scalar(yb[:, 0, 512:D], ps[0:CAP, 5, :], found[:, 0, 1:2], None, ALU.mult).then_inc(s_yd, 1)

                extra_tiles(dve, body)

            @block.tensor
            def _(pe):
                def body(j):
                    e = expert_of(pe, j)
                    pe.wait_ge(s_pick, j + 1)
                    for i in range(NT):
                        ins = nc.tensor.matmul(ps[0:CAP, 6, 0:6], pick[:, 0, i, :],
                                               gt[:, bass.ds(e, 1), i, :].rearrange("p o t -> p (o t)"), start=i == 0, stop=i == NT - 1)
                    ins.then_inc(s_find, 1)
                    pe.wait_ge(s_g, 16 * j + 16)
                    for c in range(KC):
                        ins = nc.tensor.transpose(ps[:, c // 4, (c % 4) * P:(c % 4) * P + CAP], xg[:, 0, c:D:KC], ident[0:CAP, 0:CAP])
                    ins.then_inc(s_xp, 1)
                    pe.wait_ge(s_wgu, 32 * j + 32)
                    pe.wait_ge(s_xd, j + 1)
                    pe.wait_ge(s_xa, j + 1)
                    for m in range(2):
                        for f in range(FC):
                            at = (2 * m + f) * P
                            for c in range(KC):
                                ins = nc.tensor.matmul(ps[:, 2, at:at + CAP], wgu[0][:, m, c, f * P:(f + 1) * P], xT[:, 0, c, 0:CAP],
                                                       start=c == 0, stop=c == KC - 1)
                    ins.then_inc(s_gu, 1)
                    pe.wait_ge(s_wd, 16 * j + 16)
                    pe.wait_ge(s_u, j + 1)
                    for half in range(2):
                        for f in range(FC):
                            ins = nc.tensor.matmul(ps[0:CAP, 4 + half, :], uT[:, 0, f, 0:CAP], wd[0][:, f, 512 * half:512 * (half + 1)],
                                                   start=f == 0, stop=f == FC - 1)
                    ins.then_inc(s_dn, 1)

                extra_tiles(pe, body)

        stage_final(nc, A, G)


def stage_final(nc, A, G):
    with ExitStack() as own:
        def sb(name, shape, dt=F32):
            return own.enter_context(nc.sbuf_tensor(name, shape, dt))

        G.used = []

        def sem(name):
            G.used.append(own.enter_context(nc.semaphore(name)))
            return G.used[-1]

        xt, rows = G.xt, G.rows
        y = G.big[:, 0:NT * D].rearrange("p (i d) -> p i d", i=NT)
        sq = G.big[:, NT * D:(NT + 2) * D].rearrange("p (i d) -> p i d", i=2)
        ss = sb("ss_final", [P, NT])
        rt = sb("rt_final", [P, NT])
        s_in = [sem(f"y_landed{i}") for i in range(NT)]
        s_sq, s_ms, s_rt, s_o, s_out = sem("y_squares"), sem("y_mean_square"), sem("y_root"), sem("out_ready"), sem("out_stored")
        dch = sem("dve_chain")
        block = own.enter_context(nc.Block())

        @block.sync
        def _(sp):
            for i in range(NT):
                sp.dma_start(y[:, i, :], G.y_rows[i * P:(i + 1) * P, :]).then_inc(s_in[i], 16)
            for i in range(NT):
                sp.wait_ge(s_o, i + 1)
                sp.dma_start(G.out[0, i * P:(i + 1) * P, :], xt[:, i, :]).then_inc(s_out, 16)
            sp.wait_ge(s_out, 16 * NT)

        @block.scalar
        def _(act):
            for i in range(NT):
                act.wait_ge(s_in[i], 16)
                nc.scalar.activation(sq[:, i % 2, :], y[:, i, :], ACT.Square, accum_out=ss[:, i:i + 1]).then_inc(s_sq, 1)
                act.wait_ge(s_ms, i + 1)
                nc.scalar.activation(rt[:, i:i + 1], ss[:, i:i + 1], ACT.Sqrt).then_inc(s_rt, 1)

        @block.vector
        def _(dve):
            step = Chain(dve, dch)
            for i in range(NT):
                dve.wait_ge(s_sq, i + 1)
                nc.vector.tensor_scalar(ss[:, i:i + 1], ss[:, i:i + 1], 1.0 / D, EPS, ALU.mult, ALU.add).then_inc(s_ms, 1)
                dve.wait_ge(s_rt, i + 1)
                step(nc.vector.reciprocal(rt[:, i:i + 1], rt[:, i:i + 1]))
                step(nc.vector.scalar_tensor_tensor(y[:, i, :], y[:, i, :], rt[:, i:i + 1], rows[:, 3, :], ALU.mult, ALU.mult))
                nc.vector.tensor_tensor(xt[:, i, :], xt[:, i, :], y[:, i, :], ALU.add).then_inc(s_o, 1)


def clear_semaphores(nc, sems):
    with nc.Block() as block:
        @block.gpsimd
        def _(pool):
            for s in sems:
                pool.sem_clear(s)


class Shared:
    pass


def build(nc, A, out):
    with ExitStack() as ctx:
        def sb(name, shape, dt=F32):
            return ctx.enter_context(nc.sbuf_tensor(name, shape, dt))

        G = Shared()
        G.ps = ctx.enter_context(nc.psum_tensor("ps", [P, 8, 512], F32))
        G.k = sb("consts", [P, K_W])
        G.gb = sb("gate_bias", [HEADS, 2])
        G.cols = sb("cols", [P, 44])
        G.rows = sb("rows", [P, 4, D])
        G.maskb = sb("maskb", [P, NT, SEQ])
        G.xt = sb("xt", [P, NT, D])
        G.s_roped = ctx.enter_context(nc.semaphore("attention_rotated"))
        G.s_wgu = [ctx.enter_context(nc.semaphore(f"gate_up_landed{n}")) for n in range(RING)]
        G.s_wd = [ctx.enter_context(nc.semaphore(f"down_landed{n}")) for n in range(RING)]
        G.s_wout = ctx.enter_context(nc.semaphore("w_out_landed"))
        G.posm = sb("place_in_expert", [P, E_PAD * NT])
        G.gt = sb("token_and_gate", [P, E_PAD, NT, 6], BF16)
        G.extra_base = sb("extra_base", [P, P])
        G.extra_tab = sb("extra_tab", [1, P + 1], I32)
        G.h2_rows = nc.dram_tensor("h2_rows", (SEQ, D), F32, kind="Internal").ap()
        G.y_rows = nc.dram_tensor("y_rows", (SEQ + P, D), F32, kind="Internal").ap()
        G.out = out
        G.QKC = NT * NAT_W
        G.FREE = G.QKC + 2 * HEADS * SEQ
        G.big = sb("big", [P, G.FREE + 10240])
        G.nat = G.big[:, 0:G.QKC].rearrange("p (i n) -> p i n", i=NT)
        G.qkc = G.big[:, G.QKC:G.FREE].rearrange("p (c t) -> p c t", c=2 * HEADS)
        G.arena = G.big[:, G.FREE:G.FREE + 6144]
        G.catT = G.big[:, G.FREE + 6144:G.FREE + 10240].rearrange("p (c t) -> p c t", c=2 * HEADS)
        stage_in(nc, A, G)
        clear_semaphores(nc, G.used)
        G.wout = sb("wout", [P, 2 * HEADS, D])
        wout = G.wout[:, :, :].rearrange("p f n -> p (f n)")
        G.w_gate_up = [t.rearrange("p (m c f) -> p m c f", m=2, c=KC)
                       for t in (wout[:, 0:4096], wout[:, 4096:8192], G.big[:, 0:4096], G.big[:, 4096:8192])]
        G.w_down = [G.big[:, at:at + FC * D].rearrange("p (f n) -> p f n", f=FC)
                    for at in (G.FREE + 6144, G.FREE + 8192, G.QKC, G.QKC + 2048)]
        stage_attention(nc, A, G)
        clear_semaphores(nc, G.used)
        stage_route(nc, A, G)
        stage_experts(nc, A, G)


INS = ["x", "c", "w_ada", "b_ada", "g_mix_pre", "g_mix_post", "g_ffn_pre", "g_ffn_post", "w_in", "conv_w", "conv_b",
       "b_igate", "b_fgate", "g_mlstm_head", "g_idx_k", "b_idx_k", "w_out", "w_router", "b_router", "w_exp_gate",
       "w_exp_up", "w_exp_down", "w_sh_gate", "w_sh_up", "w_sh_down"]


def kernel(**inputs):
    import concourse.bacc as bacc
    from concourse.bass_utils import run_bass_kernel_spmd

    nc = bacc.Bacc("TRN2", target_bir_lowering=False, num_devices=1)
    arrays = {f"in_{n}": np.ascontiguousarray(inputs[n]) for n in INS}
    arrays["in_consts"] = constants()
    A = {n[3:]: nc.dram_tensor(n, a.shape, mybir.dt.from_np(a.dtype), kind="ExternalInput").ap() for n, a in arrays.items()}
    out = nc.dram_tensor("out_y", (1, SEQ, D), F32, kind="ExternalOutput").ap()
    build(nc, A, out)
    return run_bass_kernel_spmd(nc, [arrays], core_ids=[0]).results[0]["out_y"]
```

```python
from contextlib import ExitStack

import numpy as np

import concourse.bass as bass
from concourse import mybir

F32 = mybir.dt.float32
FR = mybir.dt.float32r
BF16 = mybir.dt.bfloat16
I32 = mybir.dt.int32
ALU = mybir.AluOpType
ACT = mybir.ActivationFunctionType
AX = mybir.AxisListType

P = 128
SEQ = 512
D = 1024
NT = SEQ // P
KC = D // P
CHUNK = 64
HEADS = 4
DH = 128
IH = 4
IDIM = 64
CONV = 4
TOPK = 128
THETA = 500000.0
E_N = 64
E_GROUPS = 8
E_PER = E_N // E_GROUPS
E_TOPG = 4
DE = 256
FC = DE // P
ROUTE_SCALE = 2.5
EPS = 1e-6
NEG = -1e30
FMIN = -3.4028234e38
FMASK = -3.0e38
CAP = P
MAX_EXTRA = SEQ * 8 // CAP
STEPS = (SEQ - 1) // CAP
MEAN = SEQ * 8 // E_N
SIZES = [*range(MEAN - 16, CAP, 8), CAP]

QK_W = 2 * HEADS * DH
V0 = 0
O0 = V0 + HEADS * DH
I0 = O0 + HEADS * DH
F0 = I0 + HEADS
AQ0 = F0 + HEADS
AK0 = AQ0 + HEADS * DH
AV0 = AK0 + DH
IQ0 = AV0 + DH
IK0 = IQ0 + IH * IDIM
IW0 = IK0 + IDIM
NAT_W = IW0 + IH
ROT_A = DH // 4 // 2
ROT_I = IDIM // 4 // 2

K_ID = 0
K_TRI = K_ID + P
K_STRICT = K_TRI + P
K_ONES = K_STRICT + P
K_IOTA = K_ONES + P
K_SEL = K_IOTA + P
K_CAUSAL = K_SEL + HEADS * P
K_TOKH = K_CAUSAL + P
K_TOKL = K_TOKH + NT
K_PADROW = K_TOKL + NT
K_PART = K_PADROW + 1
K_COSA = K_PART + 1
K_SINA = K_COSA + NT * ROT_A
K_COSI = K_SINA + NT * ROT_A
K_SINI = K_COSI + NT * ROT_I
K_W = K_SINI + NT * ROT_I


def constants():
    k = np.zeros((P, K_W), np.float32)
    i = np.arange(P)
    k[:, K_ID:K_ID + P] = np.eye(P)
    k[:, K_TRI:K_TRI + P] = np.where(i[:, None] <= i[None, :], 0.0, NEG)
    k[:, K_STRICT:K_STRICT + P] = i[:, None] < i[None, :]
    k[:, K_ONES:K_ONES + P] = 1.0
    k[:, K_IOTA:K_IOTA + P] = i[None, :]
    for h in range(HEADS):
        k[h, K_SEL + h * P:K_SEL + (h + 1) * P] = 1.0
    k[:, K_CAUSAL:K_CAUSAL + P] = np.where(i[None, :] // CHUNK <= i[:, None] // CHUNK, 0.0, NEG)
    tok = i[:, None] + P * np.arange(NT)[None, :] + 1
    k[:, K_TOKH:K_TOKH + NT] = tok // 256 * 256
    k[:, K_TOKL:K_TOKL + NT] = tok % 256
    k[:, K_PADROW] = SEQ + 1 + i
    k[:, K_PART] = i
    for half, at_cos, at_sin in ((ROT_A, K_COSA, K_SINA), (ROT_I, K_COSI, K_SINI)):
        inv = np.exp(-np.log(np.float32(THETA)) * np.arange(half, dtype=np.float32) * np.float32(1.0 / half))
        ang = np.arange(SEQ, dtype=np.float32)[:, None] * inv.astype(np.float32)[None, :]
        for at, f in ((at_cos, np.cos), (at_sin, np.sin)):
            k[:, at:at + NT * half] = f(ang).reshape(NT, P, half).transpose(1, 0, 2).reshape(P, NT * half)
    return k


class Chain:

    def __init__(self, eng, sem):
        self.eng, self.sem, self.n = eng, sem, 0

    def __call__(self, ins):
        self.n += 1
        ins.then_inc(self.sem, 1)
        self.eng.wait_ge(self.sem, self.n)


SLOTS = 4
SLOT_W = 2176
NAT_PIECES = [(1852, 272), (1586, 266), (1320, 266), (1056, 264), (792, 264), (528, 264), (264, 264), (0, 264)]
assert sum(w for _, w in NAT_PIECES) == NAT_W
QK_PIECES = 4
ADA = [("ada", s, q) for s in range(2) for q in range(4)]
ROWS = [("row", s, q) for s in range(2, 5) for q in range(4)]
LAST_ROW = [("last", 5, q) for q in range(4)]
ITEMS = [("nat", n, 0) for n in range(5)] + [("qk", n, 0) for n in range(QK_PIECES)] + [("nat", n, 0) for n in range(5, 8)]
STREAM = (ADA + ITEMS[0:2] + ROWS[0:2] + ITEMS[2:3] + ROWS[2:5] + ITEMS[3:5] + ROWS[5:7] + ITEMS[5:6] + ROWS[7:8] + ITEMS[6:8]
          + LAST_ROW[0:1] + ITEMS[8:9] + LAST_ROW[1:2] + ITEMS[9:10] + ROWS[8:9] + LAST_ROW[2:3] + ITEMS[10:] + LAST_ROW[3:4]
          + ROWS[9:])


def stage_in(nc, A, G):
    with ExitStack() as own:
        def sb(name, shape, dt=F32):
            return own.enter_context(nc.sbuf_tensor(name, shape, dt))

        G.used, held = [], G.held[0]

        def sem(name):
            G.used.append(held.enter_context(nc.semaphore("in_" + name)))
            return G.used[-1]

        k, nat, qkc, rows, maskb, cols, ps = G.k, G.nat, G.qkc, G.rows, G.maskb, G.cols, G.ps
        ident = k[:, K_ID:K_ID + P]
        free = G.side[:, :]
        stage = free[:, 0:SLOTS * SLOT_W].rearrange("p (s n) -> p s n", s=SLOTS)
        tmp = free[:, SLOTS * SLOT_W:SLOTS * SLOT_W + 1024].rearrange("p (b n) -> p b n", b=2)
        work = free[:, SLOTS * SLOT_W + 1024:SLOTS * SLOT_W + 1536]
        x_in = G.main[:, 0:NT * D].rearrange("p (i d) -> p i d", i=NT)
        hf = G.main[:, 0:KC * SEQ].rearrange("p (c t) -> p c t", c=KC)
        xn = G.main[:, G.QKC:G.QKC + NT * D].rearrange("p (i d) -> p i d", i=NT)
        acc = maskb[:, :, :].rearrange("p i t -> p (i t)").rearrange("p (s n) -> p s n", s=2)
        hhi = sb("hT_hi", [P, KC, SEQ], FR)
        hlo = sb("hT_lo", [P, KC, SEQ], FR)
        whi = sb("w_hi", [P, 2, SLOT_W], FR)
        wlo = sb("w_lo", [P, 2, SLOT_W], FR)
        flat = G.xt[:, :, :].rearrange("p i d -> p (i d)")
        RAW = 4 * (SEQ + CONV - 1)
        raw = flat[:, 0:RAW].rearrange("p (b n) -> p b n", b=4)
        ropet = flat[:, RAW:RAW + 4 * NT * HEADS * ROT_A].rearrange("p (n i h d) -> p n i h d", n=4, i=NT, h=HEADS)
        ikT = flat[0:IDIM, 3200:3200 + SEQ]
        lnb = flat[:, 3712:3712 + NT * IDIM].rearrange("p (i d) -> p i d", i=NT)
        cT = sb("cT", [P, KC])
        cs = sb("cs", [P, KC])
        gpre = sb("gpre", [P, KC])
        bcol = sb("bcol", [P, 2, KC])
        modA = sb("modA", [P, KC])
        modB = sb("modB", [P, KC])
        colrows = sb("colrows", [44, P])
        gik = sb("gik", [P, IDIM])
        bik = sb("bik", [P, IDIM])
        ss = sb("ss", [P, 4 * NT])
        rs = sb("rs", [P, 4 * NT])
        iqT = raw[0:IDIM, :, CONV - 1:]
        iwS = flat[:, 3104:3104 + NT * IH].rearrange("p (i h) -> p i h", i=NT)
        relu = tmp
        top8 = flat[:, 3136:3144]

        s_in = sem("small")
        s_c = sem("c_landed")
        s_bias = sem("biases_landed")
        s_x = sem("x")
        landed = [sem(f"piece_landed{i}") for i in range(SLOTS)]
        s_ada_used = sem("ada_piece_used")
        s_row_used = sem("row_piece_used")
        s_last_used = sem("last_row_piece_used")
        s_scaled = sem("last_row_piece_scaled")
        dch, ach, pch = sem("dve_chain"), sem("act_chain"), sem("pool_chain")
        s_silu = sem("c_silu")
        s_ssq = sem("x_squares")
        s_ms = sem("x_mean_square")
        s_rt = sem("x_root")
        s_xn = sem("x_normed")
        s_cols = sem("cols_transposed")
        s_colsd = sem("cols_copied")
        s_mod = sem("mod_columns")
        s_modd = sem("mod_ready")
        s_xT = sem("x_transposed")
        s_hf = sem("h_modulated")
        s_hhi = sem("h_hi")
        s_hlo = sem("h_lo")
        s_whi = sem("w_hi_ready")
        s_wlo = sem("w_lo_ready")
        s_nat = sem("projected")
        s_natd = sem("projection_copied")
        s_conv = sem("conv_done")
        s_tap = sem("conv_first_tap")
        s_qk = sem("qk_activated")
        s_zero = sem("conv_pad_zero")
        s_lnv = sem("ik_variance")
        s_ln = sem("ik_normed")
        s_lnr = sem("ik_root")
        s_rope = sem("indexer_rotated")
        s_iT = sem("indexer_transposed")
        s_iTd = sem("indexer_T_copied")
        s_rel = sem("indexer_products")
        s_relu = sem("indexer_relu")
        s_sc = sem("indexer_summed")
        s_iw = sem("indexer_weights")

        first, n_out = [], 0
        for kind, _, _ in ITEMS:
            first.append(n_out)
            n_out += NT if kind == "nat" else 2
        QK_FIRST = first[5]
        IDX_DONE = first[2]
        freed, count = [], {"ada": 0, "row": 0, "last": 0}
        for piece in STREAM:
            if piece[0] in count:
                count[piece[0]] += 1
                freed.append(({"row": s_row_used, "ada": s_ada_used, "last": s_last_used}[piece[0]], count[piece[0]]))
            else:
                freed.append((s_wlo, ITEMS.index(piece) + 1))
        place = {piece: n for n, piece in enumerate(STREAM)}

        def arrived(eng, piece):
            n = place[piece]
            eng.wait_ge(landed[n % SLOTS], 16 * (n // SLOTS + 1))
            return n % SLOTS

        def width(piece):
            return NAT_PIECES[piece[1]][1] if piece[0] == "nat" else 256

        block = own.enter_context(nc.Block())

        @block.sync
        def _(sp):
            sp.dma_start(cT[:, :], A["c"].rearrange("a (p c) -> (a p) c", c=KC)).then_inc(s_c, 16)
            w_ada = A["w_ada"][0].rearrange("(p c) n -> p c n", c=KC)
            w_in = A["w_in"][0].rearrange("(p c) n -> p c n", c=KC)
            for n, piece in enumerate(STREAM):
                kind, a, b = piece
                if n >= SLOTS:
                    sp.wait_ge(*freed[n - SLOTS])
                if kind in ("ada", "row", "last"):
                    dst = stage[:, n % SLOTS, 0:2 * D].rearrange("p (c n) -> p c n", c=2)
                    src = w_ada[:, 2 * b:2 * b + 2, a * D:(a + 1) * D]
                else:
                    w = width(piece)
                    c0 = a * 256 if kind == "qk" else QK_W + NAT_PIECES[a][0]
                    dst = stage[:, n % SLOTS, 0:KC * w].rearrange("p (c n) -> p c n", c=KC)
                    src = w_in[:, :, c0:c0 + w]
                sp.dma_start(dst, src).then_inc(landed[n % SLOTS], 16)
                if n == 1:
                    sp.dma_start(x_in, A["x"][0].rearrange("(i p) d -> p i d", p=P)).then_inc(s_x, 16)

        @block.gpsimd
        def _(pool):
            step = Chain(pool, pch)
            nc.gpsimd.memset(rows[:, :, :], 0.0).then_inc(s_zero, 1)
            nc.gpsimd.memset(raw[:, :, 0:CONV - 1], 0.0).then_inc(s_zero, 1)

            def low_part(m):
                n = KC * width(ITEMS[m])
                pool.wait_ge(s_whi, m + 1)
                nc.gpsimd.tensor_tensor(wlo[:, m % 2, 0:n], stage[:, place[ITEMS[m]] % SLOTS, 0:n],
                                        whi[:, m % 2, 0:n].bitcast(F32), ALU.subtract).then_inc(s_wlo, 1)

            def rope(at, heads, dim, half, cos_at, sin_at, last):
                v = nat[:, :, at:at + heads * dim].rearrange("p i (h d) -> p i h d", h=heads)
                x1, x2 = v[:, :, :, 0:half], v[:, :, :, half:2 * half]

                def table(c):
                    t = k[:, c:c + NT * half].rearrange("p (i o d) -> p i o d", i=NT, o=1)
                    return t.broadcast_to([P, NT, heads, half])

                t = [ropet[:, n, :, 0:heads, 0:half] for n in range(4)]
                nc.gpsimd.tensor_tensor(t[0], x1, table(cos_at), ALU.mult)
                nc.gpsimd.tensor_tensor(t[1], x2, table(sin_at), ALU.mult)
                nc.gpsimd.tensor_tensor(t[2], x2, table(cos_at), ALU.mult)
                step(nc.gpsimd.tensor_tensor(t[3], x1, table(sin_at), ALU.mult))
                nc.gpsimd.tensor_tensor(x1, t[0], t[1], ALU.subtract)
                ins = nc.gpsimd.tensor_tensor(x2, t[2], t[3], ALU.add)
                step(ins) if last is None else ins.then_inc(last, 1)

            for m in range(3):
                low_part(m)
            pool.wait_ge(s_in, 16 * 8)
            pool.wait_ge(s_natd, IDX_DONE)
            nc.gpsimd.tensor_scalar(iwS[:, :, :], nat[:, :, IW0:IW0 + IH], (IH ** -0.5) * (IDIM ** -0.5), None,
                                    ALU.mult).then_inc(s_iw, 1)
            rope(IQ0, IH, IDIM, ROT_I, K_COSI, K_SINI, None)
            low_part(3)
            pool.wait_ge(s_ln, 1)
            rope(IK0, 1, IDIM, ROT_I, K_COSI, K_SINI, s_rope)
            for m in range(4, 7):
                low_part(m)
            pool.wait_ge(s_natd, first[5])
            rope(AK0, 1, DH, ROT_A, K_COSA, K_SINA, None)
            rope(AQ0, HEADS, DH, ROT_A, K_COSA, K_SINA, None)
            pool.wait_ge(s_bias, 48)
            for m in range(7, len(ITEMS)):
                low_part(m)
                if m - 7 < len(LAST_ROW):
                    pool.wait_ge(s_scaled, m - 6)
                    slot = place[LAST_ROW[m - 7]] % SLOTS
                    for c in range(2):
                        ins = nc.gpsimd.tensor_tensor(rows[:, 3, :], rows[:, 3, :], stage[:, slot, c * D:(c + 1) * D], ALU.add)
                        if c == 0:
                            step(ins)
                        else:
                            ins.then_inc(s_last_used, 1)
                    pool.wait_ge(s_last_used, m - 6)

        @block.scalar
        def _(act):
            step = Chain(act, ach)
            act.dma_start(k[:, :], A["consts"]).then_inc(s_in, 16)
            act.dma_start(gpre[:, :], A["g_mix_pre"].rearrange("a (p c) -> (a p) c", c=KC)).then_inc(s_in, 16)
            act.dma_start(bcol[:, :, :], A["b_ada"][0, 0:2 * D].rearrange("(s p c) -> p s c", s=2, c=KC)).then_inc(s_in, 16)
            act.dma_start(colrows[0:32, :], A["conv_w"][0].rearrange("j (n p) -> (j n) p", p=P)).then_inc(s_in, 16)
            act.dma_start(colrows[32:40, :], A["conv_b"][0].rearrange("(n p) -> n p", p=P)).then_inc(s_in, 16)
            act.dma_start(colrows[40:44, :], A["g_mlstm_head"][0].rearrange("(n p) -> n p", p=P)).then_inc(s_in, 16)
            act.dma_start(gik[:, :], A["g_idx_k"].broadcast_to([P, IDIM])).then_inc(s_in, 16)
            act.dma_start(bik[:, :], A["b_idx_k"].broadcast_to([P, IDIM])).then_inc(s_in, 16)
            act.dma_start(G.gb[:, 0:1], A["b_igate"].rearrange("a h -> h a")).then_inc(s_bias, 16)
            act.dma_start(G.gb[:, 1:2], A["b_fgate"].rearrange("a h -> h a")).then_inc(s_bias, 16)
            act.wait_ge(s_zero, 1)
            act.dma_start(rows[0:1, :, :], A["b_ada"][:, 2 * D:6 * D].rearrange("a (s d) -> a s d", s=4)).then_inc(s_bias, 16)
            act.wait_ge(s_c, 16)
            nc.scalar.activation(cs[:, :], cT[:, :], ACT.Silu).then_inc(s_silu, 1)
            act.wait_ge(s_x, 16)
            for i in range(NT):
                nc.scalar.activation(xn[:, i, :], x_in[:, i, :], ACT.Square, accum_out=ss[:, i:i + 1]).then_inc(s_ssq, 1)
            act.wait_ge(s_ms, 1)
            step(nc.scalar.activation(rs[:, 0:NT], ss[:, NT:2 * NT], ACT.Sqrt))
            nc.scalar.activation(rs[:, NT:2 * NT], rs[:, 0:NT], ACT.Copy).then_inc(s_rt, 1)
            act.wait_ge(s_xn, 1)
            for i in range(NT):
                nc.scalar.activation(xn[:, i, :], x_in[:, i, :], ACT.Copy, scale=rs[:, i:i + 1]).then_inc(s_xn, 1)

            def high_part(m):
                n = KC * width(ITEMS[m])
                slot = arrived(act, ITEMS[m])
                if m >= 2:
                    act.wait_ge(s_nat, first[m - 1])
                nc.scalar.activation(whi[:, m % 2, 0:n], stage[:, slot, 0:n], ACT.Copy).then_inc(s_whi, 1)

            high_part(0)
            act.wait_ge(s_modd, 1)
            for c in range(KC):
                act.wait_ge(s_xT, c + 1)
                nc.scalar.activation(hf[:, c, :], ps[:, c, :], ACT.Identity, bias=modB[:, c:c + 1],
                                     scale=modA[:, c:c + 1]).then_inc(s_hf, 1)
            high_part(1)

            def copy_nat(m):
                c0, w = NAT_PIECES[ITEMS[m][1]]
                for i in range(NT):
                    n = first[m] + i
                    act.wait_ge(s_nat, n + 1)
                    nc.scalar.activation(nat[:, i, c0:c0 + w], ps[:, n % 4, 0:w], ACT.Copy).then_inc(s_natd, 1)

            copy_nat(0)
            high_part(2)
            copy_nat(1)
            high_part(3)
            act.wait_ge(s_lnv, 1)
            nc.scalar.activation(rs[:, NT:2 * NT], ss[:, 2 * NT:3 * NT], ACT.Sqrt).then_inc(s_lnr, 1)
            copy_nat(2)
            for t in range(NT):
                act.wait_ge(s_iT, t + 1)
                nc.scalar.activation(iqT[:, :, t * P:(t + 1) * P],
                                     ps[0:IDIM, 4 + t % 2, :].rearrange("p (h t) -> p h t", h=IH), ACT.Copy).then_inc(s_iTd, 1)
            act.wait_ge(s_iT, NT + 1)
            nc.scalar.activation(ikT[:, :], ps[0:IDIM, 6, :], ACT.Copy).then_inc(s_iTd, 1)
            high_part(4)
            for i in range(1, NT):
                for h in range(IH):
                    u = (i - 1) * IH + h
                    act.wait_ge(s_rel, u + 1)
                    if u >= 2:
                        act.wait_ge(s_sc, u - 1)
                    w = P * (i + 1)
                    nc.scalar.activation(relu[:, u % 2, 0:w], ps[:, 4 + u % 4, 0:w], ACT.Relu).then_inc(s_relu, 1)
            copy_nat(3)
            high_part(5)
            copy_nat(4)
            high_part(6)

            def silu_qk(c):
                act.wait_ge(s_conv, c + 1)
                nc.scalar.activation(qkc[:, c, :], tmp[:, c % 2, :], ACT.Silu,
                                     bias=cols[:, 32 + c:33 + c]).then_inc(s_qk, 1)

            def first_tap(c):
                act.wait_ge(s_natd, QK_FIRST + c + 1)
                if c >= 2:
                    act.wait_ge(s_qk, c - 1)
                nc.scalar.activation(tmp[:, c % 2, :], raw[:, c % 4, 0:SEQ], ACT.Copy, scale=cols[:, c:c + 1]).then_inc(s_tap, 1)

            act.wait_ge(s_zero, 2)
            act.wait_ge(s_colsd, 1)
            act.wait_ge(s_sc, (NT - 1) * IH)
            for c in range(2 * HEADS):
                n = QK_FIRST + c
                act.wait_ge(s_nat, n + 1)
                if c >= 4:
                    act.wait_ge(s_conv, c - 3)
                nc.scalar.activation(raw[:, c % 4, CONV - 1:], ps[:, n % 4, :], ACT.Copy).then_inc(s_natd, 1)
                if c < 2:
                    first_tap(c)
                if c % 2:
                    high_part(7 + c // 2)
                    q = c // 2
                    slot = arrived(act, LAST_ROW[q])
                    for b in range(2):
                        w = stage[:, slot, b * D:(b + 1) * D]
                        ins = nc.scalar.activation(w, w, ACT.Copy, scale=cs[:, 2 * q + b:2 * q + b + 1])
                    ins.then_inc(s_scaled, 1)
                if c >= 4:
                    silu_qk(c - 4)
                    first_tap(c - 2)
            copy_nat(9)
            high_part(11)
            for c in range(4, 6):
                silu_qk(c)
                first_tap(c + 2)
            silu_qk(6)
            copy_nat(10)
            silu_qk(7)
            copy_nat(11)
            act.wait_ge(s_natd, n_out)

        @block.vector
        def _(dve):
            step = Chain(dve, dch)

            def modulation(piece, dst, s_done, n):
                _, s, q = piece
                slot = arrived(dve, piece)
                for c in range(2):
                    w, by = stage[:, slot, c * D:(c + 1) * D], cs[:, 2 * q + c:2 * q + c + 1]
                    if piece == ("ada", s, 0) and c == 0:
                        ins = nc.vector.tensor_scalar(dst, w, by, None, ALU.mult)
                    else:
                        ins = nc.vector.scalar_tensor_tensor(dst, w, by, dst, ALU.mult, ALU.add)
                    if c == 0:
                        step(ins)
                    else:
                        ins.then_inc(s_done, 1)
                dve.wait_ge(s_done, n + 1)

            dve.wait_ge(s_silu, 1)
            for n, piece in enumerate(ADA):
                modulation(piece, acc[:, piece[1], :], s_ada_used, n)
                if n == 3:
                    dve.wait_ge(s_cols, 1)
                    nc.vector.tensor_copy(cols[:, 0:44], ps[:, 6, 0:44]).then_inc(s_colsd, 1)
                    dve.wait_ge(s_ssq, NT)
                    nc.vector.tensor_scalar(ss[:, NT:2 * NT], ss[:, 0:NT], 1.0 / D, EPS, ALU.mult, ALU.add).then_inc(s_ms, 1)
                    dve.wait_ge(s_rt, 1)
                    nc.vector.reciprocal(rs[:, 0:NT], rs[:, NT:2 * NT]).then_inc(s_xn, 1)
            dve.wait_ge(s_mod, 1)
            step(nc.vector.tensor_tensor(modB[:, :], ps[:, 7, 0:KC], bcol[:, 0, :], ALU.add))
            step(nc.vector.scalar_tensor_tensor(modA[:, :], ps[:, 7, KC:2 * KC], 1.0, bcol[:, 1, :], ALU.add, ALU.add))
            nc.vector.tensor_tensor(modA[:, :], modA[:, :], gpre[:, :], ALU.mult).then_inc(s_modd, 1)
            for c in range(KC):
                dve.wait_ge(s_hf, c + 1)
                nc.vector.tensor_copy(hhi[:, c, :], hf[:, c, :]).then_inc(s_hhi, 1)
            for c in range(KC):
                dve.wait_ge(s_hhi, c + 1)
                nc.vector.tensor_tensor(hlo[:, c, :], hf[:, c, :], hhi[:, c, :].bitcast(F32), ALU.subtract).then_inc(s_hlo, 1)
            dve.wait_ge(s_bias, 48)
            for n, piece in enumerate(ROWS[0:5]):
                modulation(piece, rows[:, piece[1] - 2, :], s_row_used, n)
            dve.wait_ge(s_natd, IDX_DONE)
            ik = nat[:, :, IK0:IK0 + IDIM]
            mean = rs[:, 3 * NT:4 * NT]

            def wide(ap):
                return ap.rearrange("p (i o) -> p i o", o=1).broadcast_to([P, NT, IDIM])

            step(nc.vector.tensor_reduce(mean, ik, AX.X, ALU.add))
            step(nc.vector.tensor_scalar(mean, mean, 1.0 / IDIM, None, ALU.mult))
            step(nc.vector.tensor_tensor(lnb[:, :, :], ik, wide(mean), ALU.subtract))
            sq = work[:, 0:NT * IDIM].rearrange("p (i d) -> p i d", i=NT)
            step(nc.vector.tensor_tensor(sq, lnb[:, :, :], lnb[:, :, :], ALU.mult))
            step(nc.vector.tensor_reduce(ss[:, 3 * NT:4 * NT], sq, AX.X, ALU.add))
            nc.vector.tensor_scalar(ss[:, 2 * NT:3 * NT], ss[:, 3 * NT:4 * NT], 1.0 / IDIM, EPS, ALU.mult, ALU.add).then_inc(s_lnv, 1)
            dve.wait_ge(s_lnr, 1)
            step(nc.vector.reciprocal(rs[:, 2 * NT:3 * NT], rs[:, NT:2 * NT]))
            step(nc.vector.tensor_tensor(lnb[:, :, :], lnb[:, :, :], wide(rs[:, 2 * NT:3 * NT]), ALU.mult))
            gk = gik[:, :].rearrange("p (o d) -> p o d", o=1).broadcast_to([P, NT, IDIM])
            bk = bik[:, :].rearrange("p (o d) -> p o d", o=1).broadcast_to([P, NT, IDIM])
            step(nc.vector.tensor_tensor(lnb[:, :, :], lnb[:, :, :], gk, ALU.mult))
            nc.vector.tensor_tensor(ik, lnb[:, :, :], bk, ALU.add).then_inc(s_ln, 1)

            for n, piece in enumerate(ROWS[5:7]):
                modulation(piece, rows[:, piece[1] - 2, :], s_row_used, 5 + n)

            dve.wait_ge(s_iw, 1)
            for i in range(1, NT):
                w = P * (i + 1)
                sc = maskb[:, i, 0:w]
                for h in range(IH):
                    u = (i - 1) * IH + h
                    dve.wait_ge(s_relu, u + 1)
                    if h:
                        dve.wait_ge(s_sc, u)
                        nc.vector.scalar_tensor_tensor(sc, relu[:, u % 2, 0:w], iwS[:, i, h:h + 1], sc,
                                                       ALU.mult, ALU.add).then_inc(s_sc, 1)
                    else:
                        nc.vector.tensor_scalar(sc, relu[:, u % 2, 0:w], iwS[:, i, h:h + 1], None, ALU.mult).then_inc(s_sc, 1)
            def conv(c):
                dve.wait_ge(s_tap, c + 1)
                o = tmp[:, c % 2, :]
                r = raw[:, c % 4, :]
                for j in range(1, CONV):
                    w = cols[:, 8 * j + c:8 * j + c + 1]
                    ins = nc.vector.scalar_tensor_tensor(o, r[:, j:j + SEQ], w, o, ALU.mult, ALU.add)
                    if j < CONV - 1:
                        step(ins)
                    else:
                        ins.then_inc(s_conv, 1)

            conv_at = {(2, 11): 0, (2, 15): 1, (3, 3): 2, (3, 5): 3, (3, 8): 4, (3, 10): 5, (3, 13): 6, (3, 15): 7}
            dve.wait_ge(s_sc, (NT - 1) * IH)
            for i in range(1, NT):
                w = P * (i + 1)
                sc, wk = maskb[:, i, 0:w], work[:, 0:w]
                if i >= 2:
                    modulation(ROWS[5 + i], rows[:, ROWS[5 + i][1] - 2, :], s_row_used, 5 + i)
                step(nc.vector.memset(sc[0:CHUNK, w - CHUNK:w], FMASK))
                for r in range(TOPK // 8):
                    if (i, r) in conv_at:
                        conv(conv_at[i, r])
                    src = sc if r == 0 else wk
                    step(nc.vector.max(top8[:, :], src))
                    step(nc.vector.match_replace(wk, top8[:, :], src, FMIN))
                step(nc.vector.tensor_tensor(wk, wk, sc, ALU.is_equal))
                step(nc.vector.tensor_scalar(sc, wk, NEG, None, ALU.mult))
            nc.vector.tensor_copy(maskb[:, 0, 0:P], k[:, K_CAUSAL:K_CAUSAL + P])
            for n, piece in enumerate(ROWS[9:12]):
                modulation(piece, rows[:, piece[1] - 2, :], s_row_used, 9 + n)


        @block.tensor
        def _(pe):
            pe.wait_ge(s_in, 16 * 8)
            nc.tensor.transpose(ps[:, 6, 0:44], colrows[:, :], ident[0:44, 0:44]).then_inc(s_cols, 1)

            def sum_modulation(s):
                for c in range(KC):
                    ins = nc.tensor.matmul(ps[:, 7, s * KC + c:s * KC + c + 1], acc[:, s, c:D:KC], k[:, K_ONES:K_ONES + 1],
                                           start=True, stop=True)
                if s:
                    ins.then_inc(s_mod, 1)

            pe.wait_ge(s_ada_used, len(ADA) // 2)
            sum_modulation(0)
            pe.wait_ge(s_xn, NT + 1)
            pe.wait_ge(s_colsd, 1)
            for c in range(KC - 1):
                for i in range(NT):
                    ins = nc.tensor.transpose(ps[:, c, i * P:(i + 1) * P], xn[:, i, c:D:KC], ident)
                ins.then_inc(s_xT, 1)
            pe.wait_ge(s_ada_used, len(ADA))
            sum_modulation(1)
            pe.wait_ge(s_modd, 1)
            for i in range(NT):
                ins = nc.tensor.transpose(ps[:, KC - 1, i * P:(i + 1) * P], xn[:, i, KC - 1:D:KC], ident)
            ins.then_inc(s_xT, 1)
            PARTS = ((hhi, whi), (hlo, whi), (hhi, wlo))

            def project(m):
                kind, a, _ = ITEMS[m]
                w = width(ITEMS[m])
                pe.wait_ge(s_whi, m + 1)
                if m == 0:
                    for j, (hp, wp) in enumerate(PARTS):
                        wt = wp[:, 0, 0:KC * w].rearrange("p (c n) -> p c n", c=KC)
                        for i in range(NT):
                            for c in range(KC):
                                if i == 0:
                                    pe.wait_ge((s_hhi, s_hlo, s_wlo)[j], (c + 1, c + 1, 1)[j])
                                ins = nc.tensor.matmul(ps[:, i, 0:w], hp[:, c, i * P:(i + 1) * P], wt[:, c, :],
                                                       start=j == 0 and c == 0, stop=j == 2 and c == KC - 1)
                            if j == 2:
                                ins.then_inc(s_nat, 1)
                    return
                pe.wait_ge(s_wlo, m + 1)
                for i in range(NT if kind == "nat" else 2):
                    n = first[m] + i
                    if n >= 4:
                        pe.wait_ge(s_natd, n - 3)
                    for j, (hp, wp) in enumerate(PARTS):
                        wt = wp[:, m % 2, 0:KC * w].rearrange("p (c n) -> p c n", c=KC)
                        for c in range(KC):
                            lhsT = hp[:, c, i * P:(i + 1) * P] if kind == "nat" else wt[:, c, i * P:(i + 1) * P]
                            rhs = wt[:, c, :] if kind == "nat" else hp[:, c, :]
                            ins = nc.tensor.matmul(ps[:, n % 4, 0:w if kind == "nat" else SEQ], lhsT, rhs,
                                                   start=j == 0 and c == 0, stop=j == 2 and c == KC - 1)
                    ins.then_inc(s_nat, 1)

            pe.wait_ge(s_hf, KC)
            project(0)
            project(1)
            project(2)
            pe.wait_ge(s_rope, 1)
            for i in range(NT):
                if i >= 2:
                    pe.wait_ge(s_iTd, i - 1)
                for h in range(IH):
                    ins = nc.tensor.transpose(ps[0:IDIM, 4 + i % 2, h * P:(h + 1) * P],
                                              nat[:, i, IQ0 + h * IDIM:IQ0 + (h + 1) * IDIM], ident)
                ins.then_inc(s_iT, 1)
            for i in range(NT):
                ins = nc.tensor.transpose(ps[0:IDIM, 6, i * P:(i + 1) * P], nat[:, i, IK0:IK0 + IDIM], ident)
            ins.then_inc(s_iT, 1)
            pe.wait_ge(s_iTd, NT + 1)
            for i in range(1, NT):
                for h in range(IH):
                    u = (i - 1) * IH + h
                    if u >= 4:
                        pe.wait_ge(s_relu, u - 3)
                    nc.tensor.matmul(ps[:, 4 + u % 4, 0:P * (i + 1)], iqT[:, h, i * P:(i + 1) * P], ikT[:, 0:P * (i + 1)],
                                     start=True, stop=True).then_inc(s_rel, 1)
            for m in range(3, len(ITEMS)):
                project(m)


def stage_attention(nc, A, G):
    with ExitStack() as own:
        def sb(name, shape, dt=F32):
            return own.enter_context(nc.sbuf_tensor(name, shape, dt))

        G.last_used, G.used, held = G.used, [], G.held[1]

        def sem(name):
            G.used.append(held.enter_context(nc.semaphore("att_" + name)))
            return G.used[-1]

        k, nat, qkc, rows, maskb, cols, ps = G.k, G.nat, G.qkc, G.rows, G.maskb, G.cols, G.ps
        catT, wout, arena = G.catT, G.wout, G.arena
        ident = k[:, K_ID:K_ID + P]
        TRI = [0, 512, 896, 1152]
        TRI_W = 1280
        stT = arena[:, 0:2 * TRI_W].rearrange("p (b n) -> p b n", b=2)
        dm = arena[:, 2 * TRI_W:4 * TRI_W].rearrange("p (b n) -> p b n", b=2)
        md = arena[:, 4 * TRI_W:4 * TRI_W + 8 * P].rearrange("p (b n) -> p b n", b=8)
        lg = arena[:, 2560:3584].rearrange("p (b n) -> p b n", b=2)
        pr = arena[:, 3584:5120].rearrange("p (b n) -> p b n", b=3)
        prT = arena[:, 5120:6144].rearrange("p (b n) -> p b n", b=2)
        vext = sb("vext", [P, NT, HEADS, DH + 1])
        hall = sb("hall", [P, NT, HEADS * DH])
        gains = G.xt[:, 0:3, :]
        gb = G.gb
        ga = sb("gate_a", [HEADS, SEQ])
        gf = sb("gate_f", [HEADS, SEQ])
        gt = sb("gate_t", [HEADS, SEQ])
        aN = sb("gates_nat", [P, 2, NT, HEADS])
        den = sb("den", [P, NT])
        var = sb("var", [P, HEADS, NT])
        rstd = sb("rstd", [P, HEADS, NT])
        mx = sb("mx", [P, 2])
        nm = sb("nm", [P, 2])
        rsum = sb("rsum", [P, 2])
        rinv = sb("rinv", [P, 2])
        dinv = sb("rinv_diagonal", [P, 2, P])
        sqb = sb("sqb", [P, NT, DH])

        s_in = sem("small_in")
        dch, ach = sem("dve_chain"), sem("act_chain")
        s_gT = sem("gates_transposed")
        s_row = sem("row_broadcast")
        s_rowd = sem("row_ready")
        s_absf = sem("gate_abs")
        s_lse = sem("gate_log")
        s_em = sem("gate_m")
        s_emd = sem("gate_exp_m")
        s_an = sem("gates_back")
        s_and = sem("gates_nat_ready")
        s_bc = sem("negM_broadcast")
        s_md = sem("diag_masked")
        s_dm = sem("decay_ready")
        s_sT = sem("scores_T")
        s_sTd = sem("scores_T_weighted")
        s_num = sem("numerator")
        s_numd = sem("numerator_read")
        s_sig = sem("out_gate")
        s_vext = sem("v_extended")
        s_vsq = sem("head_squares")
        s_hsq = sem("head_var")
        s_hrt = sem("head_root")
        s_hr = sem("head_rstd")
        s_hn = sem("head_normed")
        s_hT = sem("head_transposed")
        s_hTd = sem("head_T_copied")
        s_qT = sem("aq_transposed")
        s_qTd = sem("aq_T_copied")
        s_lg = sem("logits")
        s_lgd = sem("logits_masked")
        s_nm = sem("neg_max")
        s_ex = sem("exps")
        s_ri = sem("sum_inverse")
        s_pn = sem("inverse_on_diagonal")
        s_pT = sem("probs_transposed")
        s_pTd = sem("probs_T_copied")
        s_o = sem("attended")
        s_od = sem("attended_copied")
        UNITS = [(h, i) for h in range(HEADS) for i in range(NT)]
        SCALE = DH ** -0.5
        ROW_BANK = [7, 2, 3, 4, 5, 6, 7, 2]
        block = own.enter_context(nc.Block())

        @block.sync
        def _(sp):
            for n, name in enumerate(("g_mix_post", "g_ffn_pre", "g_ffn_post")):
                sp.dma_start(gains[:, n, :], A[name].broadcast_to([P, D])).then_inc(s_in, 16)
            sp.dma_start(wout[:, :, :], A["w_out"][0].rearrange("(f p) n -> p f n", p=P)).then_inc(G.s_wout, 16)

        @block.gpsimd
        def _(pool):
            nc.gpsimd.memset(vext[:, :, :, DH:DH + 1], 1.0)
            nc.gpsimd.tensor_copy(vext[:, :, :, 0:DH], nat[:, :, V0:V0 + 512].rearrange("p i (h d) -> p i h d", h=HEADS)).then_inc(s_vext, 1)
            for old in G.last_used:
                pool.sem_clear(old)

        @block.scalar
        def _(act):
            step = Chain(act, ach)
            for h in range(HEADS + 1):
                act.wait_ge(s_qT, h + 1)
                at = AQ0 + h * DH
                nc.scalar.activation(nat[:, :, at:at + DH], ps[:, 2 + h, :].rearrange("p (i t) -> p i t", i=NT),
                                     ACT.Copy).then_inc(s_qTd, 1)
            act.wait_ge(s_absf, 1)
            step(nc.scalar.activation(gt[:, :], gt[:, :], ACT.Exp, scale=-1.0))
            nc.scalar.activation(gt[:, :], gt[:, :], ACT.Ln, bias=1.0).then_inc(s_lse, 1)
            act.wait_ge(s_em, 1)
            nc.scalar.activation(gt[:, :], gt[:, :], ACT.Exp, scale=-1.0).then_inc(s_emd, 1)
            act.wait_ge(s_and, 1)

            def head_squares(h):
                act.wait_ge(s_numd, h + 1)
                if h:
                    act.wait_ge(s_vsq, h)
                for i in range(NT):
                    ins = nc.scalar.activation(sqb[:, i, :], hall[:, i, h * DH:(h + 1) * DH], ACT.Square,
                                               accum_out=var[:, h, i:i + 1])
                ins.then_inc(s_vsq, 1)

            for h in range(HEADS):
                if h >= 2:
                    act.wait_ge(s_sTd, NT * (h - 1))
                act.wait_ge(s_md, NT * (h + 1))
                for j in range(NT):
                    w = SEQ - P * j
                    bias = aN[:, 0, j, h:h + 1]
                    ins = nc.scalar.activation(dm[:, h % 2, TRI[j]:TRI[j] + P], md[:, NT * (h % 2) + j, :], ACT.Exp, bias=bias)
                    if w > P:
                        ins = nc.scalar.activation(dm[:, h % 2, TRI[j] + P:TRI[j] + w], ps[:, h % 2, P * (j + 1):SEQ],
                                                   ACT.Exp, bias=bias)
                    ins.then_inc(s_dm, 1)
                if h >= 2:
                    head_squares(h - 2)
            nc.scalar.activation(nat[:, :, O0:O0 + 512], nat[:, :, O0:O0 + 512], ACT.Sigmoid).then_inc(s_sig, 1)
            for h in range(2, HEADS):
                head_squares(h)
            act.wait_ge(s_hsq, 1)
            nc.scalar.activation(rstd[:, :, :], var[:, :, :], ACT.Sqrt).then_inc(s_hrt, 1)
            act.wait_ge(s_num, HEADS)

            def exp_unit(u):
                w = P * (UNITS[u][1] + 1)
                act.wait_ge(s_nm, u + 1)
                if u >= 3:
                    act.wait_ge(s_pT, u - 2)
                nc.scalar.activation(pr[:, u % 3, 0:w], lg[:, u % 2, 0:w], ACT.Exp, bias=nm[:, u % 2:u % 2 + 1], scale=SCALE,
                                     accum_out=rsum[:, u % 2:u % 2 + 1]).then_inc(s_ex, 1)

            def copy_pT(u):
                w = P * (UNITS[u][1] + 1)
                act.wait_ge(s_pT, u + 1)
                if u >= 2:
                    act.wait_ge(s_o, u - 1)
                nc.scalar.activation(prT[:, u % 2, 0:w], ps[:, 3 + u % 3, 0:w], ACT.Copy).then_inc(s_pTd, 1)

            for u in range(len(UNITS)):
                exp_unit(u)
                if u:
                    copy_pT(u - 1)
            copy_pT(len(UNITS) - 1)

        @block.vector
        def _(dve):
            step = Chain(dve, dch)
            dve.wait_ge(s_gT, 2)
            step(nc.vector.tensor_scalar(gf[:, :], ps[0:HEADS, 1, :], gb[:, 1:2], None, ALU.add))
            step(nc.vector.tensor_scalar(gt[:, :], gf[:, :], -1.0, None, ALU.mult))
            nc.vector.tensor_tensor(gt[:, :], gf[:, :], gt[:, :], ALU.max).then_inc(s_absf, 1)
            step(nc.vector.tensor_scalar(gf[:, :], gf[:, :], 0.0, None, ALU.min))
            step(nc.vector.tensor_scalar(ga[:, :], ps[0:HEADS, 0, :], gb[:, 0:1], None, ALU.add))

            def finish_rows(r0, r1):
                for r in range(r0, r1):
                    s, c = r // 2, slice(512 * (r % 2), 512 * (r % 2 + 1))
                    dve.wait_ge(s_row, r + 1)
                    src, dst = ps[:, ROW_BANK[r], :], rows[:, s, c]
                    if s == 1:
                        ins = nc.vector.tensor_copy(dst, src)
                    elif s == 2:
                        ins = nc.vector.scalar_tensor_tensor(dst, src, 1.0, gains[:, 1, c], ALU.add, ALU.mult)
                    else:
                        ins = nc.vector.tensor_tensor(dst, src, gains[:, 0 if s == 0 else 2, c], ALU.mult)
                    ins.then_inc(s_rowd, 1)

            dve.wait_ge(s_in, 16 * 3)
            finish_rows(0, 3)
            dve.wait_ge(s_lse, 1)
            step(nc.vector.tensor_tensor(gf[:, :], gf[:, :], gt[:, :], ALU.subtract))
            one = k[0:HEADS, K_ONES:K_ONES + 1].broadcast_to([HEADS, SEQ])
            step(nc.vector.tensor_tensor_scan(gt[:, :], one, gf[:, :], 0.0, ALU.mult, ALU.add))
            step(nc.vector.tensor_tensor(ga[:, :], ga[:, :], gt[:, :], ALU.subtract))
            step(nc.vector.tensor_tensor_scan(gf[:, :], one, ga[:, :], NEG, ALU.mult, ALU.max))
            nc.vector.tensor_tensor(gt[:, :], gt[:, :], gf[:, :], ALU.add).then_inc(s_em, 1)
            step(nc.vector.tensor_scalar(gf[:, :], gf[:, :], -1.0, None, ALU.mult))
            finish_rows(3, 4)
            dve.wait_ge(s_an, 1)
            nc.vector.tensor_copy(aN[:, :, :, :], ps[:, 0, 0:2 * NT * HEADS].rearrange("p (a i h) -> p a i h", a=2, i=NT)).then_inc(s_and, 1)

            def diagonals(h):
                dve.wait_ge(s_bc, h + 1)
                if h >= 2:
                    dve.wait_ge(s_dm, NT * (h - 1))
                for j in range(NT):
                    nc.vector.tensor_tensor(md[:, NT * (h % 2) + j, :], ps[:, h % 2, j * P:(j + 1) * P],
                                            k[:, K_TRI:K_TRI + P], ALU.add).then_inc(s_md, 1)

            def weigh(h):
                for j in range(NT):
                    u, w = NT * h + j, SEQ - P * j
                    dve.wait_ge(s_sT, u + 1)
                    dve.wait_ge(s_dm, u + 1)
                    if h >= 2:
                        dve.wait_ge(s_num, h - 1)
                    nc.vector.scalar_tensor_tensor(stT[:, h % 2, TRI[j]:TRI[j] + w], ps[:, 2 + u % 2, 0:w], SCALE,
                                                   dm[:, h % 2, TRI[j]:TRI[j] + w], ALU.mult, ALU.mult).then_inc(s_sTd, 1)

            def read_head(h):
                dve.wait_ge(s_num, h + 1)
                if h:
                    dve.wait_ge(s_numd, h)
                b = 4 + 2 * (h % 2)
                v = ps[:, b:b + 2, :].rearrange("p b (t n) -> p (b t) n", n=256)
                hv = hall[:, :, h * DH:(h + 1) * DH]
                dv = den[:, :].rearrange("p (i o) -> p i o", o=1)
                step(nc.vector.scalar_tensor_tensor(dv, v[:, :, DH:DH + 1], -1.0, aN[:, 1, :, h:h + 1], ALU.mult, ALU.max))
                step(nc.vector.tensor_tensor(dv, dv, v[:, :, DH:DH + 1], ALU.max))
                step(nc.vector.reciprocal(den[:, :], den[:, :]))
                nc.vector.tensor_tensor(hv, v[:, :, 0:DH], den[:, :].rearrange("p (i o) -> p i o", o=1).broadcast_to([P, NT, DH]),
                                        ALU.mult).then_inc(s_numd, 1)

            diagonals(0)
            finish_rows(4, 8)
            for h in range(HEADS):
                if h + 1 < HEADS:
                    diagonals(h + 1)
                weigh(h)
                if h:
                    read_head(h - 1)
            read_head(HEADS - 1)
            dve.wait_ge(s_vsq, HEADS)
            nc.vector.tensor_scalar(var[:, :, :], var[:, :, :], 1.0 / DH, EPS, ALU.mult, ALU.add).then_inc(s_hsq, 1)

            def norm_head(h):
                if h == 0:
                    dve.wait_ge(s_hrt, 1)
                    nc.vector.reciprocal(rstd[:, :, :], rstd[:, :, :]).then_inc(s_hr, 1)
                    dve.wait_ge(s_hr, 1)
                    dve.wait_ge(s_sig, 1)
                for i in range(NT):
                    c = slice(h * DH, (h + 1) * DH)
                    ins = nc.vector.scalar_tensor_tensor(hall[:, i, c], hall[:, i, c], rstd[:, h, i:i + 1],
                                                         nat[:, i, O0 + h * DH:O0 + (h + 1) * DH], ALU.mult, ALU.mult)
                ins.then_inc(s_hn, 1)

            def mask_unit(u):
                h, i = UNITS[u]
                w = P * (i + 1)
                dve.wait_ge(s_lg, u + 1)
                if u >= 2:
                    dve.wait_ge(s_ex, u - 1)
                nc.vector.tensor_tensor_reduce(out=lg[:, u % 2, 0:w], in0=ps[:, u % 3, 0:w], in1=maskb[:, i, 0:w], scale=1.0,
                                               scalar=FMIN, op0=ALU.add, op1=ALU.max,
                                               accum_out=mx[:, u % 2:u % 2 + 1]).then_inc(s_lgd, 1)
                dve.wait_ge(s_lgd, u + 1)
                nc.vector.tensor_scalar(nm[:, u % 2:u % 2 + 1], mx[:, u % 2:u % 2 + 1], -SCALE, None, ALU.mult).then_inc(s_nm, 1)

            def invert(u):
                dve.wait_ge(s_ex, u + 1)
                if u >= 2:
                    dve.wait_ge(s_pT, u - 1)
                nc.vector.reciprocal(rinv[:, u % 2:u % 2 + 1], rsum[:, u % 2:u % 2 + 1]).then_inc(s_ri, 1)
                dve.wait_ge(s_ri, u + 1)
                nc.vector.tensor_scalar(dinv[:, u % 2, :], ident, rinv[:, u % 2:u % 2 + 1], None, ALU.mult).then_inc(s_pn, 1)

            def copy_out(h):
                dve.wait_ge(s_o, NT * (h + 1))
                nc.vector.tensor_copy(catT[:, HEADS + h, :], ps[:, 6 + h % 2, :]).then_inc(s_od, 1)

            def copy_head(h):
                dve.wait_ge(s_hT, h + 1)
                nc.vector.tensor_scalar(catT[:, h, :], ps[:, 7, :], cols[:, 40 + h:41 + h], None, ALU.mult).then_inc(s_hTd, 1)

            for u in range(len(UNITS)):
                mask_unit(u)
                if 1 <= u <= HEADS:
                    norm_head(u - 1)
                if u:
                    invert(u - 1)
                if 3 <= u < HEADS + 3:
                    copy_head(u - 3)
                if u >= NT + 2 and (u - 2) % NT == 0:
                    copy_out((u - 2) // NT - 1)
            invert(len(UNITS) - 1)
            copy_out(HEADS - 1)

        @block.tensor
        def _(pe):
            for b, at in ((0, I0), (1, F0)):
                for i in range(NT):
                    ins = nc.tensor.transpose(ps[0:HEADS, b, i * P:(i + 1) * P], nat[:, i, at:at + HEADS], ident)
                ins.then_inc(s_gT, 1)
            for h in range(HEADS + 1):
                for i in range(NT):
                    at = AQ0 + h * DH
                    ins = nc.tensor.transpose(ps[:, 2 + h, i * P:(i + 1) * P], nat[:, i, at:at + DH], ident)
                ins.then_inc(s_qT, 1)

            def sum_rows(r0, r1):
                for r in range(r0, r1):
                    if r >= 6:
                        pe.wait_ge(s_rowd, r - 5)
                    elif ROW_BANK[r] < 7:
                        pe.wait_ge(s_qTd, ROW_BANK[r] - 1)
                    nc.tensor.matmul(ps[:, ROW_BANK[r], :], k[:, K_ONES:K_ONES + P], rows[:, r // 2, 512 * (r % 2):512 * (r % 2 + 1)],
                                     start=True, stop=True).then_inc(s_row, 1)

            sum_rows(0, 8)
            pe.wait_ge(s_emd, 1)
            for a, src in enumerate((ga, gt)):
                for i in range(NT):
                    at = (a * NT + i) * HEADS
                    ins = nc.tensor.transpose(ps[:, 0, at:at + HEADS], src[:, i * P:(i + 1) * P], ident[0:HEADS, 0:HEADS])
            ins.then_inc(s_an, 1)
            pe.wait_ge(s_and, 1)
            def broadcast(h):
                if h >= 2:
                    pe.wait_ge(s_dm, NT * (h - 1))
                nc.tensor.matmul(ps[:, h % 2, :], k[0:HEADS, K_SEL + h * P:K_SEL + (h + 1) * P], gf[:, :],
                                 start=True, stop=True).then_inc(s_bc, 1)

            def scores(h):
                if h == 0:
                    pe.wait_ge(s_rowd, 8)
                for j in range(NT):
                    u = NT * h + j
                    if u >= 2:
                        pe.wait_ge(s_sTd, u - 1)
                    nc.tensor.matmul(ps[:, 2 + u % 2, 0:SEQ - P * j], qkc[:, HEADS + h, j * P:(j + 1) * P], qkc[:, h, j * P:SEQ],
                                     start=True, stop=True).then_inc(s_sT, 1)

            def numerators(h):
                if h == 0:
                    pe.wait_ge(s_vext, 1)
                if h >= 2:
                    pe.wait_ge(s_numd, h - 1)
                pe.wait_ge(s_sTd, NT * (h + 1))
                for i in range(NT):
                    for j in range(i + 1):
                        ins = nc.tensor.matmul(ps[:, 4 + 2 * (h % 2) + i // 2, 256 * (i % 2):256 * (i % 2) + DH + 1],
                                               stT[:, h % 2, TRI[j] + P * (i - j):TRI[j] + P * (i - j + 1)], vext[:, j, h, :],
                                               start=j == 0, stop=j == i)
                ins.then_inc(s_num, 1)

            broadcast(0)
            for h in range(HEADS):
                if h + 1 < HEADS:
                    broadcast(h + 1)
                scores(h)
                if h:
                    numerators(h - 1)
            numerators(HEADS - 1)
            pe.wait_ge(s_dm, NT * HEADS)
            pe.wait_ge(s_sTd, NT * HEADS)

            def turn_head(h):
                pe.wait_ge(s_hn, h + 1)
                if h:
                    pe.wait_ge(s_hTd, h)
                for i in range(NT):
                    ins = nc.tensor.transpose(ps[:, 7, i * P:(i + 1) * P], hall[:, i, h * DH:(h + 1) * DH], ident)
                ins.then_inc(s_hT, 1)

            def logits(u):
                h, i = UNITS[u]
                if u >= 3:
                    pe.wait_ge(s_lgd, u - 2)
                nc.tensor.matmul(ps[:, u % 3, 0:P * (i + 1)].rearrange("p (j t) -> p j t", t=P), nat[:, i, AQ0 + h * DH:AQ0 + (h + 1) * DH],
                                 nat[:, 0:i + 1, AK0:AK0 + DH], start=True, stop=True).then_inc(s_lg, 1)

            def turn(u):
                h, i = UNITS[u]
                pe.wait_ge(s_pn, u + 1)
                if u >= 3:
                    pe.wait_ge(s_pTd, u - 2)
                for j in range(i + 1):
                    ins = nc.tensor.matmul(ps[:, 3 + u % 3, j * P:(j + 1) * P], pr[:, u % 3, j * P:(j + 1) * P], dinv[:, u % 2, :],
                                           start=True, stop=True)
                ins.then_inc(s_pT, 1)

            def attend(u):
                h, i = UNITS[u]
                pe.wait_ge(s_pTd, u + 1)
                if h == 1 and i == 0:
                    pe.wait_ge(s_hTd, HEADS)
                if h >= 2 and i == 0:
                    pe.wait_ge(s_od, h - 1)
                for j in range(i + 1):
                    ins = nc.tensor.matmul(ps[:, 6 + h % 2, i * P:(i + 1) * P], nat[:, j, AV0:AV0 + DH],
                                           prT[:, u % 2, j * P:(j + 1) * P], start=j == 0, stop=j == i)
                ins.then_inc(s_o, 1)

            logits(0)
            logits(1)
            pe.wait_ge(s_numd, HEADS)
            for u in range(len(UNITS)):
                if u + 2 < len(UNITS):
                    logits(u + 2)
                turn(u)
                if u:
                    attend(u - 1)
                if 1 <= u <= HEADS:
                    turn_head(u - 1)
            attend(len(UNITS) - 1)


def stage_route(nc, A, G):
    with ExitStack() as own:
        def sb(name, shape, dt=F32):
            return own.enter_context(nc.sbuf_tensor(name, shape, dt))

        G.last_used = G.used

        def sem(name):
            return own.enter_context(nc.semaphore("route_" + name))

        k, rows, xt, ps, catT, wout = G.k, G.rows, G.xt, G.ps, G.catT, G.wout
        posm, gt = G.posm, G.gt
        ident = k[:, K_ID:K_ID + P]
        ones = k[:, K_ONES:K_ONES + P]
        flat = G.nat[:, :, :].rearrange("p i n -> p (i n)")
        h2n = flat[:, 0:NT * D].rearrange("p (i d) -> p i d", i=NT)
        wg = flat[:, 4096:4096 + KC * DE].rearrange("p (c f) -> p c f", c=KC)
        wu = flat[:, 6144:6144 + KC * DE].rearrange("p (c f) -> p c f", c=KC)
        h2T = G.qkc
        wd = G.w_shared_down
        wr = G.arena[:, 2048:2048 + KC * E_N].rearrange("p (c e) -> p c e", c=KC)
        sg = G.arena[:, 2560:3584].rearrange("p (f t) -> p f t", f=FC)
        uT = G.u_shared
        tmp = G.arena[:, 4608:5632]
        br = sb("b_router", [P, E_N])
        ssq = sb("ssq", [P, NT, 4])
        ms = sb("ms", [P, NT, 2])
        rt = sb("rt", [P, NT, 2])
        sco = sb("scores", [P, NT, E_N])
        sel = sb("sel", [P, NT, E_N])
        top2 = sb("top2", [P, NT * E_GROUPS, 8])
        gs = sb("group_score", [P, NT, E_GROUPS])
        cmp1 = sb("cmp1", [P, NT, E_GROUPS, E_GROUPS])
        cmp2 = sb("cmp2", [P, NT, E_GROUPS, E_GROUPS])
        gm = sb("group_mask", [P, NT, E_GROUPS])
        t8 = sb("top8e", [P, NT, 8])
        em = sb("expert_mask", [P, NT, E_N])
        wk = sb("sel_left", [P, NT, E_N])
        gsum = sb("gate_sum", [P, NT])
        cnt = sb("counts", [P, 4, E_N])
        tab = sb("tab", [P, 4])
        diag = sb("diag", [P, 2, P])

        s_in = sem("in")
        s_wsh = sem("shared_weights")
        s_xin = sem("x_again")
        dch = sem("dve_chain")
        s_y = sem("y_projected")
        s_sq = sem("squares")
        s_ms = sem("mean_squares")
        s_rt = sem("roots")
        s_yr = sem("y_read")
        s_x2 = sem("x2_ready")
        s_h2 = sem("h2_ready")
        s_h2T = sem("h2_transposed")
        s_h2Td = sem("h2_T_copied")
        s_lg = sem("router_logits")
        s_sco = sem("scores_ready")
        s_gu = sem("shared_gate_up")
        s_sg = sem("shared_silu")
        s_u = sem("shared_u")
        s_em = sem("expert_mask_ready")
        s_pos = sem("positions")
        s_dg = sem("diagonals_ready")
        s_tab = sem("table_rows")
        s_hw = sem("h2_stored")
        s_init = sem("tables_cleared")
        s_tabd = sem("tables_ready")
        block = own.enter_context(nc.Block())

        @block.sync
        def _(sp):
            sp.dma_start(xt[:, :, :], A["x"][0].rearrange("(i p) d -> p i d", p=P)).then_inc(s_xin, 16)
            sp.dma_start(br[:, :], A["b_router"].broadcast_to([P, E_N])).then_inc(s_in, 16)
            sp.dma_start(wr, A["w_router"][0].rearrange("(p c) e -> p c e", c=KC)).then_inc(s_in, 16)
            sp.dma_start(wg, A["w_sh_gate"][0].rearrange("(p c) f -> p c f", c=KC)).then_inc(s_wsh, 16)
            sp.dma_start(wu, A["w_sh_up"][0].rearrange("(p c) f -> p c f", c=KC)).then_inc(s_wsh, 16)
            sp.dma_start(wd, A["w_sh_down"][0].rearrange("(f p) n -> p f n", p=P)).then_inc(s_wsh, 16)
            sp.wait_ge(s_y, NT)
            for e in range(2):
                for m, name in enumerate(("w_exp_gate", "w_exp_up")):
                    sp.dma_start(G.w_gate_up[e][:, m], A[name][0, e].rearrange("(p c) f -> p c f", c=KC)).then_inc(G.s_wgu[e], 16)
            sp.dma_start(G.w_down[0], A["w_exp_down"][0, 0].rearrange("(f p) n -> p f n", p=P)).then_inc(G.s_wd[0], 16)
            for i in range(NT):
                sp.wait_ge(s_h2, i + 1)
                sp.dma_start(G.h2_rows[i * P:(i + 1) * P, :], h2n[:, i, :]).then_inc(s_hw, 16)
            sp.wait_ge(s_hw, 16 * NT)
            sp.wait_ge(s_h2T, 2 * NT)
            for m, name in enumerate(("w_exp_gate", "w_exp_up")):
                sp.dma_start(G.w_gate_up[2][:, m], A[name][0, 2].rearrange("(p c) f -> p c f", c=KC)).then_inc(G.s_wgu[2], 16)

        @block.gpsimd
        def _(pool):
            nc.gpsimd.memset(posm[:, :], -1.0).then_inc(s_init, 1)
            nc.gpsimd.memset(gt[:, :, :, :], 0.0).then_inc(s_init, 1)
            for old in G.last_used:
                pool.sem_clear(old)

        @block.scalar
        def _(act):
            def squares(i, n):
                if n == 0:
                    act.wait_ge(s_y, i + 1)
                    if i:
                        act.wait_ge(s_h2, i)
                    src = ps[:, 2 * i:2 * i + 2, :]
                else:
                    act.wait_ge(s_x2, i + 1)
                    src = xt[:, i, :].rearrange("p (a b) -> p a b", a=2)
                nc.scalar.activation(tmp.rearrange("p (a b) -> p a b", a=2), src, ACT.Square,
                                     accum_out=ssq[:, i, n:n + 1]).then_inc(s_sq, 1)
                act.wait_ge(s_ms, 2 * i + n + 1)
                nc.scalar.activation(rt[:, i, n:n + 1], ms[:, i, n:n + 1], ACT.Sqrt).then_inc(s_rt, 1)

            def copy_h2T(i):
                act.wait_ge(s_h2T, 2 * i + 2)
                nc.scalar.activation(h2T[:, 4:8, i * P:(i + 1) * P], ps[:, 2 * i + 1, :].rearrange("p (c t) -> p c t", c=4),
                                     ACT.Copy).then_inc(s_h2Td, 1)

            for i in range(NT):
                squares(i, 0)
                if i:
                    copy_h2T(i - 1)
                squares(i, 1)
            copy_h2T(NT - 1)
            act.wait_ge(s_lg, 1)
            nc.scalar.activation(sco[:, :, :], ps[:, 4, 0:NT * E_N].rearrange("p (i e) -> p i e", i=NT), ACT.Sigmoid).then_inc(s_sco, 1)
            for f in range(FC):
                act.wait_ge(s_gu, f + 1)
                nc.scalar.activation(sg[:, f, :], ps[:, f, :], ACT.Silu).then_inc(s_sg, 1)

        @block.vector
        def _(dve):
            step = Chain(dve, dch)

            def root(i, n):
                dve.wait_ge(s_sq, 2 * i + n + 1)
                nc.vector.tensor_scalar(ms[:, i, n:n + 1], ssq[:, i, n:n + 1], 1.0 / D, EPS, ALU.mult, ALU.add).then_inc(s_ms, 1)
                dve.wait_ge(s_rt, 2 * i + n + 1)
                step(nc.vector.reciprocal(rt[:, i, n:n + 1], rt[:, i, n:n + 1]))

            dve.wait_ge(s_xin, 16)
            def copy_h2T(i):
                dve.wait_ge(s_h2T, 2 * i + 1)
                nc.vector.tensor_copy(h2T[:, 0:4, i * P:(i + 1) * P], ps[:, 2 * i, :].rearrange("p (c t) -> p c t", c=4)).then_inc(s_h2Td, 1)

            for i in range(NT):
                root(i, 0)
                nc.vector.scalar_tensor_tensor(tmp, ps[:, 2 * i:2 * i + 2, :].rearrange("p a b -> p (a b)"), rt[:, i, 0:1],
                                               rows[:, 0, :], ALU.mult, ALU.mult).then_inc(s_yr, 1)
                if i:
                    copy_h2T(i - 1)
                dve.wait_ge(s_yr, i + 1)
                nc.vector.tensor_tensor(xt[:, i, :], xt[:, i, :], tmp, ALU.add).then_inc(s_x2, 1)
                root(i, 1)
                step(nc.vector.scalar_tensor_tensor(h2n[:, i, :], xt[:, i, :], rt[:, i, 1:2], rows[:, 2, :], ALU.mult, ALU.mult))
                nc.vector.tensor_tensor(h2n[:, i, :], h2n[:, i, :], rows[:, 1, :], ALU.add).then_inc(s_h2, 1)
            copy_h2T(NT - 1)

            def bc(ap, shape):
                return ap.broadcast_to(shape)

            dve.wait_ge(s_in, 32)
            dve.wait_ge(s_sco, 1)
            step(nc.vector.tensor_tensor(sel[:, :, :], sco[:, :, :],
                                         bc(br[:, :].rearrange("p (o e) -> p o e", o=1), [P, NT, E_N]), ALU.add))
            for n in range(NT * E_GROUPS):
                i, g = n // E_GROUPS, n % E_GROUPS
                ins = nc.vector.max(top2[:, n, :], sel[:, i, g * E_PER:(g + 1) * E_PER])
            step(ins)
            step(nc.vector.tensor_tensor(gs[:, :, :].rearrange("p i g -> p (i g)").rearrange("p (n o) -> p n o", o=1),
                                         top2[:, :, 0:1], top2[:, :, 1:2], ALU.add))
            full = [P, NT, E_GROUPS, E_GROUPS]
            mine = bc(gs[:, :, :].rearrange("p i (g o) -> p i g o", o=1), full)
            other = bc(gs[:, :, :].rearrange("p i (o g) -> p i o g", o=1), full)
            nc.vector.tensor_tensor(cmp1[:, :, :, :], other, mine, ALU.is_gt)
            step(nc.vector.tensor_tensor(cmp2[:, :, :, :], other, mine, ALU.is_equal))
            for g in range(E_GROUPS):
                step(nc.vector.memset(cmp2[:, :, g, g:E_GROUPS], 0.0))
            step(nc.vector.tensor_tensor(cmp1[:, :, :, :], cmp1[:, :, :, :], cmp2[:, :, :, :], ALU.add))
            step(nc.vector.tensor_reduce(gm[:, :, :], cmp1[:, :, :, :], AX.X, ALU.add))
            step(nc.vector.tensor_scalar(gm[:, :, :], gm[:, :, :], float(E_TOPG), FMASK, ALU.is_ge, ALU.mult))
            step(nc.vector.tensor_tensor(
                sel[:, :, :].rearrange("p i (g m) -> p i g m", g=E_GROUPS), sel[:, :, :].rearrange("p i (g m) -> p i g m", g=E_GROUPS),
                bc(gm[:, :, :].rearrange("p i (g o) -> p i g o", o=1), [P, NT, E_GROUPS, E_PER]), ALU.add))
            for i in range(NT):
                ins = nc.vector.max(t8[:, i, :], sel[:, i, :])
            step(ins)
            for i in range(NT):
                ins = nc.vector.match_replace(wk[:, i, :], t8[:, i, :], sel[:, i, :], FMIN)
            step(ins)
            nc.vector.tensor_tensor(em[:, :, :], wk[:, :, :], sel[:, :, :], ALU.not_equal).then_inc(s_em, 1)
            dve.wait_ge(s_em, 1)
            step(nc.vector.tensor_tensor(wk[:, :, :], sco[:, :, :], em[:, :, :], ALU.mult))
            step(nc.vector.tensor_reduce(gsum[:, :], wk[:, :, :], AX.X, ALU.add))
            step(nc.vector.reciprocal(gsum[:, :], gsum[:, :]))
            dve.wait_ge(s_init, 2)
            gv = gt[:, :, :, :].rearrange("p e i t -> p i e t")
            for i in range(NT):
                ins = nc.vector.tensor_scalar(wk[:, i, :], wk[:, i, :], gsum[:, i:i + 1], ROUTE_SCALE, ALU.mult, ALU.mult)
            step(ins)
            for n, at in enumerate((K_TOKH, K_TOKL)):
                for i in range(NT):
                    nc.vector.tensor_copy(gv[:, i, :, n], bc(k[:, at + i:at + i + 1], [P, E_N]))
            for n in range(3):
                step(nc.vector.tensor_copy(gv[:, :, :, 3 + n], wk[:, :, :]))
                if n < 2:
                    step(nc.vector.tensor_tensor(wk[:, :, :], wk[:, :, :], gv[:, :, :, 3 + n], ALU.subtract))
            dve.wait_ge(s_pos, 1)
            pp = ps[:, 7, 0:NT * E_N].rearrange("p (i e) -> p i e", i=NT)
            step(nc.vector.scalar_tensor_tensor(wk[:, :, :], pp, 1.0, em[:, :, :], ALU.add, ALU.mult))
            nc.vector.tensor_scalar(posm[:, :].rearrange("p (e i) -> p i e", i=NT), wk[:, :, :], -1.0, None, ALU.add)
            n_e, k_e, cum, at = (cnt[:, n, :] for n in range(4))
            step(nc.vector.tensor_copy(n_e, ps[:, 7, NT * E_N:(NT + 1) * E_N]))
            nc.vector.tensor_copy(G.count_tab[:, :], n_e[0:1, :])
            step(nc.vector.tensor_scalar(k_e, n_e, float(CAP), None, ALU.is_gt))
            for m in range(2, STEPS + 1):
                step(nc.vector.scalar_tensor_tensor(k_e, n_e, float(m * CAP), k_e, ALU.is_gt, ALU.add))
            step(nc.vector.tensor_tensor_scan(cum, k[:, K_ONES:K_ONES + E_N], k_e, 0.0, ALU.mult, ALU.add))
            step(nc.vector.tensor_scalar(at, cum, k[:, K_PART:K_PART + 1], None, ALU.is_le))
            step(nc.vector.tensor_reduce(tab[:, 0:1], at, AX.X, ALU.add))
            step(nc.vector.tensor_tensor(at, at, k_e, ALU.mult))
            step(nc.vector.tensor_reduce(tab[:, 1:2], at, AX.X, ALU.add))
            step(nc.vector.tensor_tensor(tab[:, 2:3], k[:, K_PART:K_PART + 1], tab[:, 1:2], ALU.subtract))
            step(nc.vector.tensor_scalar(tab[:, 2:3], tab[:, 2:3], 1.0, float(CAP), ALU.add, ALU.mult))
            step(nc.vector.tensor_scalar(diag[:, 0, :], ident, tab[:, 0:1], None, ALU.mult))
            nc.vector.tensor_scalar(diag[:, 1, :], ident, tab[:, 2:3], None, ALU.mult).then_inc(s_dg, 1)
            for f in range(FC):
                dve.wait_ge(s_sg, f + 1)
                nc.vector.tensor_tensor(uT[:, f, :], sg[:, f, :], ps[:, 2 + f, :], ALU.mult).then_inc(s_u, 1)
            dve.wait_ge(s_tab, 1)
            step(nc.vector.tensor_copy(G.extra_base[:, :], ps[:, 6, P:2 * P]))
            step(nc.vector.tensor_copy(G.extra_tab[:, 0:P], ps[0:1, 6, 0:P]))
            nc.vector.tensor_copy(G.extra_tab[:, P:P + 1], cum[0:1, E_N - 1:E_N]).then_inc(s_tabd, 1)
            dve.wait_ge(s_tabd, 1)

        @block.tensor
        def _(pe):
            def project_out(i):
                for half in range(2):
                    for f in range(2 * HEADS):
                        ins = nc.tensor.matmul(ps[:, 2 * i + half, :], catT[:, f, i * P:(i + 1) * P],
                                               wout[:, f, 512 * half:512 * (half + 1)], start=f == 0, stop=f == 2 * HEADS - 1)
                ins.then_inc(s_y, 1)

            def turn(i):
                pe.wait_ge(s_h2, i + 1)
                for c in range(KC):
                    ins = nc.tensor.transpose(ps[:, 2 * i + c // 4, (c % 4) * P:(c % 4 + 1) * P], h2n[:, i, c:D:KC], ident)
                    if c % 4 == 3:
                        ins.then_inc(s_h2T, 1)

            def router(i):
                for c in range(KC):
                    ins = nc.tensor.matmul(ps[:, 4, i * E_N:(i + 1) * E_N], h2T[:, c, i * P:(i + 1) * P], wr[:, c, :],
                                           start=c == 0, stop=c == KC - 1)
                if i == NT - 1:
                    ins.then_inc(s_lg, 1)

            def shared(f, m, t0, t1):
                for c in range(KC):
                    ins = nc.tensor.matmul(ps[:, 2 * m + f, t0:t1], (wg, wu)[m][:, c, f * P:(f + 1) * P], h2T[:, c, t0:t1],
                                           start=c == 0, stop=c == KC - 1)
                if m == 1 and t1 == SEQ:
                    ins.then_inc(s_gu, 1)

            pe.wait_ge(G.s_wout, 16)
            project_out(0)
            for i in range(1, NT):
                project_out(i)
                turn(i - 1)
            pe.wait_ge(s_h2Td, 2 * (NT - 1))
            pe.wait_ge(s_in, 32)
            pe.wait_ge(s_wsh, 48)
            for i in range(NT - 1):
                router(i)
            for m in range(2):
                shared(0, m, 0, (NT - 1) * P)
            turn(NT - 1)
            pe.wait_ge(s_h2Td, 2 * NT)
            router(NT - 1)
            def places():
                pe.wait_ge(s_em, 1)
                for i in range(NT):
                    dst = ps[:, 7, i * E_N:(i + 1) * E_N]
                    for n in range(i):
                        nc.tensor.matmul(dst, ones, em[:, n, :], start=n == 0, stop=False)
                    nc.tensor.matmul(dst, k[:, K_STRICT:K_STRICT + P], em[:, i, :], start=i == 0, stop=True)
                for n in range(NT):
                    ins = nc.tensor.matmul(ps[:, 7, NT * E_N:(NT + 1) * E_N], ones, em[:, n, :], start=n == 0, stop=n == NT - 1)
                ins.then_inc(s_pos, 1)

            for m in range(2):
                shared(0, m, (NT - 1) * P, SEQ)
            shared(1, 0, 0, SEQ)
            places()
            shared(1, 1, 0, SEQ)
            pe.wait_ge(s_dg, 1)
            for n in range(2):
                ins = nc.tensor.matmul(ps[:, 6, n * P:(n + 1) * P], ones, diag[:, n, :], start=True, stop=True)
            ins.then_inc(s_tab, 1)


RING = 4
HALF = KC // 2


def stage_experts(nc, A, G):
    with ExitStack() as own:
        def sb(name, shape, dt=F32):
            return own.enter_context(nc.sbuf_tensor(name, shape, dt))

        def sem(name):
            return own.enter_context(nc.semaphore(name))

        k, ps, posm, gt = G.k, G.ps, G.posm, G.gt
        ident = k[:, K_ID:K_ID + P]
        wgu, wd = G.w_gate_up, G.w_down
        whi = sb("w_gate_up_hi", [P, 2, HALF, 2, DE], FR)
        wlo = sb("w_gate_up_lo", [P, 2, HALF, 2, DE], FR)
        xhi = sb("xT_hi", [P, KC, CAP], FR)
        xlo = sb("xT_lo", [P, KC, CAP], FR)
        pick = sb("pick", [P, 2, NT, CAP], BF16)
        found = sb("found", [CAP, RING, 2])
        sidx = sb("row_numbers", [CAP, RING], I32)
        sidx2 = sb("scatter_rows", [CAP, 2], I32)
        pad = sb("pad", [CAP, 2])
        xg = sb("xg", [CAP, 2, D])
        sg = sb("sg", [CAP, DE])
        u = sb("u", [CAP, DE])
        uT = sb("uT", [P, 2, FC, CAP])
        yb = sb("yb", [CAP, 2, D])

        ysh = [G.rows[:, 1, :], G.rows[:, 2, :], G.qkc[:, 4:6, :].rearrange("p c t -> p (c t)"),
               G.qkc[:, 6:8, :].rearrange("p c t -> p (c t)")]
        w_gate, w_up, w_down = A["w_exp_gate"][0], A["w_exp_up"][0], A["w_exp_down"][0]

        def load_gate_up(eng, e, slot, s_wgu):
            eng.dma_start(wgu[slot][:, 0], w_gate[e].rearrange("(p c) f -> p c f", c=KC)).then_inc(s_wgu, 16)
            eng.dma_start(wgu[slot][:, 1], w_up[e].rearrange("(p c) f -> p c f", c=KC)).then_inc(s_wgu, 16)

        def load_down(eng, e, slot, s_wd):
            eng.dma_start(wd[slot], w_down[e].rearrange("(f p) n -> p f n", p=P)).then_inc(s_wd, 16)

        def pick_rows(q, n, bank):
            q(nc.vector.tensor_reduce(found[:, n, :], ps[0:CAP, bank, 0:6].rearrange("p (a b) -> p a b", a=2), AX.X, ALU.add))
            f = found[:, n, 0:1]
            q(nc.vector.tensor_scalar(pad[:, 0:1], f, 0.0, k[0:CAP, K_PADROW:K_PADROW + 1], ALU.is_equal, ALU.mult))
            return nc.vector.scalar_tensor_tensor(sidx[:, n:n + 1], f, -1.0, pad[:, 0:1], ALU.add, ALU.add)

        def gather_rows(pool, slot, n, rows=CAP):
            return pool.indirect_dma_start(out=xg[0:rows, slot, :], out_offset=None, in_=G.h2_rows,
                                           in_offset=bass.IndirectOffsetOnAxis(ap=sidx[0:rows, n:n + 1], axis=0),
                                           bounds_check=SEQ - 1, oob_is_err=False)

        def add_rows(pool, slot, rows=CAP):
            return pool.indirect_dma_start(out=G.y_rows, out_offset=bass.IndirectOffsetOnAxis(ap=sidx2[0:rows, slot:slot + 1], axis=0),
                                           in_=yb[0:rows, slot, :], in_offset=None, compute_op=ALU.add)

        with ExitStack() as inner:
            def isem(name):
                return inner.enter_context(nc.semaphore(name))

            s_wgu, s_wd = G.s_wgu, G.s_wd
            dch = isem("dve_chain")
            s_pick = isem("pick_built")
            s_find = isem("rows_found")
            s_idx = isem("row_numbers")
            s_sidx = isem("scatter_rows_kept")
            s_g = [isem(f"gathered{n}") for n in range(2)]
            s_xp = isem("x_transposed")
            s_xhi = isem("x_high_parts")
            s_xlo = isem("x_low_parts")
            s_whi = isem("w_high_half")
            s_wlo = isem("w_low_half")
            s_gu = isem("gate_up_half_done")
            s_sg = isem("silu_done")
            s_u = isem("u_ready")
            s_ut = isem("u_transposed")
            s_uTd = isem("uT_copied")
            s_dn = isem("down_done")
            s_ya = isem("y_low_ready")
            s_yd = isem("y_high_ready")
            s_sc = isem("scattered")
            s_passed = isem("pool_waits_passed")
            s_zero = isem("xg_zero")
            s_sdn = isem("shared_down_done")
            s_sdc = isem("shared_copied")
            s_yw = isem("shared_stored")
            TURNS = E_N // RING
            block = inner.enter_context(nc.Block())

            def turns(eng, step):
                with eng.Fori(0, TURNS - 1) as t:
                    for n in range(RING):
                        step(t, n, lambda m: True)
                for n in range(RING):
                    step(TURNS - 1, n, lambda m, n=n: n + m < RING)

            @block.sync
            def _(sp):
                load_down(sp, 1, 1, s_wd[1])
                load_gate_up(sp, 3, 3, s_wgu[3])

                def step(t, n, ahead):
                    e = RING * t + n
                    if ahead(RING):
                        sp.wait_ge(s_wlo, 2 * e + 2)
                        load_gate_up(sp, RING * t + (n + RING), n, s_wgu[n])
                    if ahead(2):
                        sp.wait_ge(s_dn, e + 1)
                        load_down(sp, RING * t + (n + 2), n % 2, s_wd[n % 2])

                turns(sp, step)

            @block.gpsimd
            def _(pool):
                nc.gpsimd.memset(xg[:, :, :], 0.0).then_inc(s_zero, 1)
                for n in range(2):
                    pool.dma_start(G.y_rows[SEQ + n * 64:SEQ + (n + 1) * 64, :], G.xt[0:64, 0, :]).then_inc(s_sc, 16)
                pool.wait_ge(s_zero, 1)
                for n in range(3):
                    pool.wait_ge(s_idx, n + 1)
                    if n == 2:
                        pool.wait_ge(s_xp, 1)
                    gather_rows(pool, n % 2, n).then_inc(s_g[n % 2], 16)
                pool.wait_ge(s_yw, 16 * NT)

                def by_size(count, sizes, move):
                    if len(sizes) == 1:
                        move(sizes[0])
                        return
                    half = len(sizes) // 2
                    with pool.If(count > sizes[half - 1]):
                        by_size(count, sizes[half:], move)
                    with pool.Else():
                        by_size(count, sizes[:half], move)

                def count_of(e):
                    return pool.value_load(G.count_tab[0:1, bass.ds(e, 1)], min_val=0, max_val=SEQ)

                def step(t, n, ahead):
                    e = RING * t + n
                    if ahead(3):
                        pool.wait_ge(s_idx, e + 4)
                        pool.wait_ge(s_xp, e + 2)
                        pool.sem_inc(s_passed, 1)
                        count = count_of(e + 3)
                        by_size(count, SIZES, lambda rows: gather_rows(pool, (n + 3) % 2, (n + 3) % RING, rows).then_inc(s_g[(n + 3) % 2], 16))
                    pool.wait_ge(s_ya, e + 2)
                    pool.wait_ge(s_yd, e + 2)
                    pool.wait_ge(s_sidx, e + 2)
                    pool.wait_ge(s_sc, 16 * e + 32)
                    pool.sem_inc(s_passed, 1)
                    count = count_of(e)
                    by_size(count, SIZES, lambda rows: add_rows(pool, n % 2, rows).then_inc(s_sc, 16))

                turns(pool, step)
                pool.wait_ge(s_sc, 16 * E_N + 32)

            @block.scalar
            def _(act):
                def high_half(t, n, half):
                    if half == 0:
                        act.wait_ge(s_wgu[n % RING], 32 * (t + n // RING) + 32)
                    if not (isinstance(t, int) and t == 0 and n == 0):
                        act.wait_ge(s_gu, 2 * (RING * t + n) + (half - 1))
                    nc.scalar.activation(whi[:, half], wgu[n % RING][:, :, HALF * half:HALF * (half + 1), :]
                                         .rearrange("p m c f -> p c m f"), ACT.Copy).then_inc(s_whi, 1)

                def x_high(t, n):
                    e = RING * t + n
                    act.wait_ge(s_xp, e + 1)
                    if not (isinstance(t, int) and t == 0 and n == 0):
                        act.wait_ge(s_gu, 2 * e)
                    nc.scalar.activation(xhi[:, :, :], ps[:, 0:2, :].rearrange("p b (c t) -> p (b c) t", t=P)[:, :, 0:CAP],
                                         ACT.Copy).then_inc(s_xhi, 1)

                def silu(t, n):
                    e = RING * t + n
                    act.wait_ge(s_gu, 2 * e + 2)
                    if not (isinstance(t, int) and t == 0 and n == 0):
                        act.wait_ge(s_u, e)
                    nc.scalar.activation(sg[:, :], ps[0:CAP, 2 + n % 2, 0:DE], ACT.Silu).then_inc(s_sg, 1)

                act.sem_inc(s_ya, 1)
                def store_shared(i):
                    act.wait_ge(s_sdn, i + 1)
                    nc.scalar.activation(ysh[i].rearrange("p (a b) -> p a b", a=2), ps[:, 4 + 2 * (i % 2):6 + 2 * (i % 2), :],
                                         ACT.Copy).then_inc(s_sdc, 1)
                    act.wait_ge(s_sdc, i + 1)
                    act.dma_start(G.y_rows[i * P:(i + 1) * P, :], ysh[i]).then_inc(s_yw, 16)

                high_half(0, 0, 0)
                high_half(0, 0, 1)
                store_shared(0)
                store_shared(1)
                store_shared(2)
                x_high(0, 0)
                store_shared(3)
                high_half(0, 1, 0)
                silu(0, 0)
                x_high(0, 1)
                high_half(0, 1, 1)

                def step(t, n, ahead):
                    e = RING * t + n
                    if ahead(2):
                        high_half(t, n + 2, 0)
                    if ahead(1):
                        silu(t, n + 1)
                    if ahead(2):
                        x_high(t, n + 2)
                        high_half(t, n + 2, 1)
                    act.wait_ge(s_dn, e + 1)
                    act.wait_ge(s_sc, 16 * e + 16)
                    nc.scalar.activation(yb[:, n % 2, 0:512], ps[0:CAP, 4, :], ACT.Copy,
                                         scale=found[:, n, 1:2]).then_inc(s_ya, 1)

                turns(act, step)

            @block.vector
            def _(dve):
                LINKS = 2
                count = [0]

                def build_pick(e, slot):
                    for i in range(NT):
                        ins = nc.vector.tensor_scalar(pick[:, slot, i, :], k[:, K_IOTA:K_IOTA + CAP],
                                                      posm[:, bass.ds(NT * e + i, 1)], None, ALU.is_equal)
                    ins.then_inc(s_pick, 1)

                def read_found(e, n):
                    count[0] = 0

                    def q(ins):
                        count[0] += 1
                        ins.then_inc(dch, 1)
                        dve.wait_ge(dch, LINKS * e + count[0])

                    dve.wait_ge(s_find, e + 1)
                    pick_rows(q, n, 6 + n % 2).then_inc(s_idx, 1)

                def low_half(t, n, half):
                    dve.wait_ge(s_whi, 2 * (RING * t + n) + (half + 1))
                    src = wgu[n % RING][:, :, HALF * half:HALF * (half + 1), :].rearrange("p m c f -> p c m f")
                    nc.vector.tensor_tensor(wlo[:, half], src, whi[:, half].bitcast(F32), ALU.subtract).then_inc(s_wlo, 1)

                def x_low(e):
                    dve.wait_ge(s_xhi, e + 1)
                    nc.vector.tensor_tensor(xlo[:, :, :], ps[:, 0:2, :].rearrange("p b (c t) -> p (b c) t", t=P)[:, :, 0:CAP],
                                            xhi[:, :, :].bitcast(F32), ALU.subtract).then_inc(s_xlo, 1)

                def multiply(e, slot):
                    dve.wait_ge(s_sg, e + 1)
                    nc.vector.tensor_tensor(u[:, :], sg[:, :], ps[0:CAP, 2 + slot, DE:2 * DE], ALU.mult).then_inc(s_u, 1)

                def copy_uT(e, slot):
                    dve.wait_ge(s_ut, e + 1)
                    nc.vector.tensor_copy(uT[:, slot], ps[:, 2 + slot, 0:FC * P].rearrange("p (f t) -> p f t", f=FC)[:, :, 0:CAP]
                                          ).then_inc(s_uTd, 1)

                dve.sem_inc(s_uTd, 1)
                dve.sem_inc(s_yd, 1)
                dve.sem_inc(s_sidx, 1)
                build_pick(0, 0)
                build_pick(1, 1)
                read_found(0, 0)
                read_found(1, 1)
                build_pick(2, 0)
                low_half(0, 0, 0)
                low_half(0, 0, 1)
                x_low(0)
                low_half(0, 1, 0)
                read_found(2, 2)
                multiply(0, 0)
                x_low(1)
                low_half(0, 1, 1)
                build_pick(3, 1)
                copy_uT(0, 0)

                def step(t, n, ahead):
                    e = RING * t + n
                    if ahead(2):
                        low_half(t, n + 2, 0)
                    if ahead(3):
                        dve.wait_ge(s_ya, e + 1)
                        dve.wait_ge(s_yd, e + 1)
                        dve.wait_ge(s_sidx, e + 1)
                        read_found(RING * t + (n + 3), (n + 3) % RING)
                    if ahead(1):
                        multiply(RING * t + (n + 1), (n + 1) % 2)
                    if ahead(2):
                        x_low(RING * t + (n + 2))
                        low_half(t, n + 2, 1)
                    if ahead(4):
                        build_pick(RING * t + (n + 4), n % 2)
                    dve.wait_ge(s_dn, e + 1)
                    dve.wait_ge(s_sc, 16 * e + 16)
                    nc.vector.tensor_copy(sidx2[:, n % 2:n % 2 + 1], sidx[:, n:n + 1]).then_inc(s_sidx, 1)
                    nc.vector.tensor_scalar(yb[:, n % 2, 512:D], ps[0:CAP, 5, :], found[:, n, 1:2], None, ALU.mult).then_inc(s_yd, 1)
                    if ahead(1):
                        copy_uT(RING * t + (n + 1), (n + 1) % 2)

                turns(dve, step)

            @block.tensor
            def _(pe):
                def find(e, slot):
                    pe.wait_ge(s_pick, e + 1)
                    for i in range(NT):
                        ins = nc.tensor.matmul(ps[0:CAP, 6 + slot, 0:6], pick[:, slot, i, :],
                                               gt[:, bass.ds(e, 1), i, :].rearrange("p o t -> p (o t)"), start=i == 0, stop=i == NT - 1)
                    ins.then_inc(s_find, 1)

                def transpose_x(t, n):
                    pe.wait_ge(s_g[n % 2], 16 * ((RING // 2) * t + (n // 2 + 1)))
                    for c in range(KC):
                        ins = nc.tensor.transpose(ps[:, c // 4, (c % 4) * P:(c % 4) * P + CAP], xg[:, n % 2, c:D:KC], ident[0:CAP, 0:CAP])
                    ins.then_inc(s_xp, 1)

                def gate_up(e, slot):
                    pe.wait_ge(s_xlo, e + 1)
                    for half in range(2):
                        pe.wait_ge(s_wlo, 2 * e + (half + 1))
                        for j, (xp, wp) in enumerate(((xhi, whi), (xlo, whi), (xhi, wlo))):
                            for c in range(HALF):
                                ins = nc.tensor.matmul(ps[0:CAP, 2 + slot, :], xp[:, HALF * half + c, :],
                                                       wp[:, half, c].rearrange("p m f -> p (m f)"),
                                                       start=half == 0 and j == 0 and c == 0, stop=half == 1 and j == 2 and c == HALF - 1)
                        ins.then_inc(s_gu, 1)

                def transpose_u(e, slot):
                    pe.wait_ge(s_u, e + 1)
                    for f in range(FC):
                        ins = nc.tensor.transpose(ps[:, 2 + slot, f * P:f * P + CAP], u[:, f * P:(f + 1) * P], ident[0:CAP, 0:CAP])
                    ins.then_inc(s_ut, 1)

                def shared_down(i):
                    if i >= 2:
                        pe.wait_ge(s_sdc, i - 1)
                    for half in range(2):
                        bank = 4 + 2 * (i % 2) + half
                        for f in range(FC):
                            ins = nc.tensor.matmul(ps[:, bank, :], G.u_shared[:, f, i * P:(i + 1) * P],
                                                   G.w_shared_down[:, f, 512 * half:512 * (half + 1)], start=f == 0, stop=f == FC - 1)
                    ins.then_inc(s_sdn, 1)

                find(0, 0)
                find(1, 1)
                shared_down(0)
                pe.wait_ge(s_idx, 2)
                shared_down(1)
                shared_down(2)
                transpose_x(0, 0)
                shared_down(3)
                gate_up(0, 0)
                pe.wait_ge(s_sdc, NT)
                find(2, 0)
                transpose_x(0, 1)
                transpose_u(0, 0)

                def step(t, n, ahead):
                    e = RING * t + n
                    if ahead(1):
                        pe.wait_ge(s_uTd, e + 1)
                        gate_up(RING * t + (n + 1), (n + 1) % 2)
                    if ahead(3):
                        pe.wait_ge(s_idx, e + 2)
                        find(RING * t + (n + 3), (n + 3) % 2)
                    if ahead(2):
                        transpose_x(t, n + 2)
                    pe.wait_ge(s_wd[n % 2], 16 * ((RING // 2) * t + (n // 2 + 1)))
                    pe.wait_ge(s_uTd, e + 2)
                    pe.wait_ge(s_ya, e + 1)
                    pe.wait_ge(s_yd, e + 1)
                    for half in range(2):
                        for f in range(FC):
                            ins = nc.tensor.matmul(ps[0:CAP, 4 + half, :], uT[:, n % 2, f, :],
                                                   wd[n % 2][:, f, 512 * half:512 * (half + 1)], start=f == 0, stop=f == FC - 1)
                    ins.then_inc(s_dn, 1)
                    if ahead(1):
                        transpose_u(RING * t + (n + 1), (n + 1) % 2)

                turns(pe, step)

        with ExitStack() as inner:
            def isem(name):
                return inner.enter_context(nc.semaphore(name))

            xT = G.main[:, 0:KC * P].rearrange("p (o c t) -> p o c t", o=1, c=KC)
            sg = G.main[:, KC * P:(KC + FC) * P].rearrange("p (f t) -> p f t", f=FC)
            uT = G.main[:, (KC + FC) * P:(KC + 2 * FC) * P].rearrange("p (o f t) -> p o f t", o=1, f=FC)
            s_wgu, s_wd = isem("x_gate_up_landed"), isem("x_down_landed")
            dch = isem("dve_chain")
            s_pick, s_find, s_idx, s_g = isem("x_pick_built"), isem("x_rows_found"), isem("x_row_numbers"), isem("x_gathered")
            s_xp, s_xd, s_xa = isem("x_x_transposed"), isem("x_xT_low_copied"), isem("x_xT_high_copied")
            s_gu, s_sg, s_u, s_dn = isem("x_gate_up_done"), isem("x_silu_done"), isem("x_u_ready"), isem("x_down_done")
            s_ya, s_yd, s_sc = isem("x_y_low_ready"), isem("x_y_high_ready"), isem("x_scattered")
            s_added, s_passed = isem("x_tile_added"), isem("x_pool_waits_passed")
            block = inner.enter_context(nc.Block())

            def extra_tiles(eng, body):
                total = eng.value_load(G.extra_tab[0:1, P:P + 1], min_val=0, max_val=MAX_EXTRA)
                with eng.If(total > 0):
                    with eng.Fori(0, MAX_EXTRA) as j:
                        with eng.If(total > j):
                            body(j)

            def expert_of(eng, j):
                return eng.value_load(G.extra_tab[0:1, bass.ds(j, 1)], min_val=0, max_val=E_N - 1)

            @block.sync
            def _(sp):
                def body(j):
                    sp.wait_ge(s_dn, j + 1)
                    e = expert_of(sp, j)
                    load_gate_up(sp, e, 0, s_wgu)
                    load_down(sp, e, 0, s_wd)

                sp.sem_inc(s_dn, 1)
                extra_tiles(sp, body)

            @block.gpsimd
            def _(pool):
                def body(j):
                    pool.wait_ge(s_idx, j + 1)
                    pool.sem_inc(s_passed, 1)
                    gather_rows(pool, 0, 0).then_inc(s_g, 16)
                    pool.wait_ge(s_ya, j + 1)
                    pool.wait_ge(s_yd, j + 1)
                    pool.sem_inc(s_passed, 1)
                    pool.indirect_dma_start(out=G.y_rows, out_offset=bass.IndirectOffsetOnAxis(ap=sidx[:, 0:1], axis=0),
                                            in_=yb[:, 0, :], in_offset=None, compute_op=ALU.add).then_inc(s_sc, 16)
                    pool.wait_ge(s_sc, 16 * j + 16)
                    pool.sem_inc(s_added, 1)

                pool.sem_inc(s_added, 1)
                extra_tiles(pool, body)

            @block.scalar
            def _(act):
                def body(j):
                    act.wait_ge(s_xp, j + 1)
                    nc.scalar.activation(xT[:, 0, 4:8, 0:CAP], ps[:, 1, :].rearrange("p (c t) -> p c t", c=4)[:, :, 0:CAP],
                                         ACT.Copy).then_inc(s_xa, 1)
                    act.wait_ge(s_gu, j + 1)
                    gate = ps[:, 2, 0:2 * P].rearrange("p (f t) -> p f t", f=FC)
                    nc.scalar.activation(sg[:, :, 0:CAP], gate[:, :, 0:CAP], ACT.Silu).then_inc(s_sg, 1)
                    act.wait_ge(s_dn, j + 2)
                    nc.scalar.activation(yb[:, 0, 0:512], ps[0:CAP, 4, :], ACT.Copy, scale=found[:, 0, 1:2]).then_inc(s_ya, 1)

                extra_tiles(act, body)

            @block.vector
            def _(dve):
                def body(j):
                    e = expert_of(dve, j)
                    dve.wait_ge(s_added, j + 1)
                    for i in range(NT):
                        ins = nc.vector.tensor_scalar(pick[:, 0, i, :], k[:, K_IOTA:K_IOTA + CAP], G.extra_base[:, bass.ds(j, 1)],
                                                      posm[:, bass.ds(NT * e + i, 1)], ALU.add, ALU.is_equal)
                    ins.then_inc(s_pick, 1)
                    dve.wait_ge(s_find, j + 1)
                    count = [0]

                    def q(ins):
                        count[0] += 1
                        ins.then_inc(dch, 1)
                        dve.wait_ge(dch, 2 * j + count[0])

                    pick_rows(q, 0, 6).then_inc(s_idx, 1)
                    dve.wait_ge(s_xp, j + 1)
                    nc.vector.tensor_copy(xT[:, 0, 0:4, 0:CAP], ps[:, 0, :].rearrange("p (c t) -> p c t", c=4)[:, :, 0:CAP]).then_inc(s_xd, 1)
                    dve.wait_ge(s_sg, j + 1)
                    up = ps[:, 2, 2 * P:4 * P].rearrange("p (f t) -> p f t", f=FC)
                    nc.vector.tensor_tensor(uT[:, 0, :, 0:CAP], sg[:, :, 0:CAP], up[:, :, 0:CAP], ALU.mult).then_inc(s_u, 1)
                    dve.wait_ge(s_dn, j + 2)
                    nc.vector.tensor_scalar(yb[:, 0, 512:D], ps[0:CAP, 5, :], found[:, 0, 1:2], None, ALU.mult).then_inc(s_yd, 1)

                extra_tiles(dve, body)

            @block.tensor
            def _(pe):
                def body(j):
                    e = expert_of(pe, j)
                    pe.wait_ge(s_pick, j + 1)
                    for i in range(NT):
                        ins = nc.tensor.matmul(ps[0:CAP, 6, 0:6], pick[:, 0, i, :],
                                               gt[:, bass.ds(e, 1), i, :].rearrange("p o t -> p (o t)"), start=i == 0, stop=i == NT - 1)
                    ins.then_inc(s_find, 1)
                    pe.wait_ge(s_g, 16 * j + 16)
                    for c in range(KC):
                        ins = nc.tensor.transpose(ps[:, c // 4, (c % 4) * P:(c % 4) * P + CAP], xg[:, 0, c:D:KC], ident[0:CAP, 0:CAP])
                    ins.then_inc(s_xp, 1)
                    pe.wait_ge(s_wgu, 32 * j + 32)
                    pe.wait_ge(s_xd, j + 1)
                    pe.wait_ge(s_xa, j + 1)
                    for m in range(2):
                        for f in range(FC):
                            at = (2 * m + f) * P
                            for c in range(KC):
                                ins = nc.tensor.matmul(ps[:, 2, at:at + CAP], wgu[0][:, m, c, f * P:(f + 1) * P], xT[:, 0, c, 0:CAP],
                                                       start=c == 0, stop=c == KC - 1)
                    ins.then_inc(s_gu, 1)
                    pe.wait_ge(s_wd, 16 * j + 16)
                    pe.wait_ge(s_u, j + 1)
                    for half in range(2):
                        for f in range(FC):
                            ins = nc.tensor.matmul(ps[0:CAP, 4 + half, :], uT[:, 0, f, 0:CAP], wd[0][:, f, 512 * half:512 * (half + 1)],
                                                   start=f == 0, stop=f == FC - 1)
                    ins.then_inc(s_dn, 1)

                extra_tiles(pe, body)

        stage_final(nc, A, G)


def stage_final(nc, A, G):
    with ExitStack() as own:
        def sb(name, shape, dt=F32):
            return own.enter_context(nc.sbuf_tensor(name, shape, dt))

        def sem(name):
            return own.enter_context(nc.semaphore(name))

        xt, rows = G.xt, G.rows
        y = G.main[:, 0:NT * D].rearrange("p (i d) -> p i d", i=NT)
        sq = G.main[:, NT * D:(NT + 2) * D].rearrange("p (i d) -> p i d", i=2)
        ss = sb("ss_final", [P, NT])
        rt = sb("rt_final", [P, NT])
        s_in = [sem(f"y_landed{i}") for i in range(NT)]
        s_sq, s_ms, s_rt, s_o, s_out = sem("y_squares"), sem("y_mean_square"), sem("y_root"), [sem(f"out_ready{i}") for i in range(NT)], sem("out_stored")
        s_y = sem("y_normed")
        dch = sem("dve_chain")
        block = own.enter_context(nc.Block())

        @block.sync
        def _(sp):
            for i in range(NT):
                sp.dma_start(y[:, i, :], G.y_rows[i * P:(i + 1) * P, :]).then_inc(s_in[i], 16)
            for i in range(NT):
                sp.wait_ge(s_o[i], 1)
                sp.dma_start(G.out[0, i * P:(i + 1) * P, :], xt[:, i, :]).then_inc(s_out, 16)
            sp.wait_ge(s_out, 16 * NT)

        @block.gpsimd
        def _(pool):
            for i in range(2):
                pool.wait_ge(s_y, i + 1)
                nc.gpsimd.tensor_tensor(xt[:, i, :], xt[:, i, :], y[:, i, :], ALU.add).then_inc(s_o[i], 1)

        @block.scalar
        def _(act):
            for i in range(NT):
                act.wait_ge(s_in[i], 16)
                nc.scalar.activation(sq[:, i % 2, :], y[:, i, :], ACT.Square, accum_out=ss[:, i:i + 1]).then_inc(s_sq, 1)
                act.wait_ge(s_ms, i + 1)
                nc.scalar.activation(rt[:, i:i + 1], ss[:, i:i + 1], ACT.Sqrt).then_inc(s_rt, 1)

        @block.vector
        def _(dve):
            step = Chain(dve, dch)
            for i in range(NT):
                dve.wait_ge(s_sq, i + 1)
                nc.vector.tensor_scalar(ss[:, i:i + 1], ss[:, i:i + 1], 1.0 / D, EPS, ALU.mult, ALU.add).then_inc(s_ms, 1)
                dve.wait_ge(s_rt, i + 1)
                step(nc.vector.reciprocal(rt[:, i:i + 1], rt[:, i:i + 1]))
                ins = nc.vector.scalar_tensor_tensor(y[:, i, :], y[:, i, :], rt[:, i:i + 1], rows[:, 3, :], ALU.mult, ALU.mult)
                if i < 2:
                    ins.then_inc(s_y, 1)
                else:
                    step(ins)
                    nc.vector.tensor_tensor(xt[:, i, :], xt[:, i, :], y[:, i, :], ALU.add).then_inc(s_o[i], 1)


class Shared:
    pass


def build(nc, A, out):
    with ExitStack() as ctx:
        def sb(name, shape, dt=F32):
            return ctx.enter_context(nc.sbuf_tensor(name, shape, dt))

        G = Shared()
        G.ps = ctx.enter_context(nc.psum_tensor("ps", [P, 8, 512], F32))
        G.k = sb("consts", [P, K_W])
        G.gb = sb("gate_bias", [HEADS, 2])
        G.cols = sb("cols", [P, 44])
        G.rows = sb("rows", [P, 4, D])
        G.maskb = sb("maskb", [P, NT, SEQ])
        G.xt = sb("xt", [P, NT, D])
        G.s_wgu = [ctx.enter_context(nc.semaphore(f"gate_up_landed{n}")) for n in range(RING)]
        G.s_wd = [ctx.enter_context(nc.semaphore(f"down_landed{n}")) for n in range(2)]
        G.s_wout = ctx.enter_context(nc.semaphore("w_out_landed"))
        G.w_shared_down = G.maskb[:, :, :].rearrange("p i t -> p (i t)").rearrange("p (f n) -> p f n", f=FC)
        G.u_shared = G.rows[:, 0, :].rearrange("p (f t) -> p f t", f=FC)
        G.posm = sb("place_in_expert", [P, E_N * NT])
        G.gt = sb("token_and_gate", [P, E_N, NT, 6], BF16)
        G.extra_base = sb("extra_base", [P, P])
        G.count_tab = sb("expert_counts", [1, E_N], I32)
        G.extra_tab = sb("extra_tab", [1, P + 1], I32)
        G.h2_rows = nc.dram_tensor("h2_rows", (SEQ, D), F32, kind="Internal").ap()
        G.y_rows = nc.dram_tensor("y_rows", (SEQ + P, D), F32, kind="Internal").ap()
        G.out = out
        G.QKC = NT * NAT_W
        G.main = sb("main", [P, G.QKC + 2 * HEADS * SEQ])
        G.side = sb("side", [P, 10240])
        G.nat = G.main[:, 0:G.QKC].rearrange("p (i n) -> p i n", i=NT)
        G.qkc = G.main[:, G.QKC:].rearrange("p (c t) -> p c t", c=2 * HEADS)
        G.wout = G.side[:, 0:8192].rearrange("p (f n) -> p f n", f=2 * HEADS)
        G.w_gate_up = [t.rearrange("p (m c f) -> p m c f", m=2, c=KC)
                       for t in (G.side[:, 0:4096], G.side[:, 4096:8192], G.main[:, 0:4096], G.main[:, 4096:8192])]
        G.w_down = [t.rearrange("p (f n) -> p f n", f=FC) for t in (G.side[:, 8192:10240], G.main[:, G.QKC:G.QKC + 2048])]
        G.held = [ExitStack(), ExitStack()]
        stage_in(nc, A, G)
        with ExitStack() as middle:
            G.arena = middle.enter_context(nc.sbuf_tensor("arena", [P, 6144], F32))
            G.catT = middle.enter_context(nc.sbuf_tensor("catT", [P, 2 * HEADS, SEQ], F32))
            stage_attention(nc, A, G)
            G.held[0].close()
            stage_route(nc, A, G)
            G.held[1].close()
        stage_experts(nc, A, G)


INS = ["x", "c", "w_ada", "b_ada", "g_mix_pre", "g_mix_post", "g_ffn_pre", "g_ffn_post", "w_in", "conv_w", "conv_b",
       "b_igate", "b_fgate", "g_mlstm_head", "g_idx_k", "b_idx_k", "w_out", "w_router", "b_router", "w_exp_gate",
       "w_exp_up", "w_exp_down", "w_sh_gate", "w_sh_up", "w_sh_down"]


def kernel(**inputs):
    import concourse.bacc as bacc
    from concourse.bass_utils import run_bass_kernel_spmd

    nc = bacc.Bacc("TRN2", target_bir_lowering=False, num_devices=1)
    arrays = {f"in_{n}": np.ascontiguousarray(inputs[n]) for n in INS}
    arrays["in_consts"] = constants()
    A = {n[3:]: nc.dram_tensor(n, a.shape, mybir.dt.from_np(a.dtype), kind="ExternalInput").ap() for n, a in arrays.items()}
    out = nc.dram_tensor("out_y", (1, SEQ, D), F32, kind="ExternalOutput").ap()
    build(nc, A, out)
    return run_bass_kernel_spmd(nc, [arrays], core_ids=[0]).results[0]["out_y"]
```
